# Optimizing a Trainium2 kernel written in Bass

```python
import math
import jax, jax.numpy as jnp
from jax import lax
import numpy as np

D_MODEL = 1024
BATCH = 1
SEQ = 256
DEPTH = 2

N_EVEN = (DEPTH + 1) // 2
N_ODD = DEPTH // 2

POOL_WINDOWS = (2, 4, 8, 16)
POOL_GROUPS = 4
POOL_WIDTH = D_MODEL // 2
POOL_GDIM = POOL_WIDTH // POOL_GROUPS
SGU_GROUPS = 4
SGU_WIDTH = D_MODEL // 2
SGU_GDIM = SGU_WIDTH // SGU_GROUPS
SGU_CHUNK = 128
EVEN_IN = POOL_WIDTH + 2 * SGU_WIDTH
EVEN_MIX = POOL_WIDTH + SGU_WIDTH
NSA_HEADS = 8
NSA_KV_GROUPS = 2
NSA_HPG = NSA_HEADS // NSA_KV_GROUPS
NSA_HEAD_DIM = 64
NSA_WIDTH = NSA_HEADS * NSA_HEAD_DIM
NSA_KV_WIDTH = NSA_KV_GROUPS * NSA_HEAD_DIM
CMP_BLOCK = 32
CMP_STRIDE = 16
CMP_HIDDEN = 128
SEL_BLOCK = 64
SEL_TOPK = 16
WINDOW = 512
Q_BLOCK = 128
FORCE_SCORE = 1.0e4
ROPE_THETA = 500000.0
ROPE_DIM = NSA_HEAD_DIM // 4
RET_HEADS = 4
RET_HEAD_DIM = 128
RET_WIDTH = RET_HEADS * RET_HEAD_DIM
RET_CHUNK = 128
RET_THETA = 10000.0
ODD_IN = NSA_WIDTH + 6 * NSA_KV_WIDTH + 3 * NSA_HEADS + 4 * RET_WIDTH
ODD_MIX = NSA_WIDTH + RET_WIDTH
FFN_HIDDEN = -(-8 * D_MODEL // (3 * 256)) * 256
NEG_INF = -1.0e30


def rms_norm(x, g, eps=1e-6):
    xf = x.astype(jnp.float32)
    y = xf * lax.rsqrt(jnp.mean(xf * xf, axis=-1, keepdims=True) + eps)
    return (y * g.astype(jnp.float32)).astype(x.dtype)

def layer_norm(x, g, b, eps=1e-5):
    xf = x.astype(jnp.float32)
    mu = jnp.mean(xf, axis=-1, keepdims=True)
    var = jnp.mean(jnp.square(xf - mu), axis=-1, keepdims=True)
    return ((xf - mu) * lax.rsqrt(var + eps) * g.astype(jnp.float32) + b.astype(jnp.float32)).astype(x.dtype)

def masked_softmax(s, mask):
    return jax.nn.softmax(jnp.where(mask, s.astype(jnp.float32), NEG_INF), axis=-1)

def rope_tables(positions, rot_dim, theta):
    inv_freq = 1.0 / (theta ** (jnp.arange(0, rot_dim, 2, dtype=jnp.float32) / rot_dim))
    ang = positions.astype(jnp.float32)[..., None] * inv_freq
    return jnp.cos(ang)[:, None], jnp.sin(ang)[:, None]

def apply_rope(x, cos, sin):
    half = cos.shape[-1]
    x1, x2, rest = x[..., :half], x[..., half:2 * half], x[..., 2 * half:]
    c, s = cos.astype(x.dtype), sin.astype(x.dtype)
    return jnp.concatenate([x1 * c - x2 * s, x2 * c + x1 * s, rest], axis=-1)

def to_heads(x, n):
    b, t, _ = x.shape
    return x.reshape(b, t, n, -1).transpose(0, 2, 1, 3)

def swiglu(h, w_gate, w_up, w_down):
    return (jax.nn.silu(h @ w_gate) * (h @ w_up)) @ w_down

def pool_mixer(a, pool_w, pool_scale):
    b, t_len, _ = a.shape
    af = a.astype(jnp.float32).reshape(b, t_len, POOL_GROUPS, POOL_GDIM)
    cs = jnp.concatenate([jnp.zeros_like(af[:, :1]), jnp.cumsum(af, axis=1)], axis=1)
    t = jnp.arange(t_len)
    pooled = []
    for gi, w in enumerate(POOL_WINDOWS):
        lo = jnp.maximum(t + 1 - w, 0)
        win_sum = cs[:, 1:, gi] - cs[:, lo, gi]
        pooled.append(win_sum / (t + 1 - lo).astype(jnp.float32)[None, :, None])
    pooled = jnp.stack(pooled, axis=2)
    diff = (pooled - af).astype(a.dtype)
    y = jnp.einsum('btgc,gcd->btgd', diff, pool_w)
    return y.reshape(b, t_len, POOL_WIDTH) * pool_scale

def sgu_mixer(u, v, ln_g, ln_b, w_s, b_s):
    b, t_len, _ = u.shape
    u = jax.nn.gelu(u)
    v = layer_norm(jax.nn.gelu(v), ln_g, ln_b)
    n_chunk = t_len // SGU_CHUNK
    vc = v.reshape(b, n_chunk, SGU_CHUNK, SGU_GROUPS, SGU_GDIM)
    causal = jnp.tril(jnp.ones((SGU_CHUNK, SGU_CHUNK), dtype=bool))
    w_masked = jnp.where(causal[None], w_s, 0.0).astype(v.dtype)
    mixed = jnp.einsum('gts,bcsgd->bctgd', w_masked, vc) + b_s.T[None, None, :, :, None]
    return u * mixed.reshape(b, t_len, SGU_WIDTH)

def even_mixer(h, w_in, pool_w, pool_scale, sgu_ln_g, sgu_ln_b, sgu_w, sgu_b, w_out):
    z = h @ w_in
    a = z[..., :POOL_WIDTH]
    u = z[..., POOL_WIDTH:POOL_WIDTH + SGU_WIDTH]
    v = z[..., POOL_WIDTH + SGU_WIDTH:]
    y_a = pool_mixer(a, pool_w, pool_scale)
    y_b = sgu_mixer(u, v, sgu_ln_g, sgu_ln_b, sgu_w, sgu_b)
    return jnp.concatenate([y_a, y_b], axis=-1) @ w_out

def compress_blocks(k, pos_emb, w1, w2):
    t_len = k.shape[2]
    n_cmp = (t_len - CMP_BLOCK) // CMP_STRIDE + 1
    idx = np.arange(n_cmp)[:, None] * CMP_STRIDE + np.arange(CMP_BLOCK)[None, :]
    blocks = k[:, :, idx] + pos_emb
    flat = blocks.reshape(blocks.shape[:3] + (CMP_BLOCK * NSA_HEAD_DIM,))
    return jax.nn.gelu(flat @ w1) @ w2

def nsa_attention(q, k_cmp, v_cmp, k_sel, v_sel, k_win, v_win, gates, positions,
                  cmp_k_pos, cmp_k_w1, cmp_k_w2, cmp_v_pos, cmp_v_w1, cmp_v_w2):
    b, t_len, _ = q.shape
    G, M, d = NSA_KV_GROUPS, NSA_HPG, NSA_HEAD_DIM
    cos, sin = rope_tables(positions, ROPE_DIM, ROPE_THETA)
    q = apply_rope(to_heads(q, NSA_HEADS), cos, sin) * (d ** -0.5)
    k_cmp = apply_rope(to_heads(k_cmp, G), cos, sin)
    k_sel = apply_rope(to_heads(k_sel, G), cos, sin)
    k_win = apply_rope(to_heads(k_win, G), cos, sin)
    v_cmp, v_sel, v_win = to_heads(v_cmp, G), to_heads(v_sel, G), to_heads(v_win, G)

    kc = compress_blocks(k_cmp, cmp_k_pos, cmp_k_w1, cmp_k_w2)
    vc = compress_blocks(v_cmp, cmp_v_pos, cmp_v_w1, cmp_v_w2)
    n_cmp = kc.shape[2]
    cmp_end = jnp.arange(n_cmp) * CMP_STRIDE + CMP_BLOCK - 1

    n_sel = t_len // SEL_BLOCK
    top_k = min(SEL_TOPK, n_sel)
    c_start = np.arange(n_cmp) * CMP_STRIDE
    s_start = np.arange(n_sel) * SEL_BLOCK
    cmp_to_sel = ((c_start[:, None] < s_start[None, :] + SEL_BLOCK)
                  & (c_start[:, None] + CMP_BLOCK > s_start[None, :])).astype(np.float32)
    ks_blk = k_sel.reshape(b, G, n_sel, SEL_BLOCK, d)
    vs_blk = v_sel.reshape(b, G, n_sel, SEL_BLOCK, d)
    kw_pad = jnp.pad(k_win, ((0, 0), (0, 0), (WINDOW, 0), (0, 0)))
    vw_pad = jnp.pad(v_win, ((0, 0), (0, 0), (WINDOW, 0), (0, 0)))
    g = jax.nn.sigmoid(gates.astype(jnp.float32)).reshape(b, t_len, NSA_HEADS, 3)
    g = g.transpose(0, 2, 1, 3).astype(q.dtype)
    b_idx = jnp.arange(b)[:, None, None, None]
    g_idx = jnp.arange(G)[None, :, None, None]
    j_sel = jnp.arange(n_sel)

    def block(i):
        t0 = i * Q_BLOCK
        tq = t0 + jnp.arange(Q_BLOCK)
        qb = lax.dynamic_slice_in_dim(q, t0, Q_BLOCK, axis=2).reshape(b, G, M, Q_BLOCK, d)
        gb = lax.dynamic_slice_in_dim(g, t0, Q_BLOCK, axis=2)
        s = jnp.einsum('bgmqd,bgnd->bgmqn', qb, kc)
        p_cmp = masked_softmax(s, cmp_end[None, :] <= tq[:, None])
        p_cmp = p_cmp * (tq >= CMP_BLOCK - 1).astype(jnp.float32)[:, None]
        o_cmp = jnp.einsum('bgmqn,bgnd->bgmqd', p_cmp.astype(vc.dtype), vc)
        p_slc = jnp.einsum('bgmqn,nj->bgqj', p_cmp, cmp_to_sel)
        cur = tq // SEL_BLOCK
        sel_ok = j_sel[None, :] <= cur[:, None]
        forced = (j_sel[None, :] == 0) | (j_sel[None, :] == cur[:, None]) | (j_sel[None, :] == cur[:, None] - 1)
        score = jnp.where(sel_ok, jnp.where(forced, FORCE_SCORE, p_slc), -1.0)
        top_val, top_idx = lax.top_k(score, top_k)
        ks = ks_blk[b_idx, g_idx, top_idx]
        vs = vs_blk[b_idx, g_idx, top_idx]
        tok = top_idx[..., None] * SEL_BLOCK + jnp.arange(SEL_BLOCK)
        tok_ok = (top_val >= 0.0)[..., None] & (tok <= tq[:, None, None])
        s = jnp.einsum('bgmqd,bgqkld->bgmqkl', qb, ks).reshape(b, G, M, Q_BLOCK, top_k * SEL_BLOCK)
        p = masked_softmax(s, tok_ok.reshape(b, G, 1, Q_BLOCK, top_k * SEL_BLOCK))
        p = p.reshape(b, G, M, Q_BLOCK, top_k, SEL_BLOCK).astype(vs.dtype)
        o_sel = jnp.einsum('bgmqkl,bgqkld->bgmqd', p, vs)
        kwb = lax.dynamic_slice_in_dim(kw_pad, t0, WINDOW + Q_BLOCK, axis=2)
        vwb = lax.dynamic_slice_in_dim(vw_pad, t0, WINDOW + Q_BLOCK, axis=2)
        pos = t0 - WINDOW + jnp.arange(WINDOW + Q_BLOCK)
        win_ok = (pos[None, :] >= 0) & (pos[None, :] <= tq[:, None]) & (pos[None, :] > tq[:, None] - WINDOW)
        s = jnp.einsum('bgmqd,bgsd->bgmqs', qb, kwb)
        o_win = jnp.einsum('bgmqs,bgsd->bgmqd', masked_softmax(s, win_ok).astype(vwb.dtype), vwb)
        o = jnp.stack([o_cmp, o_sel, o_win], axis=-1).reshape(b, NSA_HEADS, Q_BLOCK, d, 3)
        return jnp.einsum('bhqdc,bhqc->bqhd', o, gb)

    out = lax.map(block, jnp.arange(t_len // Q_BLOCK))
    return out.transpose(1, 0, 2, 3, 4).reshape(b, t_len, NSA_WIDTH)

def retention(q, k, v, gate, positions, gn_g):
    b, t_len, _ = q.shape
    H, d, C = RET_HEADS, RET_HEAD_DIM, RET_CHUNK
    n_chunk = t_len // C
    cos, sin = rope_tables(positions, d, RET_THETA)
    q = apply_rope(to_heads(q, H), cos, sin)
    k = apply_rope(to_heads(k, H), cos, sin) * (d ** -0.5)
    v = to_heads(v, H)
    log_gamma = jnp.log1p(-jnp.exp2(-5.0 - jnp.arange(H, dtype=jnp.float32)))
    idx = jnp.arange(C, dtype=jnp.float32)
    rel = idx[:, None] - idx[None, :]
    decay = jnp.where(rel >= 0, jnp.exp(jnp.maximum(rel, 0.0)[None] * log_gamma[:, None, None]), 0.0)
    qc = q.reshape(b, H, n_chunk, C, d)
    kc = k.reshape(b, H, n_chunk, C, d)
    vc = v.reshape(b, H, n_chunk, C, d)
    s = jnp.einsum('bhcid,bhcjd->bhcij', qc, kc) * decay[None, :, None].astype(q.dtype)
    o_intra = jnp.einsum('bhcij,bhcje->bhcie', s, vc)
    zeta = jnp.exp((C - 1 - idx)[None, :] * log_gamma[:, None])
    chunk_kv = jnp.einsum('bhcjd,bhcje->bhcde', kc * zeta[None, :, None, :, None].astype(k.dtype), vc)
    g_chunk = jnp.exp(C * log_gamma)[None, :, None, None]

    def step(state, kv):
        return state * g_chunk + kv, state

    _, prev = lax.scan(step, jnp.zeros((b, H, d, d), jnp.float32),
                       jnp.moveaxis(chunk_kv, 2, 0).astype(jnp.float32))
    prev = jnp.moveaxis(prev, 0, 2)
    xi = jnp.exp((idx + 1.0)[None, :] * log_gamma[:, None])
    o_cross = jnp.einsum('bhcid,bhcde->bhcie', qc.astype(jnp.float32) * xi[None, :, None, :, None], prev)
    o = (o_intra.astype(jnp.float32) + o_cross).reshape(b, H, t_len, d).transpose(0, 2, 1, 3)
    mu = jnp.mean(o, axis=-1, keepdims=True)
    var = jnp.mean(jnp.square(o - mu), axis=-1, keepdims=True)
    o = ((o - mu) * lax.rsqrt(var + 1e-5)).reshape(b, t_len, RET_WIDTH) * gn_g.astype(jnp.float32)
    return (jax.nn.silu(gate.astype(jnp.float32)) * o).astype(gate.dtype)

def odd_mixer(h, positions, w_in, cmp_k_pos, cmp_k_w1, cmp_k_w2, cmp_v_pos, cmp_v_w1, cmp_v_w2,
              ret_gn_g, w_out):
    z = h @ w_in
    sizes = [NSA_WIDTH] + [NSA_KV_WIDTH] * 6 + [3 * NSA_HEADS] + [RET_WIDTH] * 4
    splits = np.cumsum(sizes)[:-1].tolist()
    q, kc, vc, ks, vs, kw, vw, gt, rq, rk, rv, rg = jnp.split(z, splits, axis=-1)
    y_c = nsa_attention(q, kc, vc, ks, vs, kw, vw, gt, positions,
                        cmp_k_pos, cmp_k_w1, cmp_k_w2, cmp_v_pos, cmp_v_w1, cmp_v_w2)
    y_d = retention(rq, rk, rv, rg, positions, ret_gn_g)
    return jnp.concatenate([y_c, y_d], axis=-1) @ w_out

def first_inputs(seed: int = 0) -> dict:
    key = jax.random.key(seed)
    ks = jax.random.split(key, 32)

    def nrm(k, shape, scale):
        return jax.random.normal(k, shape, jnp.float32) * scale

    def gain(k, shape):
        return 1.0 + 0.05 * jax.random.normal(k, shape, jnp.float32)

    NE, NO, D, F = N_EVEN, N_ODD, D_MODEL, FFN_HIDDEN
    x = nrm(ks[0], (BATCH, SEQ, D), 1.0)
    start = jax.random.randint(ks[1], (BATCH, 1), 0, 2048, dtype=jnp.int32)
    positions = start + jnp.arange(SEQ, dtype=jnp.int32)[None, :]
    cmp_in = CMP_BLOCK * NSA_HEAD_DIM
    return {
        "x": x,
        "positions": positions,
        "ln_mix_pre": gain(ks[2], (DEPTH, D)),
        "ln_mix_post": gain(ks[3], (DEPTH, D)),
        "ln_ffn_pre": gain(ks[4], (DEPTH, D)),
        "ln_ffn_post": gain(ks[5], (DEPTH, D)),
        "ffn_w_gate": nrm(ks[6], (DEPTH, D, F), D ** -0.5),
        "ffn_w_up": nrm(ks[7], (DEPTH, D, F), D ** -0.5),
        "ffn_w_down": nrm(ks[8], (DEPTH, F, D), F ** -0.5),
        "ev_w_in": nrm(ks[9], (NE, D, EVEN_IN), D ** -0.5),
        "ev_pool_w": nrm(ks[10], (NE, POOL_GROUPS, POOL_GDIM, POOL_GDIM), POOL_GDIM ** -0.5),
        "ev_pool_scale": 1.0 + 0.1 * jax.random.normal(ks[11], (NE, POOL_WIDTH), jnp.float32),
        "ev_sgu_ln_g": gain(ks[12], (NE, SGU_WIDTH)),
        "ev_sgu_ln_b": nrm(ks[13], (NE, SGU_WIDTH), 0.02),
        "ev_sgu_w": nrm(ks[14], (NE, SGU_GROUPS, SGU_CHUNK, SGU_CHUNK), SGU_CHUNK ** -0.5),
        "ev_sgu_b": 1.0 + 0.1 * jax.random.normal(ks[15], (NE, SGU_GROUPS, SGU_CHUNK), jnp.float32),
        "ev_w_out": nrm(ks[16], (NE, EVEN_MIX, D), EVEN_MIX ** -0.5),
        "od_w_in": nrm(ks[17], (NO, D, ODD_IN), D ** -0.5),
        "od_cmp_k_pos": nrm(ks[18], (NO, CMP_BLOCK, NSA_HEAD_DIM), 0.1),
        "od_cmp_k_w1": nrm(ks[19], (NO, cmp_in, CMP_HIDDEN), cmp_in ** -0.5),
        "od_cmp_k_w2": nrm(ks[20], (NO, CMP_HIDDEN, NSA_HEAD_DIM), CMP_HIDDEN ** -0.5),
        "od_cmp_v_pos": nrm(ks[21], (NO, CMP_BLOCK, NSA_HEAD_DIM), 0.1),
        "od_cmp_v_w1": nrm(ks[22], (NO, cmp_in, CMP_HIDDEN), cmp_in ** -0.5),
        "od_cmp_v_w2": nrm(ks[23], (NO, CMP_HIDDEN, NSA_HEAD_DIM), CMP_HIDDEN ** -0.5),
        "od_ret_gn_g": gain(ks[24], (NO, RET_WIDTH)),
        "od_w_out": nrm(ks[25], (NO, ODD_MIX, D), ODD_MIX ** -0.5),
    }

def first_block(x, positions, ln_mix_pre, ln_mix_post, ln_ffn_pre, ln_ffn_post,
              ffn_w_gate, ffn_w_up, ffn_w_down,
              ev_w_in, ev_pool_w, ev_pool_scale, ev_sgu_ln_g, ev_sgu_ln_b, ev_sgu_w, ev_sgu_b, ev_w_out,
              od_w_in, od_cmp_k_pos, od_cmp_k_w1, od_cmp_k_w2, od_cmp_v_pos, od_cmp_v_w1, od_cmp_v_w2,
              od_ret_gn_g, od_w_out):
    for layer in range(DEPTH):
        h = rms_norm(x, ln_mix_pre[layer])
        if layer % 2 == 0:
            e = layer // 2
            m = even_mixer(h, ev_w_in[e], ev_pool_w[e], ev_pool_scale[e], ev_sgu_ln_g[e],
                           ev_sgu_ln_b[e], ev_sgu_w[e], ev_sgu_b[e], ev_w_out[e])
        else:
            o = layer // 2
            m = odd_mixer(h, positions, od_w_in[o], od_cmp_k_pos[o], od_cmp_k_w1[o], od_cmp_k_w2[o],
                          od_cmp_v_pos[o], od_cmp_v_w1[o], od_cmp_v_w2[o], od_ret_gn_g[o], od_w_out[o])
        x = x + rms_norm(m, ln_mix_post[layer])
        h = rms_norm(x, ln_ffn_pre[layer])
        x = x + rms_norm(swiglu(h, ffn_w_gate[layer], ffn_w_up[layer], ffn_w_down[layer]), ln_ffn_post[layer])
    return x


CTX_LEN = 256
GRID_W = 64
N_MIXERS = 4
ROPE_THETA_2 = 10000.0
NORM_EPS = 1e-6
N_MOD = 9
D_FF = 2816
NEG_INF_2 = -1e30

DA_QK_DIM = 64
DA_HEADS = D_MODEL // (2 * DA_QK_DIM)
DA_V_DIM = 2 * DA_QK_DIM
DA_QKV = 2 * DA_HEADS * 2 * DA_QK_DIM + DA_HEADS * DA_V_DIM
GA_HEAD_DIM = 128
GA_HEADS = D_MODEL // GA_HEAD_DIM
GA_KV_HEADS = 2
MLA_HEADS = 16
MLA_Q_RANK = 256
MLA_KV_RANK = 128
MLA_NOPE_DIM = 64
MLA_ROPE_DIM = 32
MLA_V_DIM = 64
SWA_HEAD_DIM = 64
SWA_HEADS = D_MODEL // SWA_HEAD_DIM
SWA_KV_HEADS = 2
WINDOW_2 = 128
BAND = Q_BLOCK + 2 * WINDOW_2


def rmsnorm(x, g):
    xf = x.astype(jnp.float32)
    y = xf * lax.rsqrt(jnp.mean(xf * xf, axis=-1, keepdims=True) + NORM_EPS)
    return (y * g.astype(jnp.float32)).astype(x.dtype)

def axial_rope_tables(seq_len, rot_dim):
    rows = seq_len // GRID_W
    row = jnp.repeat(jnp.arange(rows, dtype=jnp.int32), GRID_W).astype(jnp.float32)
    col = jnp.tile(jnp.arange(GRID_W, dtype=jnp.int32), rows).astype(jnp.float32)
    n_axis = rot_dim // 4
    freqs = ROPE_THETA_2 ** (-jnp.arange(n_axis, dtype=jnp.float32) / n_axis)
    ang = jnp.concatenate([row[:, None] * freqs, col[:, None] * freqs], axis=-1)
    return jnp.cos(ang), jnp.sin(ang)

def apply_rope_2(x, cos, sin):
    seq, half = cos.shape
    bshape = (seq,) + (1,) * (x.ndim - 3) + (half,)
    cs = cos.reshape(bshape).astype(x.dtype)
    sn = sin.reshape(bshape).astype(x.dtype)
    xp = x.reshape(x.shape[:-1] + (half, 2))
    x0, x1 = xp[..., 0], xp[..., 1]
    return jnp.stack([x0 * cs - x1 * sn, x0 * sn + x1 * cs], axis=-1).reshape(x.shape)

def sweep_query_blocks(fn, *qs):
    b, s = qs[0].shape[:2]
    nblk = s // Q_BLOCK
    blocks = tuple(jnp.moveaxis(q.reshape((b, nblk, Q_BLOCK) + q.shape[2:]), 1, 0) for q in qs)
    out = lax.map(lambda args: fn(*args), (jnp.arange(nblk),) + blocks)
    return jnp.moveaxis(out, 0, 1).reshape((b, s) + out.shape[3:])

def grouped_attend(q, k, v, scale):
    s = jnp.einsum('blhgd,bkhd->bhglk', q, k, preferred_element_type=jnp.float32) * scale
    p = jax.nn.softmax(s, axis=-1)
    o = jnp.einsum('bhglk,bkhd->blhgd', p.astype(v.dtype), v)
    return o.reshape(o.shape[:2] + (-1,))

def swiglu_2(h, w_in, w_out):
    gate, up = jnp.split(h @ w_in, 2, axis=-1)
    return (jax.nn.silu(gate) * up) @ w_out

def adaln(cond, w, b):
    m = jax.nn.silu(cond) @ w + b
    return m.reshape(m.shape[:-1] + (N_MOD, D_MODEL))

def modulated_norm(h, g, m, k):
    return rmsnorm(h, g) * (1.0 + m[..., k + 1, :]) + m[..., k, :]

def gated_residual(h, y, g, m, k, weight):
    return h + weight * m[..., k + 2, :] * rmsnorm(y, g)

def half_ffn(h, m, k, g_pre, g_post, w_in, w_out):
    y = swiglu_2(modulated_norm(h, g_pre, m, k), w_in, w_out)
    return gated_residual(h, y, g_post, m, k, 0.5)

def diff_attention_mixer(h, hc, w_in, lam, subln, w_out, lambda_init, ctx_out):
    b, s, _ = h.shape
    cos, sin = axial_rope_tables(s, DA_QK_DIM)

    def project(t):
        n = t.shape[1]
        q, k, v = jnp.split(t @ w_in, [DA_HEADS * 2 * DA_QK_DIM, 2 * DA_HEADS * 2 * DA_QK_DIM], axis=-1)
        return (q.reshape(b, n, DA_HEADS, 2, DA_QK_DIM), k.reshape(b, n, DA_HEADS, 2, DA_QK_DIM),
                v.reshape(b, n, DA_HEADS, DA_V_DIM))

    q, k, v = project(h)
    qc, kc, vc = project(hc)
    q, k = apply_rope_2(q, cos, sin), apply_rope_2(k, cos, sin)
    lf = lam.astype(jnp.float32)
    lam_full = jnp.exp(jnp.sum(lf[0] * lf[1])) - jnp.exp(jnp.sum(lf[2] * lf[3])) + lambda_init
    scale = DA_QK_DIM ** -0.5

    def attend(qb, kb, vb):
        sc = jnp.einsum('blhid,bkhid->bihlk', qb, kb, preferred_element_type=jnp.float32) * scale
        p = jax.nn.softmax(sc, axis=-1)
        p = p[:, 0] - lam_full * p[:, 1]
        o = jnp.einsum('bhlk,bkhd->blhd', p.astype(vb.dtype), vb)
        o = rmsnorm(o, subln) * (1.0 - lambda_init)
        return o.reshape(o.shape[0], o.shape[1], DA_HEADS * DA_V_DIM)

    k_all = jnp.concatenate([kc, k], axis=1)
    v_all = jnp.concatenate([vc, v], axis=1)
    y = sweep_query_blocks(lambda i, qb: attend(qb, k_all, v_all), q) @ w_out
    yc = attend(qc, kc, vc) @ w_out if ctx_out else None
    return y, yc

def gqa_axial_mixer(h, hc, w_in, q_norm, k_norm, w_out, ctx_out):
    b, s, _ = h.shape
    cos, sin = axial_rope_tables(s, GA_HEAD_DIM)
    grp = GA_HEADS // GA_KV_HEADS

    def project(t):
        n = t.shape[1]
        q, k, v = jnp.split(t @ w_in, [GA_HEADS * GA_HEAD_DIM, (GA_HEADS + GA_KV_HEADS) * GA_HEAD_DIM], axis=-1)
        q = rmsnorm(q.reshape(b, n, GA_KV_HEADS, grp, GA_HEAD_DIM), q_norm)
        k = rmsnorm(k.reshape(b, n, GA_KV_HEADS, GA_HEAD_DIM), k_norm)
        return q, k, v.reshape(b, n, GA_KV_HEADS, GA_HEAD_DIM)

    q, k, v = project(h)
    qc, kc, vc = project(hc)
    q, k = apply_rope_2(q, cos, sin), apply_rope_2(k, cos, sin)
    scale = GA_HEAD_DIM ** -0.5
    k_all = jnp.concatenate([kc, k], axis=1)
    v_all = jnp.concatenate([vc, v], axis=1)
    y = sweep_query_blocks(lambda i, qb: grouped_attend(qb, k_all, v_all, scale), q) @ w_out
    yc = grouped_attend(qc, kc, vc, scale) @ w_out if ctx_out else None
    return y, yc

def mla_mixer(h, hc, w_in, q_norm, kv_norm, w_uq, w_ukv, w_out, ctx_out):
    b, s, _ = h.shape
    cos, sin = axial_rope_tables(s, MLA_ROPE_DIM)

    def project(t):
        n = t.shape[1]
        cq, ckv, kr = jnp.split(t @ w_in, [MLA_Q_RANK, MLA_Q_RANK + MLA_KV_RANK], axis=-1)
        q = (rmsnorm(cq, q_norm) @ w_uq).reshape(b, n, MLA_HEADS, MLA_NOPE_DIM + MLA_ROPE_DIM)
        kv = (rmsnorm(ckv, kv_norm) @ w_ukv).reshape(b, n, MLA_HEADS, MLA_NOPE_DIM + MLA_V_DIM)
        qn, qr = jnp.split(q, [MLA_NOPE_DIM], axis=-1)
        kn, v = jnp.split(kv, [MLA_NOPE_DIM], axis=-1)
        return qn, qr, kn, kr, v

    qn, qr, kn, kr, v = project(h)
    qnc, qrc, knc, krc, vc = project(hc)
    qr, kr = apply_rope_2(qr, cos, sin), apply_rope_2(kr, cos, sin)
    scale = (MLA_NOPE_DIM + MLA_ROPE_DIM) ** -0.5

    def attend(qnb, qrb, knb, krb, vb):
        sc = (jnp.einsum('blhd,bkhd->bhlk', qnb, knb, preferred_element_type=jnp.float32)
              + jnp.einsum('blhd,bkd->bhlk', qrb, krb, preferred_element_type=jnp.float32)) * scale
        p = jax.nn.softmax(sc, axis=-1)
        o = jnp.einsum('bhlk,bkhd->blhd', p.astype(vb.dtype), vb)
        return o.reshape(o.shape[0], o.shape[1], MLA_HEADS * MLA_V_DIM)

    kn_all = jnp.concatenate([knc, kn], axis=1)
    kr_all = jnp.concatenate([krc, kr], axis=1)
    v_all = jnp.concatenate([vc, v], axis=1)
    y = sweep_query_blocks(lambda i, a, r: attend(a, r, kn_all, kr_all, v_all), qn, qr) @ w_out
    yc = attend(qnc, qrc, knc, krc, vc) @ w_out if ctx_out else None
    return y, yc

def window_sink_mixer(h, hc, w_in, sink, w_out, ctx_out):
    b, s, _ = h.shape
    cos, sin = axial_rope_tables(s, SWA_HEAD_DIM)
    grp = SWA_HEADS // SWA_KV_HEADS

    def project(t):
        n = t.shape[1]
        q, k, v = jnp.split(t @ w_in, [SWA_HEADS * SWA_HEAD_DIM, (SWA_HEADS + SWA_KV_HEADS) * SWA_HEAD_DIM], axis=-1)
        return (q.reshape(b, n, SWA_KV_HEADS, grp, SWA_HEAD_DIM), k.reshape(b, n, SWA_KV_HEADS, SWA_HEAD_DIM),
                v.reshape(b, n, SWA_KV_HEADS, SWA_HEAD_DIM))

    q, k, v = project(h)
    qc, kc, vc = project(hc)
    q, k = apply_rope_2(q, cos, sin), apply_rope_2(k, cos, sin)
    scale = SWA_HEAD_DIM ** -0.5
    sink_l = sink.astype(jnp.float32).reshape(SWA_KV_HEADS, grp)[None, :, :, None, None]

    def sink_softmax_mix(sc, vals):
        sc = jnp.concatenate([sc, jnp.broadcast_to(sink_l, sc.shape[:-1] + (1,))], axis=-1)
        p = jax.nn.softmax(sc, axis=-1)[..., :-1]
        o = jnp.einsum('bhglk,bkhd->blhgd', p.astype(vals.dtype), vals)
        return o.reshape(o.shape[:2] + (-1,))

    pad = ((0, 0), (WINDOW_2, WINDOW_2), (0, 0), (0, 0))
    k_pad, v_pad = jnp.pad(k, pad), jnp.pad(v, pad)

    def latent_block(i, qb):
        start = i * Q_BLOCK
        kb = lax.dynamic_slice_in_dim(k_pad, start, BAND, axis=1)
        vb = lax.dynamic_slice_in_dim(v_pad, start, BAND, axis=1)
        qpos = start + jnp.arange(Q_BLOCK)
        kpos = start - WINDOW_2 + jnp.arange(BAND)
        allowed = (kpos[None, :] >= 0) & (kpos[None, :] < s) & (jnp.abs(qpos[:, None] - kpos[None, :]) <= WINDOW_2)
        s_band = jnp.einsum('blhgd,bkhd->bhglk', qb, kb, preferred_element_type=jnp.float32) * scale
        s_band = jnp.where(allowed, s_band, NEG_INF_2)
        s_ctx = jnp.einsum('blhgd,bkhd->bhglk', qb, kc, preferred_element_type=jnp.float32) * scale
        return sink_softmax_mix(jnp.concatenate([s_ctx, s_band], axis=-1), jnp.concatenate([vc, vb], axis=1))

    y = sweep_query_blocks(latent_block, q) @ w_out
    yc = None
    if ctx_out:
        s_cc = jnp.einsum('blhgd,bkhd->bhglk', qc, kc, preferred_element_type=jnp.float32) * scale
        yc = sink_softmax_mix(s_cc, vc) @ w_out
    return y, yc

def second_inputs(seed: int = 0) -> dict:
    key = jax.random.key(seed)
    ks = iter(jax.random.split(key, 32))
    f32 = jnp.float32

    def nrm(shape, scale=1.0):
        return jax.random.normal(next(ks), shape, f32) * scale

    def w(shape, fan_in):
        return nrm(shape, fan_in ** -0.5)

    def gain(shape):
        return 1.0 + nrm(shape, 0.02)

    n0, n1, n2, n3 = [len(range(k, DEPTH, N_MIXERS)) for k in range(N_MIXERS)]
    return {
        "x": nrm((BATCH, SEQ, D_MODEL)),
        "c": nrm((BATCH, D_MODEL)),
        "ctx": nrm((BATCH, CTX_LEN, D_MODEL)),
        "c_ctx": nrm((D_MODEL,)),
        "ada_w": w((DEPTH, D_MODEL, N_MOD * D_MODEL), D_MODEL),
        "ada_b": nrm((DEPTH, N_MOD * D_MODEL), 0.02),
        "norm_g": gain((DEPTH, 6, D_MODEL)),
        "ffn_w_in": w((DEPTH, 2, D_MODEL, 2 * D_FF), D_MODEL),
        "ffn_w_out": w((DEPTH, 2, D_FF, D_MODEL), D_FF),
        "da_w_in": w((n0, D_MODEL, DA_QKV), D_MODEL),
        "da_lambda": nrm((n0, 4, DA_QK_DIM), 0.1),
        "da_subln": gain((n0, DA_V_DIM)),
        "da_w_out": w((n0, DA_HEADS * DA_V_DIM, D_MODEL), DA_HEADS * DA_V_DIM),
        "ga_w_in": w((n1, D_MODEL, (GA_HEADS + 2 * GA_KV_HEADS) * GA_HEAD_DIM), D_MODEL),
        "ga_q_norm": gain((n1, GA_HEAD_DIM)),
        "ga_k_norm": gain((n1, GA_HEAD_DIM)),
        "ga_w_out": w((n1, GA_HEADS * GA_HEAD_DIM, D_MODEL), GA_HEADS * GA_HEAD_DIM),
        "mla_w_in": w((n2, D_MODEL, MLA_Q_RANK + MLA_KV_RANK + MLA_ROPE_DIM), D_MODEL),
        "mla_q_norm": gain((n2, MLA_Q_RANK)),
        "mla_kv_norm": gain((n2, MLA_KV_RANK)),
        "mla_w_uq": w((n2, MLA_Q_RANK, MLA_HEADS * (MLA_NOPE_DIM + MLA_ROPE_DIM)), MLA_Q_RANK),
        "mla_w_ukv": w((n2, MLA_KV_RANK, MLA_HEADS * (MLA_NOPE_DIM + MLA_V_DIM)), MLA_KV_RANK),
        "mla_w_out": w((n2, MLA_HEADS * MLA_V_DIM, D_MODEL), MLA_HEADS * MLA_V_DIM),
        "swa_w_in": w((n3, D_MODEL, (SWA_HEADS + 2 * SWA_KV_HEADS) * SWA_HEAD_DIM), D_MODEL),
        "swa_sink": nrm((n3, SWA_HEADS), 0.5),
        "swa_w_out": w((n3, SWA_HEADS * SWA_HEAD_DIM, D_MODEL), SWA_HEADS * SWA_HEAD_DIM),
    }

def second_block(x, c, ctx, c_ctx, ada_w, ada_b, norm_g, ffn_w_in, ffn_w_out,
              da_w_in, da_lambda, da_subln, da_w_out,
              ga_w_in, ga_q_norm, ga_k_norm, ga_w_out,
              mla_w_in, mla_q_norm, mla_kv_norm, mla_w_uq, mla_w_ukv, mla_w_out,
              swa_w_in, swa_sink, swa_w_out):
    h, hc = x, ctx
    for i in range(DEPTH):
        kind, occ = i % N_MIXERS, i // N_MIXERS
        ctx_out = i < DEPTH - 1
        m = adaln(c, ada_w[i], ada_b[i])[:, None]
        mc = adaln(c_ctx, ada_w[i], ada_b[i])[None]
        g = norm_g[i]
        h = half_ffn(h, m, 0, g[0], g[1], ffn_w_in[i, 0], ffn_w_out[i, 0])
        hc = half_ffn(hc, mc, 0, g[0], g[1], ffn_w_in[i, 0], ffn_w_out[i, 0])
        u = modulated_norm(h, g[2], m, 3)
        uc = modulated_norm(hc, g[2], mc, 3)
        if kind == 0:
            lambda_init = 0.8 - 0.6 * math.exp(-0.3 * i)
            y, yc = diff_attention_mixer(u, uc, da_w_in[occ], da_lambda[occ], da_subln[occ], da_w_out[occ],
                                         lambda_init, ctx_out)
        elif kind == 1:
            y, yc = gqa_axial_mixer(u, uc, ga_w_in[occ], ga_q_norm[occ], ga_k_norm[occ], ga_w_out[occ], ctx_out)
        elif kind == 2:
            y, yc = mla_mixer(u, uc, mla_w_in[occ], mla_q_norm[occ], mla_kv_norm[occ], mla_w_uq[occ],
                              mla_w_ukv[occ], mla_w_out[occ], ctx_out)
        else:
            y, yc = window_sink_mixer(u, uc, swa_w_in[occ], swa_sink[occ], swa_w_out[occ], ctx_out)
        h = gated_residual(h, y, g[3], m, 3, 1.0)
        h = half_ffn(h, m, 6, g[4], g[5], ffn_w_in[i, 1], ffn_w_out[i, 1])
        if ctx_out:
            hc = gated_residual(hc, yc, g[3], mc, 3, 1.0)
            hc = half_ffn(hc, mc, 6, g[4], g[5], ffn_w_in[i, 1], ffn_w_out[i, 1])
    return h


def setup_inputs(seed=0):
    out = dict(first_inputs(seed))
    for name, value in second_inputs(seed + 1).items():
        if name != "x":
            out[name + "_2"] = value
    return out


def reference(
    x, positions, ln_mix_pre, ln_mix_post, ln_ffn_pre, ln_ffn_post, ffn_w_gate, ffn_w_up,
    ffn_w_down, ev_w_in, ev_pool_w, ev_pool_scale, ev_sgu_ln_g, ev_sgu_ln_b, ev_sgu_w, ev_sgu_b,
    ev_w_out, od_w_in, od_cmp_k_pos, od_cmp_k_w1, od_cmp_k_w2, od_cmp_v_pos, od_cmp_v_w1,
    od_cmp_v_w2, od_ret_gn_g, od_w_out, c_2, ctx_2, c_ctx_2, ada_w_2, ada_b_2, norm_g_2,
    ffn_w_in_2, ffn_w_out_2, da_w_in_2, da_lambda_2, da_subln_2, da_w_out_2, ga_w_in_2,
    ga_q_norm_2, ga_k_norm_2, ga_w_out_2, mla_w_in_2, mla_q_norm_2, mla_kv_norm_2, mla_w_uq_2,
    mla_w_ukv_2, mla_w_out_2, swa_w_in_2, swa_sink_2, swa_w_out_2,
):
    x = first_block(
        x, positions, ln_mix_pre, ln_mix_post, ln_ffn_pre, ln_ffn_post, ffn_w_gate, ffn_w_up,
        ffn_w_down, ev_w_in, ev_pool_w, ev_pool_scale, ev_sgu_ln_g, ev_sgu_ln_b, ev_sgu_w,
        ev_sgu_b, ev_w_out, od_w_in, od_cmp_k_pos, od_cmp_k_w1, od_cmp_k_w2, od_cmp_v_pos,
        od_cmp_v_w1, od_cmp_v_w2, od_ret_gn_g, od_w_out,
    )
    return second_block(
        x, c_2, ctx_2, c_ctx_2, ada_w_2, ada_b_2, norm_g_2, ffn_w_in_2, ffn_w_out_2, da_w_in_2,
        da_lambda_2, da_subln_2, da_w_out_2, ga_w_in_2, ga_q_norm_2, ga_k_norm_2, ga_w_out_2,
        mla_w_in_2, mla_q_norm_2, mla_kv_norm_2, mla_w_uq_2, mla_w_ukv_2, mla_w_out_2,
        swa_w_in_2, swa_sink_2, swa_w_out_2,
    )


_drawn_inputs = setup_inputs


def setup_inputs(seed=0):
    import zlib

    import numpy as np

    out = dict(_drawn_inputs(seed))
    spreads = {}
    factors = {'ev_sgu_ln_g': 2.706,
     'ev_sgu_ln_b': 6.956,
     'od_cmp_k_pos': 8.0,
     'norm_g_2': 4.208,
     'da_subln_2': 8.0,
     'ga_q_norm_2': 8.0,
     'ga_k_norm_2': 8.0}
    for name, (base, spread) in spreads.items():
        noise = np.random.default_rng([zlib.crc32(name.encode()), seed]).standard_normal(out[name].shape)
        drawn = base * np.exp(spread * noise) if base else spread * noise
        out[name] = __import__('jax').numpy.asarray(drawn.astype(out[name].dtype))
    for name, factor in factors.items():
        out[name] = (out[name] * factor).astype(out[name].dtype)
    return out
```

```python
from collections import namedtuple
from contextlib import ExitStack

import numpy as np
import concourse.bass as bass
from concourse import mybir

P = 128
D = 1024
KD = D // P
T = 256
T2 = 2 * T
F = 2816
KF = F // P
HALF = KF // 2
BLK = KD * 2 * P
DBLK = HALF * P
NADA = 9 * D // 256
NEG = -1.0e30
LAMBDA_INIT = 0.2

EV_IN, EV_OUT, OD_IN, OD_OUT, DA_IN, DA_OUT, GA_IN, GA_OUT, GU, DOWN = 6, 4, 14, 4, 12, 4, 6, 4, 2 * 11, 16
FFN = [(GU, BLK), (DOWN, DBLK)]
SEGMENTS = ([(EV_IN, BLK), (EV_OUT, BLK)] + FFN + [(OD_IN, BLK), (OD_OUT, BLK)] + FFN
            + FFN + [(DA_IN, BLK), (DA_OUT, BLK)] + FFN
            + FFN + [(GA_IN, BLK), (GA_OUT, BLK)] + FFN)
SIZES = [size for n, size in SEGMENTS for _ in range(n)]
NBLK = len(SIZES)

VEC_COLS = {}
_at = 0
for _name, _n in [("mix_pre", 16), ("mix_post", 16), ("ffn_pre", 16), ("ffn_post", 16), ("norm_g", 96),
                  ("pool_scale", 4), ("sgu_g", 4), ("sgu_b", 4), ("gn_g", 4), ("subln", 1), ("q_norm", 1),
                  ("k_norm", 1), ("ada_b", 144), ("c", 16), ("eps6", 1), ("eps5", 1), ("f_nsa", 1),
                  ("f_ret", 1), ("row_ok", 2), ("ident", 128), ("ones", 128), ("rot_nsa", 128),
                  ("rot_ret", 128), ("rot_ax", 128)]:
    VEC_COLS[_name] = (_at, _n)
    _at += _n
NVEC = _at
TAB_COLS = {}
_at = 0
for _name, _n in [("mask", 128), ("mask_c", 30), ("decay", 4 * 256), ("count", 64)]:
    TAB_COLS[_name] = (_at, _n)
    _at += _n
NTAB = _at

Mark = namedtuple("Mark", "sem n")


def build(nc, A, out):
    fp32, f32r, i32 = mybir.dt.float32, mybir.dt.float32r, mybir.dt.int32
    ACT, ALU, AX = mybir.ActivationFunctionType, mybir.AluOpType, mybir.AxisListType.X
    MUL, ADD, SUB = ALU.mult, ALU.add, ALU.subtract
    ds = bass.ds

    with ExitStack() as ctx:
        def sb(name, shape, dt=fp32):
            return ctx.enter_context(nc.sbuf_tensor(name, shape, dt))

        H = sb("H", [P, KD, T2])
        HN = [sb("HN_hi", [P, KD, T2], f32r), sb("HN_lo", [P, KD, T2], f32r)]
        Y = sb("Y", [P, KD, T2])
        RAW = [sb(f"raw{s}", [P, BLK]) for s in range(2)]
        WHI = [sb(f"whi{s}", [P, BLK], f32r) for s in range(2)]
        WLO = [sb(f"wlo{s}", [P, BLK], f32r) for s in range(2)]
        TMP = [sb(f"tmp{s}", [P, T2]) for s in range(2)]
        SQ = [sb(f"sq{s}", [P, T2]) for s in range(2)]
        ACC = sb("acc", [P, T2])
        RS = sb("rs", [P, T2])
        VEC = sb("VEC", [P, NVEC])
        MOD = sb("MOD", [P, 144, 2])
        GA = sb("GA", [P, 2, 6, KD, 2])
        SMALL = sb("SMALL", [P, 64])
        with ExitStack() as g:
            G = [g.enter_context(nc.sbuf_tensor("G_hi", [P, KF, T2], f32r)),
                 g.enter_context(nc.sbuf_tensor("G_lo", [P, KF, T2], f32r))]
        ARENA = sb("ARENA", [P, 2 * KF * T2])
        BANK = [ctx.enter_context(nc.psum_tensor(f"bank{n}", [P, 512], fp32)) for n in range(8)]
        sems = {}
        names = ["w_in0", "w_in1", "w_hi", "w_lo", "ada_used", "ada_out", "tile_done",
                 "evac", "gate_read", "up_done", "g_hi", "g_lo", "in_h", "in_vec", "in_tab", "sq",
                 "sq_sum", "total", "root", "rstd", "scaled", "hn_hi", "hn_lo", "resid", "act_c",
                 "pe_step", "act_step", "dve_step", "pool_step", "stored", "rows"]
        for n in names:
            sems[n] = ctx.enter_context(nc.semaphore(n))
        block = ctx.enter_context(nc.Block())

        def vec(name, a=0, n=None):
            at, size = VEC_COLS[name]
            return VEC[:, at + a:at + (size if n is None else a + n)]

        ident, ones = vec("ident"), vec("ones")

        def carve():
            at = [0]

            def piece(n, *dims, dt=None):
                size = n
                for d in dims:
                    size *= d
                ap = ARENA[:, at[0]:at[0] + size]
                at[0] += size
                assert at[0] <= 2 * KF * T2, at[0]
                if dt is not None:
                    ap = ap.bitcast(dt)
                if len(dims) == 1:
                    ap = ap.rearrange("p (a b) -> p a b", a=n)
                if len(dims) == 2:
                    ap = ap.rearrange("p (a b c) -> p a b c", a=n, b=dims[0])
                return ap
            return piece

        def program(pe=None, act=None, dve=None, pool=None, sp=None):
            count = dict.fromkeys(names, 0)
            NV, NS, NT, NG = nc.vector, nc.scalar, nc.tensor, nc.gpsimd

            def up(name, n=1):
                count[name] += n
                return Mark(sems[name], count[name])

            def now(name):
                return Mark(sems[name], count[name])

            split = [0]

            def loop(eng, n, body):
                if n > 1:
                    with eng.Fori(0, n - 1) as i:
                        body(i, False)
                body(n - 1, True)

            def load_weights():
                for s in range(2):
                    sp.dma_start(RAW[s][:, :], A["w_ada"][s]).then_inc(sems[f"w_in{s}"], 16)
                with sp.Fori(1, NADA) as i:
                    for s in range(2):
                        sp.wait_ge(sems["ada_used"], 2 * i + s - 1)
                        sp.dma_start(RAW[s][:, :], A["w_ada"][ds(2 * i + s, 1)].rearrange("a p n -> p (a n)"))\
                            .then_inc(sems[f"w_in{s}"], 16)
                n = n8 = nd = 0
                for blocks, size in SEGMENTS:
                    src, at = (A["w_main"], n8) if size == BLK else (A["w_down"], nd)
                    first = 1 if n == 0 else 0
                    if first:
                        for s in range(2):
                            sp.wait_ge(sems["ada_used"], 2 * NADA - 1 + s)
                            sp.dma_start(RAW[s][:, :], src[s]).then_inc(sems[f"w_in{s}"], 16)
                    with sp.Fori(first, blocks // 2) as i:
                        for s in range(2):
                            sp.wait_ge(sems["w_lo"], 2 * i + (n + s - 1))
                            sp.dma_start(RAW[s][:, 0:size], src[ds(2 * i + (at + s), 1)].rearrange("a p n -> p (a n)"))\
                                .then_inc(sems[f"w_in{s}"], 16)
                    n += blocks
                    if size == BLK:
                        n8 += blocks
                    else:
                        nd += blocks

            def split_hi(n, slot, size):
                act.wait_ge(sems[f"w_in{slot}"], n * 8 + (16 * (NADA + 1) - 8 * slot))
                NS.activation(WHI[slot][:, 0:size], RAW[slot][:, 0:size], ACT.Copy).then_inc(sems["w_hi"], 1)

            def split_lo(n, slot, size):
                dve.wait_ge(sems["w_hi"], n + 1)
                NV.tensor_tensor(WLO[slot][:, 0:size], RAW[slot][:, 0:size], WHI[slot][:, 0:size].bitcast(fp32), SUB)\
                    .then_inc(sems["w_lo"], 1)

            def ahead(fn, n, step, last, static):
                if last:
                    if static + 2 < NBLK:
                        fn(static + 2, (static + 2) % 2, SIZES[static + 2])
                else:
                    fn(n + 2, step % 2, SIZES[static])

            def three(bank, N, w, x, col, kt, wk, x0=0, start=True, stop=True):
                steps = [(a, b, k) for a, b in ((0, 0), (0, 1), (1, 0)) for k in range(kt)]
                for j, (a, b, k) in enumerate(steps):
                    mm = NT.matmul(bank[:, 0:N], (WHI, WLO)[a][w][:, k * wk + col:k * wk + col + P],
                                   x[b][:, x0 + k, 0:N], start=start and j == 0, stop=stop and j == len(steps) - 1)
                return mm

            def linear(blocks, N, dst, ready):
                n0, e0, t0 = split[0], count["evac"], count["tile_done"]
                bodies = blocks // 2
                if pe:
                    for m in ready:
                        pe.wait_ge(*m)

                    def body(i, last):
                        for s in range(2):
                            pe.wait_ge(sems["w_lo"], 2 * i + (n0 + s + 1))
                            for m in range(2):
                                if e0:
                                    pe.wait_ge(sems["evac"], 4 * i + (e0 + 2 * s + m - 3))
                                elif s == 0 and m == 0:
                                    pe.wait_ge(sems["evac"], 4 * i)
                                three(BANK[2 * s + m], N, s, HN, m * P, KD, 2 * P).then_inc(sems["tile_done"], 1)
                    loop(pe, bodies, body)
                if act:
                    def body(i, last):
                        for s in range(2):
                            for m in range(2):
                                act.wait_ge(sems["tile_done"], 4 * i + (t0 + 2 * s + m + 1))
                                NS.activation(dst[:, ds(4 * i + (2 * s + m), 1), 0:N], BANK[2 * s + m][:, 0:N], ACT.Copy)\
                                    .then_inc(sems["evac"], 1)
                            ahead(split_hi, 2 * i + (n0 + s), s, last, n0 + s + (2 * bodies - 2 if last else 0))
                    loop(act, bodies, body)
                if dve:
                    def body(i, last):
                        for s in range(2):
                            ahead(split_lo, 2 * i + (n0 + s), s, last, n0 + s + (2 * bodies - 2 if last else 0))
                    loop(dve, bodies, body)
                split[0] += blocks
                up("tile_done", 2 * blocks)
                return up("evac", 2 * blocks)

            def ffn(N, ready):
                n0, t0 = split[0], count["tile_done"]
                g0, u0, h0, l0 = (count[x] for x in ("gate_read", "up_done", "g_hi", "g_lo"))
                bodies = GU // 2
                if pe:
                    for m in ready:
                        pe.wait_ge(*m)

                    def body(i, last):
                        for s in range(2):
                            pe.wait_ge(sems["w_lo"], 2 * i + (n0 + s + 1))
                            pe.wait_ge(sems["gate_read" if s == 0 else "up_done"], 2 * i + (u0 if s else g0))
                            for m in range(2):
                                three(BANK[2 * s + m], N, s, HN, m * P, KD, 2 * P).then_inc(sems["tile_done"], 1)
                    loop(pe, bodies, body)
                if act:
                    def body(i, last):
                        stat = n0 + (2 * bodies - 2 if last else 0)
                        for m in range(2):
                            act.wait_ge(sems["tile_done"], 4 * i + (t0 + m + 1))
                            act.wait_ge(sems["g_lo"], 2 * i + l0)
                            NS.activation(TMP[m][:, 0:N], BANK[m][:, 0:N], ACT.Silu).then_inc(sems["gate_read"], 1)
                        ahead(split_hi, 2 * i + n0, 0, last, stat)
                        act.wait_ge(sems["tile_done"], 4 * i + (t0 + 4))
                        ahead(split_hi, 2 * i + (n0 + 1), 1, last, stat + 1)
                        for m in range(2):
                            act.wait_ge(sems["up_done"], 2 * i + (u0 + m + 1))
                            NS.activation(G[0][:, ds(2 * i + m, 1), 0:N], TMP[m][:, 0:N], ACT.Copy)\
                                .then_inc(sems["g_hi"], 1)
                    loop(act, bodies, body)
                if dve:
                    def body(i, last):
                        stat = n0 + (2 * bodies - 2 if last else 0)
                        ahead(split_lo, 2 * i + n0, 0, last, stat)
                        for m in range(2):
                            dve.wait_ge(sems["gate_read"], 2 * i + (g0 + m + 1))
                            dve.wait_ge(sems["tile_done"], 4 * i + (t0 + 2 + m + 1))
                            NV.tensor_tensor(TMP[m][:, 0:N], TMP[m][:, 0:N], BANK[2 + m][:, 0:N], MUL)\
                                .then_inc(sems["up_done"], 1)
                        ahead(split_lo, 2 * i + (n0 + 1), 1, last, stat + 1)
                        for m in range(2):
                            dve.wait_ge(sems["g_hi"], 2 * i + (h0 + m + 1))
                            NV.tensor_tensor(G[1][:, ds(2 * i + m, 1), 0:N], TMP[m][:, 0:N],
                                             G[0][:, ds(2 * i + m, 1), 0:N].bitcast(fp32), SUB).then_inc(sems["g_lo"], 1)
                    loop(dve, bodies, body)
                split[0] += GU
                up("tile_done", 2 * GU)
                for x in ("gate_read", "up_done", "g_hi"):
                    up(x, KF)
                hidden = up("g_lo", KF)

                n1, t1, e1 = split[0], count["tile_done"], count["evac"]
                bodies = KD // 2
                if pe:
                    pe.wait_ge(*hidden)
                    pe.wait_ge(*now("gate_read"))

                    def body(i, last):
                        for m in range(2):
                            pe.wait_ge(sems["evac"], 2 * i + (e1 + m - 1))
                            for s in range(2):
                                pe.wait_ge(sems["w_lo"], 4 * i + (n1 + 2 * m + s + 1))
                                mm = three(BANK[m], N, s, G, 0, HALF, P, s * HALF, s == 0, s == 1)
                                if s == 0:
                                    mm.then_inc(sems["tile_done"], 1)
                            mm.then_inc(sems["tile_done"], 1)
                    loop(pe, bodies, body)
                if act:
                    def body(i, last):
                        stat = n1 + (4 * bodies - 4 if last else 0)
                        for m in range(2):
                            for s in range(2):
                                j = 2 * m + s
                                act.wait_ge(sems["tile_done"], 4 * i + (t1 + j + 1))
                                if s == 1:
                                    NS.activation(Y[:, ds(2 * i + m, 1), 0:N], BANK[m][:, 0:N], ACT.Copy)\
                                        .then_inc(sems["evac"], 1)
                                ahead(split_hi, 4 * i + (n1 + j), s, last, stat + j)
                    loop(act, bodies, body)
                if dve:
                    def body(i, last):
                        stat = n1 + (4 * bodies - 4 if last else 0)
                        for j in range(4):
                            ahead(split_lo, 4 * i + (n1 + j), j % 2, last, stat + j)
                    loop(dve, bodies, body)
                split[0] += DOWN
                up("tile_done", DOWN)
                return up("evac", KD)


            def on(eng, *marks):
                if eng is None:
                    return False
                for m in marks:
                    if m is not None:
                        eng.wait_ge(*m)
                return True

            def bcast(ap, *shape):
                return ap.to_broadcast([P, *shape])

            def norm(src, N, groups, ready, residual=False):
                q0, s0, h0, l0 = (count[x] for x in ("sq", "sq_sum", "hn_hi", "hn_lo"))
                if act:
                    for m in ready:
                        act.wait_ge(*m)
                    for k in range(KD):
                        if k >= 3:
                            act.wait_ge(sems["sq_sum"], s0 + k - 2)
                        NS.activation((SQ[k % 2] if k else ACC)[:, 0:N], src[:, k, 0:N], ACT.Square).then_inc(sems["sq"], 1)
                if dve:
                    for k in range(1, KD):
                        dve.wait_ge(sems["sq"], q0 + k + 1)
                        if k >= 2:
                            dve.wait_ge(sems["sq_sum"], s0 + k - 1)
                        NV.tensor_tensor(ACC[:, 0:N], ACC[:, 0:N], SQ[k % 2][:, 0:N], ADD).then_inc(sems["sq_sum"], 1)
                up("sq", KD)
                summed = up("sq_sum", KD - 1)
                total = up("total")
                if on(pe, summed):
                    NT.matmul(BANK[7][:, 0:N], ones, ACC[:, 0:N], start=True, stop=True).then_inc(total.sem, 1)
                root = up("root")
                if on(act, total):
                    NS.activation(RS[:, 0:N], BANK[7][:, 0:N], ACT.Sqrt, bias=vec("eps6"), scale=1.0 / D).then_inc(root.sem, 1)
                rstd = up("rstd")
                if on(dve, root):
                    NV.reciprocal(RS[:, 0:N], RS[:, 0:N]).then_inc(rstd.sem, 1)
                c0, r0 = count["scaled"], count["resid"]
                if dve:
                    dve.wait_ge(*rstd)
                    for k in range(KD + 1):
                        if k < KD:
                            if not residual and k >= 2:
                                dve.wait_ge(sems["hn_lo"], l0 + k - 1)
                            if residual and k >= 2:
                                dve.wait_ge(sems["resid"], r0 + k - 1)
                            for j, (c, n, gain, shift) in enumerate(groups):
                                op = NV.scalar_tensor_tensor(TMP[k % 2][:, c:c + n], src[:, k, c:c + n], gain(k), RS[:, c:c + n], MUL, MUL)
                            op.then_inc(sems["scaled"], 1)
                        if k and residual:
                            dve.wait_ge(sems["scaled"], c0 + k)
                            NV.tensor_tensor(H[:, k - 1, 0:N], H[:, k - 1, 0:N], TMP[(k - 1) % 2][:, 0:N], ADD)\
                                .then_inc(sems["resid"], 1)
                        elif k:
                            dve.wait_ge(sems["hn_hi"], h0 + k)
                            for j, (c, n, gain, shift) in enumerate(groups):
                                t, hi = TMP[(k - 1) % 2][:, c:c + n], HN[0][:, k - 1, c:c + n].bitcast(fp32)
                                if shift is None:
                                    op = NV.tensor_tensor(HN[1][:, k - 1, c:c + n], t, hi, SUB)
                                else:
                                    op = NV.scalar_tensor_tensor(HN[1][:, k - 1, c:c + n], t, shift(k - 1), hi, ADD, SUB)
                            op.then_inc(sems["hn_lo"], 1)
                if act and not residual:
                    for k in range(KD):
                        act.wait_ge(sems["scaled"], c0 + k + 1)
                        for j, (c, n, gain, shift) in enumerate(groups):
                            if shift is None:
                                op = NS.activation(HN[0][:, k, c:c + n], TMP[k % 2][:, c:c + n], ACT.Copy)
                            else:
                                op = NS.activation(HN[0][:, k, c:c + n], TMP[k % 2][:, c:c + n], ACT.Identity, bias=shift(k))
                        op.then_inc(sems["hn_hi"], 1)
                up("scaled", KD)
                if residual:
                    return [up("resid", KD)]
                up("hn_hi", KD)
                return [up("hn_lo", KD)]

            def keep_split(src, k, cols, *ready):
                hi = up("hn_hi")
                if on(act, *ready):
                    NS.activation(HN[0][:, k, cols], src, ACT.Copy).then_inc(hi.sem, 1)
                lo = up("hn_lo")
                if on(dve, hi):
                    NV.tensor_tensor(HN[1][:, k, cols], src, HN[0][:, k, cols].bitcast(fp32), SUB).then_inc(lo.sem, 1)
                return lo

            def rope(tiles, rot, cos, sin, ready):
                free = [ready, ready]
                for j, t in enumerate(tiles):
                    turned = up("pe_step")
                    if on(pe, free[j % 2], ready):
                        NT.matmul(BANK[4 + j % 2][:, 0:T], rot, t, start=True, stop=True).then_inc(turned.sem, 1)
                    part = up("dve_step")
                    if on(dve, turned):
                        NV.tensor_tensor(TMP[j % 2][:, 0:T], BANK[4 + j % 2][:, 0:T], sin, MUL).then_inc(part.sem, 1)
                    free[j % 2] = part
                    straight = up("dve_step")
                    if on(dve):
                        NV.tensor_tensor(t, t, cos, MUL).then_inc(straight.sem, 1)
                    done = up("dve_step")
                    if on(dve, straight):
                        NV.tensor_tensor(t, t, TMP[j % 2][:, 0:T], ADD).then_inc(done.sem, 1)
                return done

            def tile_norm(items, N, gain, extra, ready):
                free = [None, None]
                for j, (src, k) in enumerate(items):
                    b = j % 2
                    sq = up("act_step")
                    if on(act, free[b], *ready):
                        NS.activation(SQ[b][:, 0:N], src, ACT.Square).then_inc(sq.sem, 1)
                    total = up("pe_step")
                    if on(pe, sq):
                        NT.matmul(BANK[4 + b][:, 0:N], ones, SQ[b][:, 0:N], start=True, stop=True).then_inc(total.sem, 1)
                    root = up("act_step")
                    if on(act, total):
                        NS.activation(SQ[b][:, 0:N], BANK[4 + b][:, 0:N], ACT.Sqrt, bias=vec("eps6"), scale=1.0 / P)\
                            .then_inc(root.sem, 1)
                    inv = up("dve_step")
                    if on(dve, root):
                        NV.reciprocal(SQ[b][:, 0:N], SQ[b][:, 0:N]).then_inc(inv.sem, 1)
                    done = up("dve_step")
                    if on(dve, inv):
                        NV.scalar_tensor_tensor(src, src, gain, SQ[b][:, 0:N], MUL, MUL).then_inc(done.sem, 1)
                    free[b] = done
                    if k is not None:
                        if extra is not None:
                            more = up("dve_step")
                            if on(dve, done):
                                NV.tensor_scalar(src, src, extra, None, MUL).then_inc(more.sem, 1)
                            done = more
                        done = keep_split(src, k, slice(0, N), done)
                return done

            def by_token(src, dst, ready, free=None):
                last = [free, free]
                for j in range(0, len(src), 4):
                    b = (j // 4) % 2
                    turned = up("pe_step")
                    n = min(4, len(src) - j)
                    if on(pe, last[b], ready):
                        for m in range(n):
                            mm = NT.transpose(BANK[4 + b][:, m * P:(m + 1) * P], src[j + m], ident)
                        mm.then_inc(turned.sem, 1)
                    kept = up("act_step")
                    if on(act, turned):
                        for m in range(n):
                            cp = NS.activation(dst[j + m], BANK[4 + b][:, m * P:(m + 1) * P], ACT.Copy)
                        cp.then_inc(kept.sem, 1)
                    last[b] = kept
                return kept

            in_h, in_vec = up("in_h", 16), up("in_vec", 16)
            if act:
                act.dma_start(VEC[:, :], A["vec"]).then_inc(in_vec.sem, 16)
                act.dma_start(H[:, :, :], A["x0"]).then_inc(in_h.sem, 16)
            if sp:
                load_weights()

            silu_c = up("act_c")
            C = SMALL[:, 48:64].rearrange("p (k s) -> p k s", s=2)
            if on(act, in_vec):
                NS.activation(SMALL[:, 48:64], vec("c"), ACT.Silu).then_inc(silu_c.sem, 1)
            if on(pe, silu_c):
                with pe.Fori(0, NADA) as i:
                    for s in range(2):
                        pe.wait_ge(sems[f"w_in{s}"], 16 * i + 16)
                        if s == 0:
                            pe.wait_ge(sems["ada_out"], i)
                        for m in range(2):
                            for k in range(KD):
                                mm = NT.matmul(BANK[4][:, 4 * s + 2 * m:4 * s + 2 * m + 2],
                                               RAW[s][:, k * 2 * P + m * P:k * 2 * P + (m + 1) * P], C[:, k, :],
                                               start=k == 0, stop=k == KD - 1)
                        mm.then_inc(sems["ada_used"], 1)
            if dve:
                with dve.Fori(0, NADA) as i:
                    dve.wait_ge(sems["ada_used"], 2 * i + 2)
                    NV.tensor_tensor(MOD[:, ds(4 * i, 4), :], BANK[4][:, 0:8].rearrange("p (a s) -> p a s", s=2),
                                     vec("ada_b")[:, ds(4 * i, 4)].unsqueeze(2).to_broadcast([P, 4, 2]), ADD)\
                        .then_inc(sems["ada_out"], 1)
            up("ada_used", 2 * NADA)
            mods = up("ada_out", NADA)
            gains = None
            for L in range(2):
                for j in range(3):
                    def mod(row):
                        return MOD[:, 72 * L + 8 * row:72 * L + 8 * row + 8, :]

                    def g(n):
                        return vec("norm_g", (6 * L + n) * KD, KD).unsqueeze(2).to_broadcast([P, KD, 2])
                    pre, post = up("dve_step"), up("dve_step")
                    if on(dve, mods):
                        NV.scalar_tensor_tensor(GA[:, L, j], mod(3 * j + 1), 1.0, g(2 * j), ADD, MUL).then_inc(pre.sem, 1)
                        NV.scalar_tensor_tensor(GA[:, L, 3 + j], mod(3 * j + 2), 1.0 if j == 1 else 0.5, g(2 * j + 1), MUL, MUL)\
                            .then_inc(post.sem, 1)
                    gains = post

            for n in range(2):
                if act:
                    split_hi(n, n, BLK)
                if dve:
                    split_lo(n, n, BLK)

            def gain1(name, layer):
                return [(0, T, lambda k: vec(name, layer * KD + k, 1), None)]

            piece = carve()
            Z = piece(12, T)
            DIFF = piece(4, T)
            W1, W2 = piece(T), piece(T)
            POOLW, SGUW, SGUB = piece(4, P), piece(4, P), piece(4, P)
            COUNT = piece(4, 16)
            VT = piece(8, P)
            ready = norm(H, T, gain1("mix_pre", 0), [in_h, in_vec])
            in_tab = up("in_tab", 64)
            if act:
                act.dma_start(POOLW, A["pool_w"]).then_inc(in_tab.sem, 16)
                act.dma_start(SGUW, A["sgu_w"]).then_inc(in_tab.sem, 16)
                act.dma_start(SGUB, A["sgu_b"]).then_inc(in_tab.sem, 16)
                act.dma_start(COUNT, A["tab_count"].rearrange("p (a b) -> p a b", a=4)).then_inc(in_tab.sem, 16)
            z = linear(EV_IN, T, Z, ready)

            sguw = up("pool_step")
            if on(pool, in_tab):
                NG.affine_select(out=SGUW, in_=SGUW, compare_op=ALU.is_ge, fill=0.0, base=0,
                                 pattern=[[0, 4], [1, P]], channel_multiplier=-1).then_inc(sguw.sem, 1)
            act_uv = up("act_step")
            if on(act, z):
                NS.activation(Z[:, 4:12, :], Z[:, 4:12, :], ACT.Gelu_apprx_tanh).then_inc(act_uv.sem, 1)

            last = z
            for g in range(4):
                a = Z[:, g, :]
                src, w = a, 1
                for level in range(g + 1):
                    dst = (W1, W2)[level % 2]
                    s1, s2 = up("dve_step"), up("dve_step")
                    if on(dve, last):
                        NV.tensor_copy(dst[:, 0:w], src[:, 0:w]).then_inc(s1.sem, 1)
                        NV.tensor_tensor(dst[:, w:T], src[:, w:T], src[:, 0:T - w], ADD).then_inc(s2.sem, 1)
                    src, w, last = dst, 2 * w, s2
                d1, d2, d3 = up("dve_step"), up("dve_step"), up("dve_step")
                if on(dve, last):
                    NV.scalar_tensor_tensor(DIFF[:, g, w:T], src[:, w:T], 1.0 / w, a[:, w:T], MUL, SUB).then_inc(d1.sem, 1)
                    dve.wait_ge(*in_tab)
                    NV.tensor_tensor(DIFF[:, g, 0:w], src[:, 0:w], COUNT[:, g, 0:w], MUL).then_inc(d2.sem, 1)
                    dve.wait_ge(*d2)
                    NV.tensor_tensor(DIFF[:, g, 0:w], DIFF[:, g, 0:w], a[:, 0:w], SUB).then_inc(d3.sem, 1)
                last = d3
                pooled = up("pe_step")
                if on(pe, d3, in_tab):
                    NT.matmul(BANK[g][:, 0:T], POOLW[:, g, :], DIFF[:, g, :], start=True, stop=True).then_inc(pooled.sem, 1)
                scaled = up("act_step")
                if on(act, pooled):
                    NS.activation(DIFF[:, g, :], BANK[g][:, 0:T], ACT.Copy, scale=vec("pool_scale", g, 1)).then_inc(scaled.sem, 1)
                mixed = keep_split(DIFF[:, g, :], g, slice(0, T), scaled)

            V = Z[:, 8:12, :]

            def feature_sum(src, b, m0):
                s1, s2, s3, tot = up("dve_step"), up("dve_step"), up("dve_step"), up("pe_step")
                if on(dve, m0):
                    NV.tensor_tensor(W1, src[:, 0, :], src[:, 1, :], ADD).then_inc(s1.sem, 1)
                    NV.tensor_tensor(W2, src[:, 2, :], src[:, 3, :], ADD).then_inc(s2.sem, 1)
                    dve.wait_ge(*s2)
                    NV.tensor_tensor(W1, W1, W2, ADD).then_inc(s3.sem, 1)
                if on(pe, s3):
                    NT.matmul(BANK[b][:, 0:T], ones, W1, start=True, stop=True).then_inc(tot.sem, 1)
                return tot

            tot = feature_sum(V, 4, act_uv)
            mu = up("act_step")
            if on(act, tot):
                NS.activation(RS[:, 0:T], BANK[4][:, 0:T], ACT.Copy, scale=1.0 / 512).then_inc(mu.sem, 1)
            cen = up("dve_step")
            if on(dve, mu):
                NV.tensor_tensor(V, V, RS[:, 0:T].unsqueeze(1).to_broadcast([P, 4, T]), SUB).then_inc(cen.sem, 1)
            vsq = up("act_step")
            if on(act, cen, mixed):
                NS.activation(DIFF, V, ACT.Square).then_inc(vsq.sem, 1)
            tot = feature_sum(DIFF, 5, vsq)
            root = up("act_step")
            if on(act, tot):
                NS.activation(RS[:, 0:T], BANK[5][:, 0:T], ACT.Sqrt, bias=vec("eps5"), scale=1.0 / 512).then_inc(root.sem, 1)
            inv = up("dve_step")
            if on(dve, root):
                NV.reciprocal(RS[:, 0:T], RS[:, 0:T]).then_inc(inv.sem, 1)
            nrm = up("dve_step")
            if on(dve, inv):
                NV.tensor_tensor(V, V, RS[:, 0:T].unsqueeze(1).to_broadcast([P, 4, T]), MUL).then_inc(nrm.sem, 1)
            aff = up("dve_step")
            if on(dve, nrm):
                for g in range(4):
                    op = NV.tensor_scalar(Z[:, 8 + g, :], Z[:, 8 + g, :], vec("sgu_g", g, 1), vec("sgu_b", g, 1), MUL, ADD)
                op.then_inc(aff.sem, 1)
            vt = by_token([Z[:, 8 + g, c * P:(c + 1) * P] for g in range(4) for c in range(2)], [VT[:, j, :] for j in range(8)], aff)
            for g in range(4):
                mm_done = up("pe_step")
                if on(pe, vt, sguw, mixed):
                    for c in range(2):
                        mm = NT.matmul(BANK[g][:, c * P:(c + 1) * P], VT[:, 2 * g + c, :], SGUW[:, g, :], start=True, stop=True)
                    mm.then_inc(mm_done.sem, 1)
                b1, b2 = up("dve_step"), up("dve_step")
                if on(dve, mm_done):
                    NV.tensor_tensor(DIFF[:, g, :].rearrange("p (c t) -> p c t", c=2), BANK[g][:, 0:T].rearrange("p (c t) -> p c t", c=2),
                                     SGUB[:, g, :].unsqueeze(1).to_broadcast([P, 2, P]), ADD).then_inc(b1.sem, 1)
                    dve.wait_ge(*b1)
                    NV.tensor_tensor(DIFF[:, g, :], DIFF[:, g, :], Z[:, 4 + g, :], MUL).then_inc(b2.sem, 1)
                mixed = keep_split(DIFF[:, g, :], 4 + g, slice(0, T), b2)
            y = linear(EV_OUT, T, Y, [mixed])
            res = norm(Y, T, gain1("mix_post", 0), [y], residual=True)
            ready = norm(H, T, gain1("ffn_pre", 0), res)
            y = ffn(T, ready)
            res = norm(Y, T, gain1("ffn_post", 0), [y], residual=True)

            piece = carve()
            Z = piece(28, T)
            MASK, MASKC, DECAY, POSI = piece(2 * P), piece(2, 15), piece(4, T), piece(T, dt=i32)
            CW1 = [piece(32, P), piece(32, P)]
            CW2 = piece(2, 64)
            CPOS = piece(2, 32)
            COSN, SINN, COSR, SINR = (piece(T) for _ in range(4))
            BLKS = piece(32, 15)
            HID = piece(4, 15)
            KCT, VC = piece(15), piece(P)
            VTOK = piece(4, P)
            GT = piece(2, 24)
            PB = [piece(2, T) for _ in range(2)]
            PC = [piece(15) for _ in range(2)]
            PT = [piece(5, P) for _ in range(2)]
            in_tab = up("in_tab", 8 * 16)
            if on(act, y):
                for dst, name in [(MASK, "tab_mask"), (MASKC, "tab_mask_c"), (DECAY, "tab_decay"), (POSI, "pos"),
                                  (CW1[0], "cmp_k_w1"), (CW1[1], "cmp_v_w1"), (CW2, "cmp_w2"), (CPOS, "cmp_pos")]:
                    act.dma_start(dst, A[name]).then_inc(in_tab.sem, 16)

            posf = up("dve_step")
            if on(dve, in_tab):
                NV.tensor_copy(ACC[:, 0:T], POSI).then_inc(posf.sem, 1)
            tables = []
            for f, cos, sin in (("f_nsa", COSN, SINN), ("f_ret", COSR, SINR)):
                m = [up("dve_step") for _ in range(11)]
                if on(dve, posf):
                    ang, q = RS[:, 0:T], RS[:, T:T2]
                    C1 = 6.28125
                    C2 = float(np.float32(np.round((2 * np.pi - C1) * 2**20) / 2**20))
                    C3 = float(2 * np.pi - C1 - C2)
                    PI = 3.1415925
                    NV.tensor_scalar(ang, ACC[:, 0:T], vec(f), None, MUL).then_inc(m[0].sem, 1)
                    dve.wait_ge(*m[0])
                    NV.tensor_scalar(q, ang, 1.0 / (2 * np.pi), 12582912.0, MUL, ADD).then_inc(m[1].sem, 1)
                    dve.wait_ge(*m[1])
                    NV.tensor_scalar(q, q, -12582912.0, None, ADD).then_inc(m[2].sem, 1)
                    for j, c in enumerate((C1, C2, C3)):
                        dve.wait_ge(*m[2 + j])
                        NV.scalar_tensor_tensor(ang, q, -c, ang, MUL, ADD).then_inc(m[3 + j].sem, 1)
                    dve.wait_ge(*m[5])
                    NV.tensor_scalar(sin, ang, PI, -PI, ALU.min, ALU.max).then_inc(m[6].sem, 1)
                    NV.tensor_scalar(cos, ang, 0.5 * np.pi, None, ADD).then_inc(m[7].sem, 1)
                    dve.wait_ge(*m[7])
                    NV.tensor_scalar(q, cos, PI, -2 * np.pi, ALU.is_gt, MUL).then_inc(m[8].sem, 1)
                    dve.wait_ge(*m[8])
                    NV.tensor_tensor(cos, cos, q, ADD).then_inc(m[9].sem, 1)
                    dve.wait_ge(*m[9])
                    NV.tensor_scalar(cos, cos, PI, -PI, ALU.min, ALU.max).then_inc(m[10].sem, 1)
                posf = m[10]
                tables.append(m[10])

            ready = norm(H, T, gain1("mix_pre", 1), res + [tables[1]])
            trig = up("act_step", 4)
            if on(act, tables[1]):
                for t in (COSN, SINN, COSR, SINR):
                    NS.activation(t, t, ACT.Sin).then_inc(trig.sem, 1)
            z = linear(OD_IN, T, Z, ready)

            turned = up("pe_step")
            if on(pe, z):
                for c in range(2):
                    mm = NT.transpose(BANK[6][:, c * P:(c + 1) * P], Z[:, 26, c * P:(c + 1) * P], ident)
                mm.then_inc(turned.sem, 1)
            th = up("act_step")
            if on(act, turned):
                NS.activation(GT, BANK[6][:, 0:T].rearrange("p (c g) -> p c g", c=2)[:, :, 0:24], ACT.Tanh, scale=0.5).then_inc(th.sem, 1)
            sg, ok = up("dve_step"), up("dve_step")
            if on(dve, th):
                NV.tensor_scalar(GT, GT, 0.5, 0.5, MUL, ADD).then_inc(sg.sem, 1)
                dve.wait_ge(*sg)
                for c in range(2):
                    op = NV.tensor_scalar(GT[:, c, 0:24:3], GT[:, c, 0:24:3], vec("row_ok", c, 1), None, MUL)
                op.then_inc(ok.sem, 1)
            gates = ok
            if dve:
                dve.wait_ge(*trig)
            roped = rope([Z[:, t, :] for t in (4, 6, 8, 0, 1, 2, 3)], vec("rot_nsa"), COSN, SINN, z)
            roped = rope([Z[:, t, :] for t in range(10, 18)], vec("rot_ret"), COSR, SINR, roped)

            last = roped
            for kv in range(2):
                blk = up("dve_step")
                src = Z[:, 4 + kv, :]
                win = bass.AP(tensor=src.tensor, offset=src.offset, ap=[list(src.ap[0]), [1, 32], [16, 15]])
                if on(dve, last):
                    NV.tensor_tensor(BLKS, win, CPOS[:, kv, :].unsqueeze(2).to_broadcast([P, 32, 15]), ADD).then_inc(blk.sem, 1)
                hid = up("pe_step")
                if on(pe, blk, gates):
                    for g in range(2):
                        for l in range(32):
                            mm = NT.matmul(BANK[2 * kv + g][:, 0:15], CW1[kv][64 * g:64 * g + 64, l, :],
                                           BLKS[64 * g:64 * g + 64, l, :], start=l == 0, stop=l == 31)
                    mm.then_inc(hid.sem, 1)
                ge = up("act_step")
                if on(act, hid):
                    for g in range(2):
                        op = NS.activation(HID[:, 2 * kv + g, :], BANK[2 * kv + g][:, 0:15], ACT.Gelu_apprx_tanh)
                    op.then_inc(ge.sem, 1)
                last = hid
            cmp_mm = up("pe_step")
            if on(pe, ge):
                for g in range(2):
                    NT.matmul(BANK[6][64 * g:64 * g + 64, 0:15], CW2[:, 0, :], HID[:, g, :], start=True, stop=True)
                for g in range(2):
                    mm = NT.matmul(BANK[7][0:15, 64 * g:64 * g + 64], HID[:, 2 + g, :], CW2[:, 1, :], start=True, stop=True)
                mm.then_inc(cmp_mm.sem, 1)
            cmp_kv = up("act_step")
            if on(act, cmp_mm):
                NS.activation(KCT, BANK[6][:, 0:15], ACT.Copy)
                NS.activation(VC[0:15, :], BANK[7][0:15, 0:P], ACT.Copy).then_inc(cmp_kv.sem, 1)
            vtok = by_token([Z[:, t, c * P:(c + 1) * P] for t in (7, 9) for c in range(2)], [VTOK[:, j, :] for j in range(4)], cmp_kv)

            units = [(j, qt, hf) for j in range(4) for qt in range(2) for hf in range(2)]
            S_MAX, S_NEG, S_SUM, S_CO = 0, 6, 12, 18

            def small(at, u, n=3):
                return SMALL[:, at + 3 * (u % 2):at + 3 * (u % 2) + n]
            probs, read_s, mult, trans, copied, pv = {}, {}, {}, {}, {}, {}
            o_kept = {}
            for u in range(len(units) + 1):
                if u < len(units):
                    j, qt, hf = units[u]
                    n, b, h64 = (qt + 1) * P, u % 2, slice(64 * hf, 64 * hf + 64)
                    sc = up("pe_step")
                    if on(pe, roped, vtok, read_s.get(u - 2)):
                        q = Z[h64, j, qt * P:(qt + 1) * P]
                        NT.matmul(BANK[2 + b][:, 0:15], q, KCT[h64, :], start=True, stop=True)
                        NT.matmul(BANK[b][:, 0:n], q, Z[h64, 6, 0:n], start=True, stop=True)
                        NT.matmul(BANK[b][:, T:T + n], q, Z[h64, 8, 0:n], start=True, stop=True).then_inc(sc.sem, 1)
                    m1, m2, m3, m4, m5 = (up("dve_step") for _ in range(5))
                    if on(dve, sc, trans.get(u - 2)):
                        NV.scalar_tensor_tensor(PC[b], BANK[2 + b][:, 0:15], 0.125, MASKC[:, qt, :], MUL, ADD).then_inc(m1.sem, 1)
                        NV.scalar_tensor_tensor(PB[b][:, :, 0:n], BANK[b][:, :].rearrange("p (a n) -> p a n", a=2)[:, :, 0:n], 0.125,
                                                MASK[:, 2 * P - n:2 * P].unsqueeze(1).to_broadcast([P, 2, n]), MUL, ADD).then_inc(m2.sem, 1)
                        dve.wait_ge(*m2)
                        NV.tensor_reduce(small(S_MAX, u, 1), PC[b], AX, ALU.max).then_inc(m3.sem, 1)
                        NV.tensor_reduce(small(S_MAX, u)[:, 1:3], PB[b][:, :, 0:n], AX, ALU.max).then_inc(m4.sem, 1)
                        dve.wait_ge(*m4)
                        NV.tensor_scalar(small(S_NEG, u), small(S_MAX, u), -1.0, None, MUL).then_inc(m5.sem, 1)
                    read_s[u] = m2
                    ex = up("act_step", 3)
                    if on(act, m5, mult.get(u - 2)):
                        NS.activation(PC[b], PC[b], ACT.Exp, bias=small(S_NEG, u)[:, 0:1], accum_out=small(S_SUM, u)[:, 0:1]).then_inc(ex.sem, 1)
                        for a in range(2):
                            NS.activation(PB[b][:, a, 0:n], PB[b][:, a, 0:n], ACT.Exp, bias=small(S_NEG, u)[:, 1 + a:2 + a],
                                          accum_out=small(S_SUM, u)[:, 1 + a:2 + a]).then_inc(ex.sem, 1)
                    probs[u] = ex
                if u >= 1:
                    w = u - 1
                    j, qt, hf = units[w]
                    n, b, h64 = (qt + 1) * P, w % 2, slice(64 * hf, 64 * hf + 64)
                    head = j + 4 * hf
                    m1, m2, m3 = up("dve_step"), up("dve_step"), up("dve_step")
                    if on(dve, probs[w], gates):
                        NV.reciprocal(small(S_CO, w), small(S_SUM, w)).then_inc(m1.sem, 1)
                        dve.wait_ge(*m1)
                        NV.tensor_tensor(small(S_CO, w), small(S_CO, w), GT[:, qt, 3 * head:3 * head + 3], MUL).then_inc(m2.sem, 1)
                        dve.wait_ge(*m2)
                        NV.tensor_scalar(PC[b], PC[b], small(S_CO, w)[:, 0:1], None, MUL)
                        for a in range(2):
                            op = NV.tensor_scalar(PB[b][:, a, 0:n], PB[b][:, a, 0:n], small(S_CO, w)[:, 1 + a:2 + a], None, MUL)
                        op.then_inc(m3.sem, 1)
                    mult[w] = m3
                    tr = up("pe_step")
                    if on(pe, m3, copied.get(w - 2)):
                        NT.transpose(BANK[2 + b][0:15, P:2 * P], PC[b], ident)
                        for a in range(2):
                            for c in range(qt + 1):
                                mm = NT.transpose(BANK[4 + b][:, (2 * a + c) * P:(2 * a + c + 1) * P], PB[b][:, a, c * P:(c + 1) * P], ident)
                        mm.then_inc(tr.sem, 1)
                    trans[w] = tr
                    cp = up("act_step")
                    if on(act, tr, pv.get(w - 2)):
                        NS.activation(PT[b][0:15, 4, :], BANK[2 + b][0:15, P:2 * P], ACT.Copy)
                        view = BANK[4 + b][:, :].rearrange("p (a c q) -> p a c q", a=2, c=2)[:, :, 0:qt + 1, :]
                        NS.activation(PT[b][:, 0:4, :].rearrange("p (a c) q -> p a c q", a=2)[:, :, 0:qt + 1, :], view, ACT.Copy)\
                            .then_inc(cp.sem, 1)
                    copied[w] = cp
                    o = up("pe_step")
                    ob = BANK[6 + (w // 2) % 2]
                    if on(pe, cp, o_kept.get(w // 2 - 2)):
                        dst = ob[h64, 0:P]
                        NT.matmul(dst, VC[0:15, 64 * hf:64 * hf + 64], PT[b][0:15, 4, :], start=True, stop=False)
                        for a in range(2):
                            for c in range(qt + 1):
                                mm = NT.matmul(dst, VTOK[:, 2 * a + c, 64 * hf:64 * hf + 64], PT[b][:, 2 * a + c, :],
                                               start=False, stop=a == 1 and c == qt)
                        mm.then_inc(o.sem, 1)
                    pv[w] = o
                    if hf == 1:
                        o_kept[w // 2] = keep_split(ob[:, 0:P], j, slice(qt * P, (qt + 1) * P), o)
            attended = o_kept[7]

            RV = CW1[0][:, 0:8, :]
            RSC = [CW1[1][:, 3 * b:3 * b + 3, :].rearrange("p a q -> p (a q)") for b in range(2)]
            RO = CW1[1][:, 8:16, :].rearrange("p a q -> p (a q)").rearrange("p (h t) -> p h t", h=4)
            rv = by_token([Z[:, 18 + h, c * P:(c + 1) * P] for h in range(4) for c in range(2)], [RV[:, j, :] for j in range(8)],
                          attended, attended)
            got, used_s = {}, {}
            for h in range(4):
                b = h % 2
                sc = up("pe_step")
                if on(pe, rv, used_s.get(h - 2)):
                    NT.matmul(BANK[b][:, 0:T], Z[:, 14 + h, 0:P], Z[:, 10 + h, :], start=True, stop=True)
                    NT.matmul(BANK[b][:, T:T + P], Z[:, 14 + h, P:T], Z[:, 10 + h, P:T], start=True, stop=True).then_inc(sc.sem, 1)
                de = up("dve_step")
                if on(dve, sc, got.get(h - 2)):
                    NV.tensor_tensor(RSC[b][:, 0:T], BANK[b][:, 0:T], DECAY[:, h, :], MUL)
                    NV.tensor_tensor(RSC[b][:, T:T + P], BANK[b][:, T:T + P], DECAY[:, h, 0:P], MUL).then_inc(de.sem, 1)
                used_s[h] = de
                ro = up("pe_step")
                if on(pe, de):
                    NT.matmul(BANK[2 + b][:, 0:T], RV[:, 2 * h, :], RSC[b][:, 0:T], start=True, stop=False)
                    NT.matmul(BANK[2 + b][:, P:T], RV[:, 2 * h + 1, :], RSC[b][:, T:T + P], start=False, stop=True).then_inc(ro.sem, 1)
                got[h] = ro
                cp = up("act_step")
                if on(act, ro):
                    NS.activation(RO[:, h, :], BANK[2 + b][:, 0:T], ACT.Copy).then_inc(cp.sem, 1)
                used_s[h] = cp
            sg = up("act_step")
            if on(act):
                NS.activation(Z[:, 22:26, :], Z[:, 22:26, :], ACT.Silu).then_inc(sg.sem, 1)
            for hh in range(2):
                o2 = RO[:, 2 * hh:2 * hh + 2, :].rearrange("p h t -> p (h t)")
                tot = up("pe_step")
                if on(pe, cp):
                    NT.matmul(BANK[4 + hh][:, :], ones, o2, start=True, stop=True).then_inc(tot.sem, 1)
                cen = up("dve_step")
                if on(dve, tot):
                    NV.scalar_tensor_tensor(o2, BANK[4 + hh][:, :], -1.0 / P, o2, MUL, ADD).then_inc(cen.sem, 1)
                sq = up("act_step")
                if on(act, cen):
                    NS.activation(SQ[hh][:, :], o2, ACT.Square).then_inc(sq.sem, 1)
                tot = up("pe_step")
                if on(pe, sq):
                    NT.matmul(BANK[6 + hh][:, :], ones, SQ[hh][:, :], start=True, stop=True).then_inc(tot.sem, 1)
                root = up("act_step")
                if on(act, tot):
                    NS.activation(SQ[hh][:, :], BANK[6 + hh][:, :], ACT.Sqrt, bias=vec("eps5"), scale=1.0 / P).then_inc(root.sem, 1)
                inv = up("dve_step")
                if on(dve, root):
                    NV.reciprocal(SQ[hh][:, :], SQ[hh][:, :]).then_inc(inv.sem, 1)
                for h in (2 * hh, 2 * hh + 1):
                    a1, a2 = up("dve_step"), up("dve_step")
                    if on(dve, inv, sg):
                        NV.scalar_tensor_tensor(RO[:, h, :], RO[:, h, :], vec("gn_g", h, 1), SQ[hh][:, (h % 2) * T:(h % 2 + 1) * T], MUL, MUL)\
                            .then_inc(a1.sem, 1)
                        dve.wait_ge(*a1)
                        NV.tensor_tensor(RO[:, h, :], RO[:, h, :], Z[:, 22 + h, :], MUL).then_inc(a2.sem, 1)
                    mixed = keep_split(RO[:, h, :], 4 + h, slice(0, T), a2)
            y = linear(OD_OUT, T, Y, [mixed])
            res = norm(Y, T, gain1("mix_post", 1), [y], residual=True)
            ready = norm(H, T, gain1("ffn_pre", 1), res)
            y = ffn(T, ready)
            res = norm(Y, T, gain1("ffn_post", 1), [y], residual=True)

            def pre(L, j, seqs=2):
                return [(T * s, T, lambda k, s=s: GA[:, L, j, k, s:s + 1], lambda k, s=s: MOD[:, 72 * L + 24 * j + k, s:s + 1])
                        for s in range(seqs)]

            def post(L, j, seqs=2):
                return [(T * s, T, lambda k, s=s: GA[:, L, 3 + j, k, s:s + 1], None) for s in range(seqs)]

            def attend(unit_list, scale, V, PB, PT, neg_lam, ready):
                exps, maxed, mult, trans, copied, pv, kept = {}, {}, {}, {}, {}, {}, {}

                def small(at, u, n=2):
                    return SMALL[:, at + 2 * (u % 2):at + 2 * (u % 2) + n]
                for u in range(len(unit_list) + 1):
                    if u < len(unit_list):
                        q, k, v, q0, k0, parts, dest = unit_list[u]
                        b, nk = u % 2, T2 - k0
                        sc = up("pe_step", len(parts))
                        if on(pe, exps.get(u - 2), *ready):
                            for a, pr in enumerate(parts):
                                NT.matmul(BANK[2 * b + a][:, 0:nk], q[pr, q0:q0 + P], k[pr, k0:T2], start=True, stop=True)\
                                    .then_inc(sc.sem, 1)
                        mx, ng = up("dve_step"), up("dve_step")
                        if on(dve, sc, exps.get(u - 2)):
                            for a in range(len(parts)):
                                op = NV.tensor_reduce(small(0, u)[:, a:a + 1], BANK[2 * b + a][:, 0:nk], AX, ALU.max)
                            op.then_inc(mx.sem, 1)
                            dve.wait_ge(*mx)
                            NV.tensor_scalar(small(4, u, len(parts)), small(0, u, len(parts)), -scale, None, MUL).then_inc(ng.sem, 1)
                        ex = up("act_step", len(parts))
                        if on(act, ng, mult.get(u - 2), trans.get(u - 2)):
                            for a in range(len(parts)):
                                NS.activation(PB[b][:, a, 0:nk], BANK[2 * b + a][:, 0:nk], ACT.Exp, bias=small(4, u)[:, a:a + 1],
                                              scale=scale, accum_out=small(8, u)[:, a:a + 1]).then_inc(ex.sem, 1)
                        exps[u] = ex
                    if u >= 1:
                        w = u - 1
                        q, k, v, q0, k0, parts, dest = unit_list[w]
                        b, nk = w % 2, T2 - k0
                        m1, m2, m3, m4 = (up("dve_step") for _ in range(4))
                        if on(dve, exps[w]):
                            NV.reciprocal(small(12, w, len(parts)), small(8, w, len(parts))).then_inc(m1.sem, 1)
                            dve.wait_ge(*m1)
                            if len(parts) == 2:
                                NV.tensor_tensor(small(12, w)[:, 1:2], small(12, w)[:, 1:2], neg_lam, MUL).then_inc(m2.sem, 1)
                                NV.tensor_scalar(PB[b][:, 0, 0:nk], PB[b][:, 0, 0:nk], small(12, w)[:, 0:1], None, MUL).then_inc(m3.sem, 1)
                                dve.wait_ge(*m3)
                                NV.scalar_tensor_tensor(PB[b][:, 0, 0:nk], PB[b][:, 1, 0:nk], small(12, w)[:, 1:2], PB[b][:, 0, 0:nk], MUL, ADD)\
                                    .then_inc(m4.sem, 1)
                            else:
                                NV.tensor_scalar(PB[b][:, 0, 0:nk], PB[b][:, 0, 0:nk], small(12, w)[:, 0:1], None, MUL).then_inc(m4.sem, 3)
                        mult[w] = m4
                        tr = up("pe_step")
                        if on(pe, m4, copied.get(w - 2)):
                            for c in range(nk // P):
                                mm = NT.transpose(BANK[4 + b][:, c * P:(c + 1) * P], PB[b][:, 0, c * P:(c + 1) * P], ident)
                            mm.then_inc(tr.sem, 1)
                        trans[w] = tr
                        cp = up("act_step")
                        if on(act, tr, pv.get(w - 2)):
                            NS.activation(PT[b][:, 0:nk], BANK[4 + b][:, 0:nk], ACT.Copy).then_inc(cp.sem, 1)
                        copied[w] = cp
                        o = up("pe_step")
                        if on(pe, cp, kept.get(w - 2)):
                            for c in range(nk // P):
                                mm = NT.matmul(BANK[6 + b][:, 0:P], V(k0 // P + c, v), PT[b][:, c * P:(c + 1) * P],
                                               start=c == 0, stop=c == nk // P - 1)
                            mm.then_inc(o.sem, 1)
                        pv[w] = o
                        ke = up("act_step")
                        if on(act, o):
                            NS.activation(Y[:, dest, q0:q0 + P], BANK[6 + b][:, 0:P], ACT.Copy)\
                                .then_inc(ke.sem, 1)
                        kept[w] = ke
                return ke

            ready = norm(H, T2, pre(0, 0), res + [gains])
            y = ffn(T2, ready)
            res = norm(Y, T2, post(0, 0), [y], residual=True)
            piece = carve()
            Z = piece(24, T2)
            VTK = piece(32, P)
            PB = [piece(2, T2) for _ in range(2)]
            PT = [piece(T2) for _ in range(2)]
            CS = piece(2, T)
            LAM = piece(4, 64)
            in_tab = up("in_tab", 32)
            if on(act, y):
                act.dma_start(CS, A["tab_da"]).then_inc(in_tab.sem, 16)
                act.dma_start(LAM, A["da_lambda"]).then_inc(in_tab.sem, 16)
            ready = norm(H, T2, pre(0, 1), res)
            z = linear(DA_IN, T2, Z, ready)
            l1, l2, l3 = up("dve_step"), up("dve_step"), up("dve_step")
            LP = SMALL[:, 16:24]
            if on(dve, in_tab, z):
                NV.tensor_tensor(LAM[:, 0, :], LAM[:, 0, :], LAM[:, 1, :], MUL).then_inc(l1.sem, 1)
                NV.tensor_tensor(LAM[:, 2, :], LAM[:, 2, :], LAM[:, 3, :], MUL).then_inc(l2.sem, 1)
                dve.wait_ge(*l2)
                NV.tensor_reduce(LP[:, 0:1], LAM[:, 0, :], AX, ADD)
                NV.tensor_reduce(LP[:, 1:2], LAM[:, 2, :], AX, ADD).then_inc(l3.sem, 1)
            le = up("act_step")
            if on(act, l3):
                NS.activation(LP[:, 2:4], LP[:, 0:2], ACT.Exp).then_inc(le.sem, 1)
            l4, l5 = up("dve_step"), up("dve_step")
            if on(dve, le):
                NV.tensor_tensor(LP[:, 4:5], LP[:, 3:4], LP[:, 2:3], SUB).then_inc(l4.sem, 1)
                dve.wait_ge(*l4)
                NV.tensor_scalar(LP[:, 5:6], LP[:, 4:5], -LAMBDA_INIT, None, ADD).then_inc(l5.sem, 1)
            vt = by_token([Z[:, 16 + h, c * P:(c + 1) * P] for c in range(4) for h in range(8)], [VTK[:, j, :] for j in range(32)], z)
            roped = rope([Z[:, t, 0:T] for t in range(16)], vec("rot_ax"), CS[:, 0, :], CS[:, 1, :], vt)
            both = (slice(0, 64), slice(64, P))
            units = [(Z[:, h, :], Z[:, 8 + h, :], h, qt * P, 0 if qt < 2 else T, both, h) for h in range(8) for qt in range(4)]
            o = attend(units, 0.125, lambda c, h: VTK[:, 8 * c + h, :], PB, PT, LP[:, 5:6], [roped, l5])
            mixed = tile_norm([(Y[:, h, :], h) for h in range(8)], T2, vec("subln"), 1.0 - LAMBDA_INIT, [o])
            y = linear(DA_OUT, T2, Y, [mixed])
            res = norm(Y, T2, post(0, 1), [y], residual=True)
            ready = norm(H, T2, pre(0, 2), res)
            y = ffn(T2, ready)
            res = norm(Y, T2, post(0, 2), [y], residual=True)

            ready = norm(H, T2, pre(1, 0), res)
            y = ffn(T2, ready)
            res = norm(Y, T2, post(1, 0), [y], residual=True)
            piece = carve()
            Z = piece(12, T2)
            VTK = piece(8, P)
            PB = [piece(2, T2) for _ in range(2)]
            PT = [piece(T2) for _ in range(2)]
            CS = piece(2, T)
            in_tab = up("in_tab", 16)
            if on(act, y):
                act.dma_start(CS, A["tab_ga"]).then_inc(in_tab.sem, 16)
            ready = norm(H, T2, pre(1, 1), res)
            z = linear(GA_IN, T2, Z, ready)
            nq = tile_norm([(Z[:, t, 0:T], None) for t in range(8)], T, vec("q_norm"), None, [z])
            nk = tile_norm([(Z[:, t, :], None) for t in (8, 9)], T2, vec("k_norm"), None, [nq])
            vt = by_token([Z[:, 10 + g, c * P:(c + 1) * P] for c in range(4) for g in range(2)], [VTK[:, j, :] for j in range(8)], nk)
            if dve:
                dve.wait_ge(*in_tab)
            roped = rope([Z[:, t, 0:T] for t in range(10)], vec("rot_ax"), CS[:, 0, :], CS[:, 1, :], vt)
            full = (slice(0, P),)
            units = [(Z[:, h, :], Z[:, 8 + h // 4, :], h // 4, qt * P, 0, full, h) for h in range(8) for qt in range(2)]
            o = attend(units, float(np.float32(P ** -0.5)), lambda c, g: VTK[:, 2 * c + g, :], PB, PT, None, [roped, vt])
            last = o
            for h in range(8):
                last = keep_split(Y[:, h, 0:T], h, slice(0, T), o)
            y = linear(GA_OUT, T, Y, [last])
            res = norm(Y, T, post(1, 1, 1), [y], residual=True)
            ready = norm(H, T, pre(1, 2, 1), res)
            y = ffn(T, ready)
            res = norm(Y, T, post(1, 2, 1), [y], residual=True)
            finish(sp, res)

        def finish(sp, res):
            if sp:
                for m in res:
                    sp.wait_ge(*m)
                sp.dma_start(out, H[:, :, 0:T]).then_inc(sems["stored"], 16)
                sp.wait_ge(sems["stored"], 16)

        @block.sync
        def _(eng):
            program(sp=eng)

        @block.gpsimd
        def _(eng):
            program(pool=eng)

        @block.scalar
        def _(eng):
            program(act=eng)

        @block.vector
        def _(eng):
            program(dve=eng)

        @block.tensor
        def _(eng):
            program(pe=eng)


def by_feature(a):
    return np.ascontiguousarray(a.reshape(-1, P).T)


def main_blocks(w):
    return w.reshape(KD, P, -1, 256).transpose(2, 1, 0, 3).reshape(-1, P, BLK)


def down_blocks(w):
    return w.reshape(2, HALF, P, KD, P).transpose(3, 0, 2, 1, 4).reshape(-1, P, DBLK)


def gate_up_blocks(gate, up):
    return np.stack([main_blocks(gate), main_blocks(up)], axis=1).reshape(-1, P, BLK)


def axial(rot_dim, heads):
    rows = T // 64
    row = np.repeat(np.arange(rows), 64).astype(np.float32)
    col = np.tile(np.arange(64), rows).astype(np.float32)
    n = rot_dim // 4
    freqs = np.float32(10000.0) ** (-np.arange(n, dtype=np.float32) / np.float32(n))
    ang = np.concatenate([row[:, None] * freqs, col[:, None] * freqs], axis=-1)
    both = np.stack([np.cos(ang), np.sin(ang)]).astype(np.float32)
    return np.ascontiguousarray(np.tile(np.repeat(both, 2, axis=2), (1, 1, heads)).transpose(2, 0, 1))


def rotations():
    nsa, ret, ax = (np.zeros((P, P), np.float32) for _ in range(3))
    for b in (0, 64):
        for j in range(8):
            nsa[b + 8 + j, b + j], nsa[b + j, b + 8 + j] = -1, 1
    for j in range(64):
        ret[64 + j, j], ret[j, 64 + j] = -1, 1
        ax[2 * j + 1, 2 * j], ax[2 * j, 2 * j + 1] = -1, 1
    return nsa, ret, ax


def tables():
    t, f32 = np.arange(P), np.float32
    mask = np.zeros((P, 2 * P), f32)
    mask[:, P:] = np.where(t[None, :] <= t[:, None], 0, NEG)
    tq = np.arange(T).reshape(2, P)
    mask_c = np.where(np.arange(15) * 16 + 31 <= tq[:, :, None], 0, NEG).astype(f32).transpose(1, 0, 2)
    row_ok = (tq >= 31).astype(f32).T
    log_gamma = np.log1p(-np.exp2(-5.0 - np.arange(4)))
    rel = t[None, :] - t[:, None]
    same = np.where(rel[:, None] >= 0, np.exp(np.maximum(rel, 0)[:, None] * log_gamma[:, None]), 0)
    cross = np.exp((rel + P)[:, None] * log_gamma[:, None])
    decay = (np.concatenate([same, cross], axis=2) * P ** -0.5).astype(f32)
    count = np.stack([1.0 / np.minimum(np.arange(16) + 1, 2 ** (g + 1)) for g in range(4)]).reshape(1, 64)
    inv = 1.0 / f32(500000.0) ** (np.arange(0, 16, 2, dtype=f32) / f32(16))
    f_nsa = np.zeros(P, f32)
    for b in (0, 8, 64, 72):
        f_nsa[b:b + 8] = inv
    inv = 1.0 / f32(10000.0) ** (np.arange(0, P, 2, dtype=f32) / f32(P))
    return dict(mask=mask, mask_c=np.ascontiguousarray(mask_c), row_ok=row_ok, decay=decay,
                count=np.tile(count, (P, 1)).astype(f32), f_nsa=f_nsa[:, None], f_ret=np.tile(inv, 2)[:, None])


def kernel(**inputs):
    import concourse.bacc as bacc
    from concourse.bass_utils import run_bass_kernel_spmd

    I = {k: np.asarray(v) for k, v in inputs.items()}
    f32 = np.float32
    tab = tables()
    nsa, ret, ax = rotations()

    w = I["od_w_in"][0]
    heads = [h for j in range(4) for h in (j, j + 4)]
    cols = np.concatenate([np.arange(64 * h, 64 * h + 64) for h in heads] + [np.arange(512, 1280), np.arange(1304, 3352), np.arange(1280, 1304)])
    od_in = np.concatenate([w[:, cols], np.zeros((D, 28 * P - len(cols)), f32)], axis=1)
    rows = np.concatenate([np.arange(64 * h, 64 * h + 64) for h in heads] + [np.arange(512, 1024)])
    F2 = I["ffn_w_in_2"]
    main = [main_blocks(I["ev_w_in"][0]), main_blocks(I["ev_w_out"][0]),
            gate_up_blocks(I["ffn_w_gate"][0], I["ffn_w_up"][0]),
            main_blocks(od_in), main_blocks(I["od_w_out"][0][rows]),
            gate_up_blocks(I["ffn_w_gate"][1], I["ffn_w_up"][1]),
            gate_up_blocks(F2[0, 0][:, :F], F2[0, 0][:, F:]), main_blocks(I["da_w_in_2"][0]), main_blocks(I["da_w_out_2"][0]),
            gate_up_blocks(F2[0, 1][:, :F], F2[0, 1][:, F:]),
            gate_up_blocks(F2[1, 0][:, :F], F2[1, 0][:, F:]), main_blocks(I["ga_w_in_2"][0]), main_blocks(I["ga_w_out_2"][0]),
            gate_up_blocks(F2[1, 1][:, :F], F2[1, 1][:, F:])]
    down = [down_blocks(a) for a in (I["ffn_w_down"][0], I["ffn_w_down"][1], *I["ffn_w_out_2"].reshape(4, F, D))]

    parts = dict(
        mix_pre=by_feature(I["ln_mix_pre"]), mix_post=by_feature(I["ln_mix_post"]), ffn_pre=by_feature(I["ln_ffn_pre"]),
        ffn_post=by_feature(I["ln_ffn_post"]), norm_g=by_feature(I["norm_g_2"]), pool_scale=by_feature(I["ev_pool_scale"]),
        sgu_g=by_feature(I["ev_sgu_ln_g"]), sgu_b=by_feature(I["ev_sgu_ln_b"]), gn_g=by_feature(I["od_ret_gn_g"]),
        subln=by_feature(I["da_subln_2"]), q_norm=by_feature(I["ga_q_norm_2"]), k_norm=by_feature(I["ga_k_norm_2"]),
        ada_b=by_feature(I["ada_b_2"]),
        c=np.stack([by_feature(I["c_2"]), by_feature(I["c_ctx_2"])], axis=2).reshape(P, 16),
        eps6=np.full((P, 1), 1e-6, f32), eps5=np.full((P, 1), 1e-5, f32), f_nsa=tab["f_nsa"], f_ret=tab["f_ret"],
        row_ok=tab["row_ok"], ident=np.eye(P, dtype=f32), ones=np.ones((P, P), f32), rot_nsa=nsa, rot_ret=ret, rot_ax=ax)
    arrays = {
        "w_main": np.concatenate(main), "w_down": np.concatenate(down),
        "w_ada": np.concatenate([main_blocks(a) for a in I["ada_w_2"]]),
        "vec": np.concatenate([parts[n] for n in VEC_COLS], axis=1),
        "x0": np.ascontiguousarray(np.concatenate([I["x"][0].T, I["ctx_2"][0].T], axis=1).reshape(KD, P, T2).transpose(1, 0, 2)),
        "pool_w": np.ascontiguousarray(I["ev_pool_w"][0].transpose(1, 0, 2)),
        "sgu_w": np.ascontiguousarray(I["ev_sgu_w"][0].transpose(2, 0, 1)),
        "sgu_b": np.ascontiguousarray(np.broadcast_to(I["ev_sgu_b"][0], (P, 4, P))),
        "tab_count": tab["count"], "tab_mask": tab["mask"], "tab_mask_c": tab["mask_c"], "tab_decay": tab["decay"],
        "tab_da": axial(64, 2), "tab_ga": axial(128, 1),
        "pos": np.ascontiguousarray(np.broadcast_to(I["positions"].astype(np.int32), (P, T))),
        "cmp_w2": np.ascontiguousarray(np.stack([I["od_cmp_k_w2"][0], I["od_cmp_v_w2"][0]], axis=1)),
        "cmp_pos": np.ascontiguousarray(np.tile(np.stack([I["od_cmp_k_pos"][0].T, I["od_cmp_v_pos"][0].T], axis=1), (2, 1, 1))),
        "da_lambda": np.ascontiguousarray(np.broadcast_to(I["da_lambda_2"][0], (P, 4, 64))),
    }
    for kv in "kv":
        arrays[f"cmp_{kv}_w1"] = np.ascontiguousarray(np.tile(I[f"od_cmp_{kv}_w1"][0].reshape(32, 64, P).transpose(1, 0, 2), (2, 1, 1)))

    nc = bacc.Bacc("TRN2", target_bir_lowering=False, num_devices=1, dynamic_dma_scratch_size=1024)
    A = {}
    for name, a in arrays.items():
        A[name] = nc.dram_tensor(name, a.shape, mybir.dt.from_np(a.dtype), kind="ExternalInput").ap()
    out = nc.dram_tensor("out", (P, KD, T), mybir.dt.float32, kind="ExternalOutput").ap()
    build(nc, A, out)
    r = run_bass_kernel_spmd(nc, [arrays], core_ids=[0])
    return r.results[0]["out"].transpose(2, 1, 0).reshape(1, T, D)
```

```python
from collections import namedtuple
from contextlib import ExitStack

import numpy as np
import concourse.bass as bass
from concourse import mybir

P = 128
D = 1024
KD = D // P
T = 256
T2 = 2 * T
F = 2816
KF = F // P
HALF = KF // 2
BLK = KD * 2 * P
DBLK = HALF * P
NADA = 9 * D // 256
NEG = -1.0e30
LAMBDA_INIT = 0.2

GU, DOWN = 2 * 11, 16


def SEG(blocks):
    return blocks, BLK, 2


FFN = [SEG(GU), (DOWN, DBLK, 1)]
SEGMENTS = ([SEG(6), SEG(4)] + FFN + [SEG(14), SEG(4)] + FFN + FFN + [SEG(12), SEG(4)] + FFN
            + FFN + [SEG(6), SEG(4)] + FFN)
FILL = {0: 2, 1: 8, 2: 2, 4: 2, 5: 20, 6: 2, 8: 0, 10: 2, 11: 32, 12: 2}
assert sum(FILL[k] for k in FILL if k <= 8) == NADA == sum(FILL[k] for k in FILL if k > 8)
SLOTS = 4

SIZES, DONE, ARRIVED, ORDER, ADA_SEG = [], [], [], [], []


def plan():
    loads, done, ada = [0] * SLOTS, 0, 0
    starts = []
    for seg, (blocks, size, tiles) in enumerate(SEGMENTS):
        starts.append(len(SIZES))
        for b in range(blocks):
            n = len(SIZES)
            done += tiles
            loads[n % SLOTS] += 1
            SIZES.append(size)
            DONE.append(done)
            ARRIVED.append(loads[n % SLOTS])
            ORDER.append(("w", seg, n))
            if b == 1:
                for j in range(FILL.get(seg, 0)):
                    slot = (n + 1 + j % 2) % SLOTS
                    loads[slot] += 1
                    ORDER.append(("ada", ada, slot, loads[slot]))
                    ADA_SEG.append(seg)
                    ada += 1
    return starts


STARTS = plan()
NBLK = len(SIZES)
FILLS = {seg: [x[1] for x in ORDER if x[0] == "ada" and ADA_SEG[x[1]] == seg] for seg in range(len(SEGMENTS))}
ADA_AT = {x[1]: (x[2], x[3]) for x in ORDER if x[0] == "ada"}


def lin(table, n, i):
    return table[n] if isinstance(i, int) else i * (table[n + SLOTS] - table[n]) + table[n]


VEC_COLS = {}
_at = 0
for _name, _n in [("mix_pre", 16), ("mix_post", 16), ("ffn_pre", 16), ("ffn_post", 16), ("norm_g", 96),
                  ("pool_scale", 4), ("sgu_g", 4), ("sgu_b", 4), ("gn_g", 4), ("subln", 1), ("q_norm", 1),
                  ("k_norm", 1), ("ada_b", 144), ("c", 16), ("eps6", 1), ("eps5", 1), ("f_nsa", 1),
                  ("f_ret", 1), ("row_ok", 2), ("ident", 128), ("ones", 128), ("rot_nsa", 128),
                  ("rot_ret", 128), ("rot_ax", 128)]:
    VEC_COLS[_name] = (_at, _n)
    _at += _n
NVEC = _at
TAB_COLS = {}
_at = 0
for _name, _n in [("mask", 128), ("mask_c", 30), ("decay", 4 * 256), ("count", 64)]:
    TAB_COLS[_name] = (_at, _n)
    _at += _n
NTAB = _at

Mark = namedtuple("Mark", "sem n")


def build(nc, A, out):
    fp32, f32r, i32 = mybir.dt.float32, mybir.dt.float32r, mybir.dt.int32
    ACT, ALU, AX = mybir.ActivationFunctionType, mybir.AluOpType, mybir.AxisListType.X
    MUL, ADD, SUB = ALU.mult, ALU.add, ALU.subtract
    ds = bass.ds

    with ExitStack() as ctx:
        def sb(name, shape, dt=fp32):
            return ctx.enter_context(nc.sbuf_tensor(name, shape, dt))

        H = sb("H", [P, KD, T2])
        HN = [sb("HN_hi", [P, KD, T2], f32r), sb("HN_lo", [P, KD, T2], f32r)]
        Y = sb("Y", [P, KD, T2])
        WHI = [sb(f"whi{s}", [P, BLK], f32r) for s in range(2)]
        with ExitStack() as g:
            RAW = [g.enter_context(nc.sbuf_tensor(f"raw{s}", [P, BLK], fp32)) for s in range(SLOTS)]
        WLO = [sb(f"wlo{s}", [P, BLK], f32r) for s in range(SLOTS)]
        TMP = [sb(f"tmp{s}", [P, T2]) for s in range(2)]
        SQ = [sb(f"sq{s}", [P, T2]) for s in range(2)]
        ACC = sb("acc", [P, T2])
        DIAG = sb("diag", [P, T2])
        VEC = sb("VEC", [P, NVEC])
        MOD = sb("MOD", [P, 144, 2])
        GA = sb("GA", [P, 2, 6, KD, 2])
        SMALL = sb("SMALL", [P, 64])
        with ExitStack() as g:
            G = [g.enter_context(nc.sbuf_tensor("G_hi", [P, KF, T2], f32r)),
                 g.enter_context(nc.sbuf_tensor("G_lo", [P, KF, T2], f32r))]
        ARENA = sb("ARENA", [P, 2 * KF * T2])
        BANK = [ctx.enter_context(nc.psum_tensor(f"bank{n}", [P, 512], fp32)) for n in range(8)]
        sems = {}
        names = ["w_in0", "w_in1", "w_in2", "w_in3", "w_hi", "w_lo", "ada_used", "ada_out", "tile_done",
                 "evac", "gate_read", "up_done", "g_hi", "g_lo", "in_h", "in_vec", "in_tab", "sq",
                 "sq_sum", "total", "root", "rstd", "scaled", "hn_hi", "hn_lo", "resid", "act_c",
                 "pe_step", "act_step", "dve_step", "pool_step", "stored", "rows"]
        for n in names:
            sems[n] = ctx.enter_context(nc.semaphore(n))
        block = ctx.enter_context(nc.Block())

        def vec(name, a=0, n=None):
            at, size = VEC_COLS[name]
            return VEC[:, at + a:at + (size if n is None else a + n)]

        ident, ones = vec("ident"), vec("ones")

        def carve():
            at = [0]

            def piece(n, *dims, dt=None):
                size = n
                for d in dims:
                    size *= d
                ap = ARENA[:, at[0]:at[0] + size]
                at[0] += size
                assert at[0] <= 2 * KF * T2, at[0]
                if dt is not None:
                    ap = ap.bitcast(dt)
                if len(dims) == 1:
                    ap = ap.rearrange("p (a b) -> p a b", a=n)
                if len(dims) == 2:
                    ap = ap.rearrange("p (a b c) -> p a b c", a=n, b=dims[0])
                return ap
            return piece

        def program(pe=None, act=None, dve=None, pool=None, sp=None):
            count = dict.fromkeys(names, 0)
            NV, NS, NT, NG = nc.vector, nc.scalar, nc.tensor, nc.gpsimd

            def up(name, n=1):
                count[name] += n
                return Mark(sems[name], count[name])

            def now(name):
                return Mark(sems[name], count[name])

            held_acc = [None]
            split = [0]

            def run(eng, blocks, unit, body, head=0):
                n, end = split[0], split[0] + blocks
                for _ in range(head):
                    body(0, n)
                    n += unit
                steps = (end - n - 2) // SLOTS
                if steps >= 2:
                    with eng.Fori(0, steps) as i:
                        for j in range(0, SLOTS, unit):
                            body(i, n + j)
                    n += SLOTS * steps
                while n < end:
                    body(0, n)
                    n += unit

            def load_weights():
                holds = [None] * SLOTS

                def load(slot, src, size, n_sem, n_count, dst_i=None):
                    if n_sem is not None:
                        sp.wait_ge(sems[n_sem], n_count)
                    sp.dma_start(RAW[slot][:, 0:size], src).then_inc(sems[f"w_in{slot}"], 16)

                n8 = nd = 0
                for seg, (blocks, size, tiles) in enumerate(SEGMENTS):
                    base = STARTS[seg]
                    src, at = (A["w_main"], n8) if size == BLK else (A["w_down"], nd)
                    if size == BLK:
                        n8 += blocks
                    else:
                        nd += blocks

                    def one(b):
                        slot = (base + b) % SLOTS
                        load(slot, src[at + b], size, *(holds[slot] or (None, 0)))
                        holds[slot] = ("tile_done", DONE[base + b])
                    for b in range(2):
                        one(b)
                    for x in ORDER:
                        if x[0] == "ada" and x[1] in FILLS[seg]:
                            slot = x[2]
                            load(slot, A["w_ada"][x[1]], BLK, *(holds[slot] or (None, 0)))
                            holds[slot] = ("ada_used", x[1] + 1)
                    for b in range(2, 6 if blocks > 4 else 4):
                        one(b)
                    b, steps = 6, (blocks - 6) // SLOTS
                    if steps >= 2:
                        with sp.Fori(0, steps) as i:
                            for j in range(SLOTS):
                                slot = (base + b + j) % SLOTS
                                sp.wait_ge(sems["tile_done"], lin(DONE, base + b + j - SLOTS, i))
                                sp.dma_start(RAW[slot][:, 0:size],
                                             src[ds(i * SLOTS + (at + b + j), 1)].rearrange("a p n -> p (a n)"))\
                                    .then_inc(sems[f"w_in{slot}"], 16)
                        b += SLOTS * steps
                        for j in range(SLOTS):
                            holds[(base + b - SLOTS + j) % SLOTS] = ("tile_done", DONE[base + b - SLOTS + j])
                    while b < blocks:
                        one(b)
                        b += 1

            def split_hi(i, n):
                if n < NBLK:
                    slot, size = n % SLOTS, SIZES[n]
                    act.wait_ge(sems[f"w_in{slot}"], lin(ARRIVED, n, i) * 16)
                    NS.activation(WHI[n % 2][:, 0:size], RAW[slot][:, 0:size], ACT.Copy).then_inc(sems["w_hi"], 1)

            def split_lo(i, n):
                if n < NBLK:
                    slot, size = n % SLOTS, SIZES[n]
                    dve.wait_ge(sems["w_hi"], lin(range(1, NBLK + 1), n, i))
                    NV.tensor_tensor(WLO[slot][:, 0:size], RAW[slot][:, 0:size], WHI[n % 2][:, 0:size].bitcast(fp32), SUB)\
                        .then_inc(sems["w_lo"], 1)

            def product(out, n, col, wk, x, k, kx, N, w, xp, start, stop):
                return NT.matmul(out[:, 0:N], (WHI[n % 2], WLO[n % SLOTS])[w][:, k * wk + col:k * wk + col + P],
                                 x[xp][:, kx, 0:N], start=start, stop=stop)

            def three(bank, N, n, x, col, kt, wk, x0=0, start=True, stop=True):
                steps = [(a, b, k) for a, b in ((0, 0), (0, 1), (1, 0)) for k in range(kt)]
                for j, (a, b, k) in enumerate(steps):
                    mm = product(bank, n, col, wk, x, k, x0 + k, N, a, b, start and j == 0, stop and j == len(steps) - 1)
                return mm

            def first_pair(banks, N, n, ready):
                for m in range(2):
                    for k in range(KD):
                        if m == 0:
                            pe.wait_ge(*ready[0][k])
                        for w in range(2):
                            product(banks[m], n, m * P, 2 * P, HN, k, k, N, w, 0, k == 0 and w == 0, False)
                for m in range(2):
                    for k in range(KD):
                        if m == 0:
                            pe.wait_ge(*ready[1][k])
                        mm = product(banks[m], n, m * P, 2 * P, HN, k, k, N, 0, 1, False, k == KD - 1)
                    mm.then_inc(sems["tile_done"], 1)

            def clear_sum(N):
                z = up("dve_step")
                if on(dve, held_acc[0]):
                    NV.memset(ACC[:, 0:N], 0.0).then_inc(z.sem, 1)
                return z

            def add_square(i, s0, step, index, buf, N):
                dve.wait_ge(sems["sq"], i * step + (s0[0] + index + 1))
                if index or not isinstance(i, int):
                    dve.wait_ge(sems["sq_sum"], i * step + (s0[1] + index))
                NV.tensor_tensor(ACC[:, 0:N], ACC[:, 0:N], SQ[buf][:, 0:N], ADD).then_inc(sems["sq_sum"], 1)

            def put_out(i, s0, step, index, dst, bank, buf, N, squares):
                if squares:
                    if index >= 2 or not isinstance(i, int):
                        act.wait_ge(sems["sq_sum"], i * step + (s0[1] + index - 1))
                    NS.activation(SQ[buf][:, 0:N], bank[:, 0:N], ACT.Square).then_inc(sems["sq"], 1)
                NS.activation(dst, bank[:, 0:N], ACT.Copy).then_inc(sems["evac"], 1)

            def linear(blocks, N, dst, ready, squares=False, d0=0, after=None):
                n0, e0, s0 = split[0], count["evac"], (count["sq"], count["sq_sum"])
                zero = clear_sum(N) if squares else None

                def at(i, n, per=2):
                    return 2 * (n - n0)
                if on(pe, after):
                    def body(i, n):
                        pe.wait_ge(sems["w_lo"], lin(range(1, NBLK + 1), n, i))
                        banks = [BANK[2 * ((n - n0) % 2) + m] for m in range(2)]
                        if n - n0 >= 2:
                            pe.wait_ge(sems["evac"], i * 8 + (e0 + at(i, n) - 2))
                        if n == n0 and isinstance(i, int) and ready[0] is not None:
                            return first_pair(banks, N, n, ready)
                        for m in range(2):
                            three(banks[m], N, n, HN, m * P, KD, 2 * P).then_inc(sems["tile_done"], 1)
                    run(pe, blocks, 1, body, head=2)
                if act:
                    def body(i, n):
                        for m in range(2):
                            t = at(i, n) + m
                            act.wait_ge(sems["tile_done"], i * 8 + (DONE[n] - 1 + m))
                            put_out(i, s0, 8, t, dst[:, ds(i * 8 + (d0 + t), 1), 0:N], BANK[2 * ((n - n0) % 2) + m], m, N, squares)
                        split_hi(i, n + 2)
                    run(act, blocks, 1, body, head=2)
                if on(dve, zero):
                    def body(i, n):
                        if squares:
                            for m in range(2):
                                add_square(i, s0, 8, at(i, n) + m, m, N)
                        split_lo(i, n + 2)
                    run(dve, blocks, 1, body, head=2)
                split[0] += blocks
                if squares:
                    up("sq", 2 * blocks)
                    up("sq_sum", 2 * blocks)
                return up("evac", 2 * blocks)

            def ffn(N, ready, after=None):
                n0 = split[0]
                g0, u0, h0, l0 = (count[x] for x in ("gate_read", "up_done", "g_hi", "g_lo"))
                if pe:
                    def body(i, n):
                        for s in range(2):
                            pe.wait_ge(sems["w_lo"], lin(range(1, NBLK + 1), n + s, i))
                            if n > n0:
                                pe.wait_ge(sems["up_done" if s else "gate_read"], i * 4 + ((u0 if s else g0) + n - n0))
                            elif s:
                                if after is not None:
                                    pe.wait_ge(*after)
                            if n == n0 and s == 0:
                                first_pair(BANK[0:2], N, n, ready)
                                continue
                            for m in range(2):
                                three(BANK[2 * s + m], N, n + s, HN, m * P, KD, 2 * P).then_inc(sems["tile_done"], 1)
                    run(pe, GU, 2, body, head=1)
                if act:
                    def body(i, n):
                        for m in range(2):
                            act.wait_ge(sems["tile_done"], i * 8 + (DONE[n] - 1 + m))
                            act.wait_ge(sems["g_lo"], i * 4 + (l0 + n - n0))
                            NS.activation(TMP[m][:, 0:N], BANK[m][:, 0:N], ACT.Silu).then_inc(sems["gate_read"], 1)
                        split_hi(i, n + 2)
                        act.wait_ge(sems["tile_done"], lin(DONE, n + 1, i))
                        split_hi(i, n + 3)
                        for m in range(2):
                            act.wait_ge(sems["up_done"], i * 4 + (u0 + n - n0 + m + 1))
                            NS.activation(G[0][:, ds(i * 4 + (n - n0 + m), 1), 0:N], TMP[m][:, 0:N], ACT.Copy)\
                                .then_inc(sems["g_hi"], 1)
                    run(act, GU, 2, body, head=1)
                if dve:
                    def body(i, n):
                        split_lo(i, n + 2)
                        for m in range(2):
                            dve.wait_ge(sems["gate_read"], i * 4 + (g0 + n - n0 + m + 1))
                            dve.wait_ge(sems["tile_done"], i * 8 + (DONE[n + 1] - 1 + m))
                            NV.tensor_tensor(TMP[m][:, 0:N], TMP[m][:, 0:N], BANK[2 + m][:, 0:N], MUL)\
                                .then_inc(sems["up_done"], 1)
                        split_lo(i, n + 3)
                        for m in range(2):
                            dve.wait_ge(sems["g_hi"], i * 4 + (h0 + n - n0 + m + 1))
                            kt = ds(i * 4 + (n - n0 + m), 1)
                            NV.tensor_tensor(G[1][:, kt, 0:N], TMP[m][:, 0:N], G[0][:, kt, 0:N].bitcast(fp32), SUB)\
                                .then_inc(sems["g_lo"], 1)
                    run(dve, GU, 2, body, head=1)
                split[0] += GU
                for x in ("gate_read", "up_done", "g_hi"):
                    up(x, KF)
                hidden = up("g_lo", KF)

                n1, e1, s0 = split[0], count["evac"], (count["sq"], count["sq_sum"])
                zero = clear_sum(N)
                if pe:
                    pe.wait_ge(*now("gate_read"))
                    pe.wait_ge(hidden.sem, hidden.n - 2)

                    def body(i, n):
                        m = (n - n1) // 2
                        if m >= 2 or not isinstance(i, int):
                            pe.wait_ge(sems["evac"], i * 2 + (e1 + m - 1))
                        for s in range(2):
                            pe.wait_ge(sems["w_lo"], lin(range(1, NBLK + 1), n + s, i))
                            if m == 0 and s == 1:
                                pe.wait_ge(*hidden)
                            three(BANK[m % 2], N, n + s, G, 0, HALF, P, s * HALF, s == 0, s == 1).then_inc(sems["tile_done"], 1)
                    run(pe, DOWN, 2, body, head=1)
                if act:
                    NS.activation(SMALL[:, 47:48], vec("eps6"), ACT.Sqrt)

                    def body(i, n):
                        m = (n - n1) // 2
                        act.wait_ge(sems["tile_done"], lin(DONE, n, i))
                        split_hi(i, n + 2)
                        act.wait_ge(sems["tile_done"], lin(DONE, n + 1, i))
                        put_out(i, s0, 2, m, Y[:, ds(i * 2 + m, 1), 0:N], BANK[m % 2], m % 2, N, True)
                        split_hi(i, n + 3)
                    run(act, DOWN, 2, body, head=1)
                if on(dve, zero):
                    def body(i, n):
                        split_lo(i, n + 2)
                        add_square(i, s0, 2, (n - n1) // 2, (n - n1) // 2 % 2, N)
                        split_lo(i, n + 3)
                    run(dve, DOWN, 2, body, head=1)
                split[0] += DOWN
                up("sq", KD)
                up("sq_sum", KD)
                return up("evac", KD)

            def on(eng, *marks):
                if eng is None:
                    return False
                for m in marks:
                    if m is not None:
                        eng.wait_ge(*m)
                return True

            def bcast(ap, *shape):
                return ap.to_broadcast([P, *shape])

            filling = {}

            def fill_begin(seg, bank, *free):
                filling.update(blocks=FILLS[seg], at=0, bank=BANK[bank], free=free)

            def fill(products):
                for _ in range(products):
                    block, tile, k = filling["at"] // 16, filling["at"] // 8, filling["at"] % 8
                    if block >= len(filling["blocks"]):
                        return
                    if pe:
                        slot, loads = ADA_AT[filling["blocks"][block]]
                        if filling["at"] == 0:
                            for m in (*filling["free"], silu_c):
                                if m is not None:
                                    pe.wait_ge(*m)
                        if filling["at"] % 16 == 0:
                            pe.wait_ge(sems[f"w_in{slot}"], 16 * loads)
                        col = k * 2 * P + (tile % 2) * P
                        mm = NT.matmul(filling["bank"][:, 2 * tile:2 * tile + 2], RAW[slot][:, col:col + P], C[:, k, :],
                                       start=k == 0, stop=k == KD - 1)
                        if filling["at"] % 16 == 15:
                            mm.then_inc(sems["ada_used"], 1)
                    filling["at"] += 1

            def fill_end():
                fill(16 * len(filling["blocks"]))
                n = len(filling["blocks"])
                if not n:
                    return None
                done = up("ada_used", n)
                tiles = slice(2 * filling["blocks"][0], 2 * filling["blocks"][0] + 2 * n)
                kept = up("ada_out")
                if on(dve, done):
                    NV.tensor_tensor(MOD[:, tiles, :], filling["bank"][:, 0:4 * n].rearrange("p (a s) -> p a s", s=2),
                                     vec("ada_b")[:, tiles].unsqueeze(2).to_broadcast([P, 2 * n, 2]), ADD).then_inc(kept.sem, 1)
                return kept

            def inverse_root(N, total, sums, out_bank, at, fills):
                c = N // P
                root = up("root")
                if on(act, total):
                    NS.activation(SMALL[:, at:at + c], sums[:, 0:c], ACT.Sqrt, bias=vec("eps6"), scale=1.0 / D).then_inc(root.sem, 1)
                inv = up("rstd")
                if on(dve, root):
                    NV.reciprocal(SMALL[:, at:at + c], SMALL[:, at:at + c]).then_inc(inv.sem, 1)
                diag = up("dve_step")
                if on(dve, inv):
                    for j in range(c):
                        op = NV.tensor_scalar(DIAG[:, j * P:(j + 1) * P], ident, SMALL[:, at + j:at + j + 1], None, MUL)
                    op.then_inc(diag.sem, 1)
                fill(fills)
                spread = up("pe_step")
                if on(pe, diag):
                    NT.matmul(out_bank[:, 0:N], ones, DIAG[:, 0:N], start=True, stop=True).then_inc(spread.sem, 1)
                return spread

            def norms(N, post, n_pre, pre, ready, seg):
                fill_begin(seg, 3, *ready) if seg is not None else filling.update(blocks=[], at=0)
                resid = None
                if post:
                    total = up("total")
                    if on(pe, now("sq_sum"), *ready):
                        for c in range(N // P):
                            mm = NT.matmul(BANK[6][:, c:c + 1], ACC[:, c * P:(c + 1) * P], ones[:, 0:1], start=True, stop=True)
                        mm.then_inc(total.sem, 1)
                    held_acc[0] = total
                    rs = inverse_root(N, total, BANK[6], BANK[7], 32, 8)
                    fill(16)
                    c0, r0 = count["scaled"], count["resid"]
                    if on(dve, rs, *ready):
                        for k in range(KD + 1):
                            if k < KD:
                                if k >= 2:
                                    dve.wait_ge(sems["resid"], r0 + k - 1)
                                for c, n, gain, shift in post:
                                    op = NV.scalar_tensor_tensor(TMP[k % 2][:, c:c + n], Y[:, k, c:c + n], gain(k), BANK[7][:, c:c + n], MUL, MUL)
                                op.then_inc(sems["scaled"], 1)
                            if k:
                                dve.wait_ge(sems["scaled"], c0 + k)
                                NV.tensor_tensor(H[:, k - 1, 0:N], H[:, k - 1, 0:N], TMP[(k - 1) % 2][:, 0:N], ADD)\
                                    .then_inc(sems["resid"], 1)
                    up("scaled", KD)
                    resid = Mark(sems["resid"], r0)
                    up("resid", KD)
                if not pre:
                    return [now("resid")]
                squares, sums = count["sq"], count["total"]
                if on(act, *ready):
                    for k in range(KD):
                        if post:
                            act.wait_ge(resid.sem, resid.n + k + 1)
                        if k >= 2:
                            act.wait_ge(sems["total"], sums + k - 1)
                        NS.activation(SQ[k % 2][:, 0:n_pre], H[:, k, 0:n_pre], ACT.Square).then_inc(sems["sq"], 1)
                for k in range(KD):
                    if pe:
                        pe.wait_ge(sems["sq"], squares + k + 1)
                        for c in range(n_pre // P):
                            mm = NT.matmul(BANK[4][:, c:c + 1], SQ[k % 2][:, c * P:(c + 1) * P], ones[:, 0:1],
                                           start=k == 0 and c == 0, stop=k == KD - 1, skip_group_check=True)
                        mm.then_inc(sems["total"], 1)
                    fill(N // T)
                up("sq", KD)
                total = up("total", KD)
                rs = inverse_root(n_pre, total, BANK[4], BANK[5], 36, 8)
                c0, h0, l0 = count["scaled"], count["hn_hi"], count["hn_lo"]
                if on(dve, rs, *ready):
                    for k in range(KD):
                        for c, n, gain, shift in pre:
                            op = NV.scalar_tensor_tensor(Y[:, k, c:c + n], H[:, k, c:c + n], gain(k), BANK[5][:, c:c + n], MUL, MUL)
                        op.then_inc(sems["scaled"], 1)
                if act:
                    for k in range(KD):
                        act.wait_ge(sems["scaled"], c0 + k + 1)
                        for c, n, gain, shift in pre:
                            if shift is None:
                                op = NS.activation(HN[0][:, k, c:c + n], Y[:, k, c:c + n], ACT.Copy)
                            else:
                                op = NS.activation(HN[0][:, k, c:c + n], Y[:, k, c:c + n], ACT.Identity, bias=shift(k))
                        op.then_inc(sems["hn_hi"], 1)
                kept = fill_end()
                if dve:
                    for k in range(KD):
                        dve.wait_ge(sems["hn_hi"], h0 + k + 1)
                        for c, n, gain, shift in pre:
                            t, hi = Y[:, k, c:c + n], HN[0][:, k, c:c + n].bitcast(fp32)
                            if shift is None:
                                op = NV.tensor_tensor(HN[1][:, k, c:c + n], t, hi, SUB)
                            else:
                                op = NV.scalar_tensor_tensor(HN[1][:, k, c:c + n], t, shift(k), hi, ADD, SUB)
                        op.then_inc(sems["hn_lo"], 1)
                up("scaled", KD)
                up("hn_hi", KD)
                up("hn_lo", KD)
                return [[Mark(sems["hn_hi"], h0 + k + 1) for k in range(KD)],
                        [Mark(sems["hn_lo"], l0 + k + 1) for k in range(KD)], kept]

            def keep_split(src, k, cols, *ready):
                hi = up("hn_hi")
                if on(act, *ready):
                    NS.activation(HN[0][:, k, cols], src, ACT.Copy).then_inc(hi.sem, 1)
                lo = up("hn_lo")
                if on(dve, hi):
                    NV.tensor_tensor(HN[1][:, k, cols], src, HN[0][:, k, cols].bitcast(fp32), SUB).then_inc(lo.sem, 1)
                return lo

            def rope(tiles, rot, cos, sin, ready, banks=(4, 5), between=None):
                free = [ready, ready]
                for j, t in enumerate(tiles):
                    bank = BANK[banks[j % 2]]
                    turned = up("pe_step")
                    if on(pe, free[j % 2], ready):
                        NT.matmul(bank[:, 0:T], rot, t, start=True, stop=True).then_inc(turned.sem, 1)
                    if between:
                        between(j)
                    part = up("dve_step")
                    if on(dve, turned):
                        NV.tensor_tensor(TMP[j % 2][:, 0:T], bank[:, 0:T], sin, MUL).then_inc(part.sem, 1)
                    free[j % 2] = part
                    straight = up("dve_step")
                    if on(dve):
                        NV.tensor_tensor(t, t, cos, MUL).then_inc(straight.sem, 1)
                    done = up("dve_step")
                    if on(dve, straight):
                        NV.tensor_tensor(t, t, TMP[j % 2][:, 0:T], ADD).then_inc(done.sem, 1)
                return done

            def tile_norm(items, gain, factor, ready, eps=vec("eps6"), banks=(5, 6)):
                sums, chunks, last = BANK[4], 0, [None, None]
                for j, (src, N, k) in enumerate(items):
                    sq, total = up("act_step"), up("pe_step")
                    if on(act, last[j % 2], *ready):
                        NS.activation(SQ[j % 2][:, 0:N], src, ACT.Square).then_inc(sq.sem, 1)
                    if on(pe, sq):
                        for c in range(N // P):
                            mm = NT.matmul(sums[:, chunks + c:chunks + c + 1], SQ[j % 2][:, c * P:(c + 1) * P], ones[:, 0:1],
                                           start=True, stop=True)
                        mm.then_inc(total.sem, 1)
                    last[j % 2] = total
                    chunks += N // P
                root, inv, fac = up("act_step"), up("dve_step"), up("dve_step")
                if on(act, total):
                    NS.activation(TMP[0][:, 0:chunks], sums[:, 0:chunks], ACT.Sqrt, bias=eps, scale=1.0 / P).then_inc(root.sem, 1)
                if on(dve, root):
                    NV.reciprocal(TMP[0][:, 0:chunks], TMP[0][:, 0:chunks]).then_inc(inv.sem, 1)
                    dve.wait_ge(*inv)
                    NV.tensor_scalar(TMP[0][:, 0:chunks], TMP[0][:, 0:chunks], 1.0 if factor is None else factor, None, MUL).then_inc(fac.sem, 1)
                at, last, used, his, los = 0, [None, None], [None, None], [], []
                for j, (src, N, k) in enumerate(items):
                    b = j % 2
                    diag, spread, done = up("dve_step"), up("pe_step"), up("dve_step")
                    if on(dve, fac, used[b]):
                        for c in range(N // P):
                            op = NV.tensor_scalar(SQ[b][:, c * P:(c + 1) * P], ident, TMP[0][:, at + c:at + c + 1], None, MUL)
                        op.then_inc(diag.sem, 1)
                    if on(pe, diag, last[b]):
                        NT.matmul(BANK[banks[b]][:, 0:N], ones, SQ[b][:, 0:N], start=True, stop=True).then_inc(spread.sem, 1)
                    fill(4)
                    if on(dve, spread):
                        NV.scalar_tensor_tensor(src, src, gain(j), BANK[banks[b]][:, 0:N], MUL, MUL).then_inc(done.sem, 1)
                    last[b], used[b] = done, spread
                    at += N // P
                    if k is not None:
                        keep_split(src, k, slice(0, N), done)
                        his.append(now("hn_hi"))
                        los.append(now("hn_lo"))
                return [his, los, None] if his else done

            def by_token(src, dst, ready, free=None):
                last, marks = [free, free], []

                def step(g):
                    j, b = 4 * g, g % 2
                    if j >= len(src):
                        return
                    turned = up("pe_step")
                    n = min(4, len(src) - j)
                    if on(pe, last[b], ready):
                        for m in range(n):
                            mm = NT.transpose(BANK[4 + b][:, m * P:(m + 1) * P], src[j + m], ident)
                        mm.then_inc(turned.sem, 1)
                    kept = up("act_step")
                    if on(act, turned):
                        NS.activation(dst[:, j:j + n, :].rearrange("p a q -> p (a q)"), BANK[4 + b][:, 0:n * P], ACT.Copy).then_inc(kept.sem, 1)
                    last[b] = kept
                    marks.append(kept)
                return step, marks

            def all_by_token(src, dst, ready, free=None):
                step, marks = by_token(src, dst, ready, free)
                for g in range((len(src) + 3) // 4):
                    step(g)
                return marks[-1]

            in_h, in_vec = up("in_h", 16), up("in_vec", 16)
            if act:
                act.dma_start(VEC[:, :], A["vec"]).then_inc(in_vec.sem, 16)
                act.dma_start(H[:, :, :], A["x0"]).then_inc(in_h.sem, 16)
            if sp:
                load_weights()

            silu_c = up("act_c")
            C = SMALL[:, 48:64].rearrange("p (k s) -> p k s", s=2)
            if on(act, in_vec):
                NS.activation(SMALL[:, 48:64], vec("c"), ACT.Silu).then_inc(silu_c.sem, 1)

            for n in range(2):
                if act:
                    split_hi(0, n)
                if dve:
                    split_lo(0, n)

            def adaln_gains(L, mods):
                for j in range(3):
                    def mod(row):
                        return MOD[:, 72 * L + 8 * row:72 * L + 8 * row + 8, :]

                    def g(n):
                        return vec("norm_g", (6 * L + n) * KD, KD).unsqueeze(2).to_broadcast([P, KD, 2])
                    pre, post = up("dve_step"), up("dve_step")
                    if on(dve, mods):
                        NV.scalar_tensor_tensor(GA[:, L, j], mod(3 * j + 1), 1.0, g(2 * j), ADD, MUL).then_inc(pre.sem, 1)
                        NV.scalar_tensor_tensor(GA[:, L, 3 + j], mod(3 * j + 2), 1.0 if j == 1 else 0.5, g(2 * j + 1), MUL, MUL)\
                            .then_inc(post.sem, 1)
                return post

            def gain1(name, layer):
                return [(0, T, lambda k: vec(name, layer * KD + k, 1), None)]

            def pre(L, j, seqs=2):
                return [(T * s, T, lambda k, s=s: GA[:, L, j, k, s:s + 1], lambda k, s=s: MOD[:, 72 * L + 24 * j + k, s:s + 1])
                        for s in range(seqs)]

            def post(L, j, seqs=2):
                return [(T * s, T, lambda k, s=s: GA[:, L, 3 + j, k, s:s + 1], None) for s in range(seqs)]

            piece = carve()
            Z = piece(12, T)
            DIFF = piece(4, T)
            W1, W2 = piece(T), piece(T)
            POOLW, SGUW, SGUB = piece(4, P), piece(4, P), piece(4, P)
            COUNT = piece(4, 16)
            VT = piece(8, P)
            x = norms(T, None, T, gain1("mix_pre", 0), [in_h, in_vec], 0)
            in_tab = up("in_tab", 64)
            if act:
                act.dma_start(POOLW, A["pool_w"]).then_inc(in_tab.sem, 16)
                act.dma_start(SGUW, A["sgu_w"]).then_inc(in_tab.sem, 16)
                act.dma_start(SGUB, A["sgu_b"]).then_inc(in_tab.sem, 16)
                act.dma_start(COUNT, A["tab_count"].rearrange("p (a b) -> p a b", a=4)).then_inc(in_tab.sem, 16)
            z = linear(6, T, Z, x, after=x[2])
            fill_begin(1, 6, z)

            sguw = up("pool_step")
            if on(pool, in_tab):
                NG.affine_select(out=SGUW, in_=SGUW, compare_op=ALU.is_ge, fill=0.0, base=0,
                                 pattern=[[0, 4], [1, P]], channel_multiplier=-1).then_inc(sguw.sem, 1)
            act_uv = up("act_step")
            if on(act, z):
                NS.activation(Z[:, 4:12, :], Z[:, 4:12, :], ACT.Gelu_apprx_tanh).then_inc(act_uv.sem, 1)

            last = z
            for g in range(4):
                a = Z[:, g, :]
                src, w = a, 1
                for level in range(g + 1):
                    dst = (W1, W2)[level % 2]
                    s1, s2 = up("dve_step"), up("dve_step")
                    if on(dve, last):
                        NV.tensor_copy(dst[:, 0:w], src[:, 0:w]).then_inc(s1.sem, 1)
                        NV.tensor_tensor(dst[:, w:T], src[:, w:T], src[:, 0:T - w], ADD).then_inc(s2.sem, 1)
                    src, w, last = dst, 2 * w, s2
                d1, d2, d3 = up("dve_step"), up("dve_step"), up("dve_step")
                if on(dve, last):
                    NV.scalar_tensor_tensor(DIFF[:, g, w:T], src[:, w:T], 1.0 / w, a[:, w:T], MUL, SUB).then_inc(d1.sem, 1)
                    dve.wait_ge(*in_tab)
                    NV.tensor_tensor(DIFF[:, g, 0:w], src[:, 0:w], COUNT[:, g, 0:w], MUL).then_inc(d2.sem, 1)
                    dve.wait_ge(*d2)
                    NV.tensor_tensor(DIFF[:, g, 0:w], DIFF[:, g, 0:w], a[:, 0:w], SUB).then_inc(d3.sem, 1)
                last = d3
                fill(12)
                pooled = up("pe_step")
                if on(pe, d3, in_tab):
                    NT.matmul(BANK[g][:, 0:T], POOLW[:, g, :], DIFF[:, g, :], start=True, stop=True).then_inc(pooled.sem, 1)
                scaled = up("act_step")
                if on(act, pooled):
                    NS.activation(DIFF[:, g, :], BANK[g][:, 0:T], ACT.Copy, scale=vec("pool_scale", g, 1)).then_inc(scaled.sem, 1)
                mixed = keep_split(DIFF[:, g, :], g, slice(0, T), scaled)

            V = Z[:, 8:12, :]

            def feature_sum(src, b, m0):
                s1, s2, s3, tot = up("dve_step"), up("dve_step"), up("dve_step"), up("pe_step")
                if on(dve, m0):
                    NV.tensor_tensor(W1, src[:, 0, :], src[:, 1, :], ADD).then_inc(s1.sem, 1)
                    NV.tensor_tensor(W2, src[:, 2, :], src[:, 3, :], ADD).then_inc(s2.sem, 1)
                    dve.wait_ge(*s2)
                    NV.tensor_tensor(W1, W1, W2, ADD).then_inc(s3.sem, 1)
                if on(pe, s3):
                    NT.matmul(BANK[b][:, 0:T], ones, W1, start=True, stop=True).then_inc(tot.sem, 1)
                return tot

            fill(8)
            tot = feature_sum(V, 4, act_uv)
            fill(16)
            mu = up("act_step")
            if on(act, tot):
                NS.activation(DIAG[:, 0:T], BANK[4][:, 0:T], ACT.Copy, scale=1.0 / 512).then_inc(mu.sem, 1)
            cen = up("dve_step")
            if on(dve, mu):
                NV.tensor_tensor(V, V, DIAG[:, 0:T].unsqueeze(1).to_broadcast([P, 4, T]), SUB).then_inc(cen.sem, 1)
            vsq = up("act_step")
            if on(act, cen, mixed):
                NS.activation(DIFF, V, ACT.Square).then_inc(vsq.sem, 1)
            tot = feature_sum(DIFF, 5, vsq)
            fill(24)
            root = up("act_step")
            if on(act, tot):
                NS.activation(DIAG[:, 0:T], BANK[5][:, 0:T], ACT.Sqrt, bias=vec("eps5"), scale=1.0 / 512).then_inc(root.sem, 1)
            inv = up("dve_step")
            if on(dve, root):
                NV.reciprocal(DIAG[:, 0:T], DIAG[:, 0:T]).then_inc(inv.sem, 1)
            nrm = up("dve_step")
            if on(dve, inv):
                NV.tensor_tensor(V, V, DIAG[:, 0:T].unsqueeze(1).to_broadcast([P, 4, T]), MUL).then_inc(nrm.sem, 1)
            aff = up("dve_step")
            if on(dve, nrm):
                for g in range(4):
                    op = NV.tensor_scalar(Z[:, 8 + g, :], Z[:, 8 + g, :], vec("sgu_g", g, 1), vec("sgu_b", g, 1), MUL, ADD)
                op.then_inc(aff.sem, 1)
            vt = all_by_token([Z[:, 8 + g, c * P:(c + 1) * P] for g in range(4) for c in range(2)], VT, aff)
            for g in range(4):
                mm_done = up("pe_step")
                if on(pe, vt, sguw, mixed):
                    for c in range(2):
                        mm = NT.matmul(BANK[g][:, c * P:(c + 1) * P], VT[:, 2 * g + c, :], SGUW[:, g, :], start=True, stop=True)
                    mm.then_inc(mm_done.sem, 1)
                b1, b2 = up("dve_step"), up("dve_step")
                if on(dve, mm_done):
                    NV.tensor_tensor(DIFF[:, g, :].rearrange("p (c t) -> p c t", c=2), BANK[g][:, 0:T].rearrange("p (c t) -> p c t", c=2),
                                     SGUB[:, g, :].unsqueeze(1).to_broadcast([P, 2, P]), ADD).then_inc(b1.sem, 1)
                    dve.wait_ge(*b1)
                    NV.tensor_tensor(DIFF[:, g, :], DIFF[:, g, :], Z[:, 4 + g, :], MUL).then_inc(b2.sem, 1)
                mixed = keep_split(DIFF[:, g, :], 4 + g, slice(0, T), b2)
                fill(16)
            kept = fill_end()
            y = linear(4, T, Y, [None], squares=True, after=mixed)
            x = norms(T, gain1("mix_post", 0), T, gain1("ffn_pre", 0), [y], 2)
            y = ffn(T, x, x[2])
            x = norms(T, gain1("ffn_post", 0), T, gain1("mix_pre", 1), [y], 4)

            piece = carve()
            Z = piece(28, T)
            MASK, MASKC, DECAY, POSI = piece(2 * P), piece(2, 15), piece(4, T), piece(T, dt=i32)
            CW1 = [piece(32, P), piece(32, P)]
            CW2 = piece(2, 64)
            CPOS = piece(2, 32)
            COSN, SINN, COSR, SINR = (piece(T) for _ in range(4))
            BLKS = piece(32, 15)
            HID = piece(4, 15)
            KCT, VC = piece(15), piece(P)
            VTOK = piece(4, P)
            GT = piece(2, 24)
            PB = [piece(2, T) for _ in range(3)]
            PC = [piece(15) for _ in range(3)]
            PT = [piece(5, P) for _ in range(2)]
            in_tab = up("in_tab", 8 * 16)
            if on(act, y):
                for dst, name in [(MASK, "tab_mask"), (MASKC, "tab_mask_c"), (DECAY, "tab_decay"), (POSI, "pos"),
                                  (CW1[0], "cmp_k_w1"), (CW1[1], "cmp_v_w1"), (CW2, "cmp_w2"), (CPOS, "cmp_pos")]:
                    act.dma_start(dst, A[name]).then_inc(in_tab.sem, 16)

            posf = up("dve_step")
            if on(dve, in_tab):
                NV.tensor_copy(ACC[:, 0:T], POSI).then_inc(posf.sem, 1)
            tables = []
            for f, cos, sin in (("f_nsa", COSN, SINN), ("f_ret", COSR, SINR)):
                m = [up("dve_step") for _ in range(11)]
                if on(dve, posf):
                    ang, q = DIAG[:, 0:T], DIAG[:, T:T2]
                    C1 = 6.28125
                    C2 = float(np.float32(np.round((2 * np.pi - C1) * 2**20) / 2**20))
                    C3 = float(2 * np.pi - C1 - C2)
                    PI = 3.1415925
                    NV.tensor_scalar(ang, ACC[:, 0:T], vec(f), None, MUL).then_inc(m[0].sem, 1)
                    dve.wait_ge(*m[0])
                    NV.tensor_scalar(q, ang, 1.0 / (2 * np.pi), 12582912.0, MUL, ADD).then_inc(m[1].sem, 1)
                    dve.wait_ge(*m[1])
                    NV.tensor_scalar(q, q, -12582912.0, None, ADD).then_inc(m[2].sem, 1)
                    for j, c in enumerate((C1, C2, C3)):
                        dve.wait_ge(*m[2 + j])
                        NV.scalar_tensor_tensor(ang, q, -c, ang, MUL, ADD).then_inc(m[3 + j].sem, 1)
                    dve.wait_ge(*m[5])
                    NV.tensor_scalar(sin, ang, PI, -PI, ALU.min, ALU.max).then_inc(m[6].sem, 1)
                    NV.tensor_scalar(cos, ang, 0.5 * np.pi, None, ADD).then_inc(m[7].sem, 1)
                    dve.wait_ge(*m[7])
                    NV.tensor_scalar(q, cos, PI, -2 * np.pi, ALU.is_gt, MUL).then_inc(m[8].sem, 1)
                    dve.wait_ge(*m[8])
                    NV.tensor_tensor(cos, cos, q, ADD).then_inc(m[9].sem, 1)
                    dve.wait_ge(*m[9])
                    NV.tensor_scalar(cos, cos, PI, -PI, ALU.min, ALU.max).then_inc(m[10].sem, 1)
                posf = m[10]
                tables.append(m[10])

            trig = up("act_step", 4)
            if on(act, tables[1]):
                for t in (COSN, SINN, COSR, SINR):
                    NS.activation(t, t, ACT.Sin).then_inc(trig.sem, 1)
            z = linear(14, T, Z, x, after=x[2])
            fill_begin(5, 7, z)

            turned = up("pe_step")
            if on(pe, z):
                for c in range(2):
                    mm = NT.transpose(BANK[6][:, c * P:(c + 1) * P], Z[:, 26, c * P:(c + 1) * P], ident)
                mm.then_inc(turned.sem, 1)
            th = up("act_step")
            if on(act, turned):
                NS.activation(GT, BANK[6][:, 0:T].rearrange("p (c g) -> p c g", c=2)[:, :, 0:24], ACT.Tanh, scale=0.5).then_inc(th.sem, 1)
            sg, ok = up("dve_step"), up("dve_step")
            if on(dve, th):
                NV.tensor_scalar(GT, GT, 0.5, 0.5, MUL, ADD).then_inc(sg.sem, 1)
                dve.wait_ge(*sg)
                for c in range(2):
                    op = NV.tensor_scalar(GT[:, c, 0:24:3], GT[:, c, 0:24:3], vec("row_ok", c, 1), None, MUL)
                op.then_inc(ok.sem, 1)
            gates = ok
            vtok_step, vtok = by_token([Z[:, t, c * P:(c + 1) * P] for t in (7, 9) for c in range(2)], VTOK, z)
            vtok_step(0)
            if dve:
                dve.wait_ge(*trig)
            roped = rope([Z[:, t, :] for t in (4, 6, 8, 0, 1, 2, 3)], vec("rot_nsa"), COSN, SINN, z, (0, 1), lambda j: fill(4))

            last = roped
            for kv in range(2):
                blk = up("dve_step")
                src = Z[:, 4 + kv, :]
                win = bass.AP(tensor=src.tensor, offset=src.offset, ap=[list(src.ap[0]), [1, 32], [16, 15]])
                if on(dve, last):
                    NV.tensor_tensor(BLKS, win, CPOS[:, kv, :].unsqueeze(2).to_broadcast([P, 32, 15]), ADD).then_inc(blk.sem, 1)
                hid = up("pe_step")
                if on(pe, blk, gates, roped):
                    for g in range(2):
                        for l in range(32):
                            mm = NT.matmul(BANK[2 * kv + g][:, 0:15], CW1[kv][64 * g:64 * g + 64, l, :],
                                           BLKS[64 * g:64 * g + 64, l, :], start=l == 0, stop=l == 31)
                    mm.then_inc(hid.sem, 1)
                fill(8)
                ge = up("act_step")
                if on(act, hid):
                    for g in range(2):
                        op = NS.activation(HID[:, 2 * kv + g, :], BANK[2 * kv + g][:, 0:15], ACT.Gelu_apprx_tanh)
                    op.then_inc(ge.sem, 1)
                last = hid
            cmp_mm = up("pe_step")
            if on(pe, ge):
                for g in range(2):
                    NT.matmul(BANK[6][64 * g:64 * g + 64, 0:15], CW2[:, 0, :], HID[:, g, :], start=True, stop=True)
                for g in range(2):
                    mm = NT.matmul(BANK[0][0:15, 64 * g:64 * g + 64], HID[:, 2 + g, :], CW2[:, 1, :], start=True, stop=True)
                mm.then_inc(cmp_mm.sem, 1)
            cmp_kv = up("act_step")
            if on(act, cmp_mm):
                NS.activation(KCT, BANK[6][:, 0:15], ACT.Copy)
                NS.activation(VC[0:15, :], BANK[0][0:15, 0:P], ACT.Copy).then_inc(cmp_kv.sem, 1)
            units = [(j, qt, hf) for j in range(4) for qt in range(2) for hf in range(2)]
            S_NEG, S_MAX, S_SUM, S_CO = 0, 9, 18, 27

            def small(at, u, n=3):
                return SMALL[:, at + 3 * (u % 3):at + 3 * (u % 3) + n]
            probs, read_s, mult, trans, copied, pv, o_kept = {}, {}, {}, {}, {}, {}, {}

            def parts(u):
                j, qt, hf = units[u]
                return j, qt, hf, (qt + 1) * P, slice(64 * hf, 64 * hf + 64)
            for it in range(len(units) + 3):
                u, x1, w, v = it, it - 1, it - 2, it - 3
                if u < len(units):
                    j, qt, hf, n, h64 = parts(u)
                    sc = up("pe_step")
                    if on(pe, roped, vtok[0], cmp_kv, read_s.get(u - 1)):
                        q = Z[h64, j, qt * P:(qt + 1) * P]
                        NT.matmul(BANK[2][:, 0:15], q, KCT[h64, :], start=True, stop=True)
                        NT.matmul(BANK[u % 2][:, 0:n], q, Z[h64, 6, 0:n], start=True, stop=True)
                        NT.matmul(BANK[u % 2][:, T:T + n], q, Z[h64, 8, 0:n], start=True, stop=True).then_inc(sc.sem, 1)
                fill(6)
                if 0 <= w < len(units):
                    j, qt, hf, n, h64 = parts(w)
                    b, head = w % 3, j + 4 * hf
                    m1, m2, m3 = up("dve_step"), up("dve_step"), up("dve_step")
                    if on(dve, probs[w], gates):
                        NV.reciprocal(small(S_CO, w), small(S_SUM, w)).then_inc(m1.sem, 1)
                        dve.wait_ge(*m1)
                        NV.tensor_tensor(small(S_CO, w), small(S_CO, w), GT[:, qt, 3 * head:3 * head + 3], MUL).then_inc(m2.sem, 1)
                        dve.wait_ge(*m2)
                        NV.tensor_scalar(PC[b], PC[b], small(S_CO, w)[:, 0:1], None, MUL)
                        for a in range(2):
                            op = NV.tensor_scalar(PB[b][:, a, 0:n], PB[b][:, a, 0:n], small(S_CO, w)[:, 1 + a:2 + a], None, MUL)
                        op.then_inc(m3.sem, 1)
                    mult[w] = m3
                if u < len(units):
                    j, qt, hf, n, h64 = parts(u)
                    b = u % 3
                    m1, m2, m3, m4, m5 = (up("dve_step") for _ in range(5))
                    if on(dve, sc, trans.get(u - 3)):
                        NV.scalar_tensor_tensor(PC[b], BANK[2][:, 0:15], 0.125, MASKC[:, qt, :], MUL, ADD).then_inc(m1.sem, 1)
                        NV.scalar_tensor_tensor(PB[b][:, :, 0:n], BANK[u % 2][:, :].rearrange("p (a n) -> p a n", a=2)[:, :, 0:n], 0.125,
                                                MASK[:, 2 * P - n:2 * P].unsqueeze(1).to_broadcast([P, 2, n]), MUL, ADD).then_inc(m2.sem, 1)
                        dve.wait_ge(*m2)
                        NV.tensor_reduce(small(S_MAX, u, 1), PC[b], AX, ALU.max).then_inc(m3.sem, 1)
                        NV.tensor_reduce(small(S_MAX, u)[:, 1:3], PB[b][:, :, 0:n], AX, ALU.max).then_inc(m4.sem, 1)
                        dve.wait_ge(*m4)
                        NV.tensor_scalar(small(S_NEG, u), small(S_MAX, u), -1.0, None, MUL).then_inc(m5.sem, 1)
                    read_s[u], probs[u] = m2, m5
                if 0 <= x1 < len(units):
                    j, qt, hf, n, h64 = parts(x1)
                    b = x1 % 3
                    ex = up("act_step", 3)
                    if on(act, probs[x1]):
                        NS.activation(PC[b], PC[b], ACT.Exp, bias=small(S_NEG, x1)[:, 0:1], accum_out=small(S_SUM, x1)[:, 0:1]).then_inc(ex.sem, 1)
                        for a in range(2):
                            NS.activation(PB[b][:, a, 0:n], PB[b][:, a, 0:n], ACT.Exp, bias=small(S_NEG, x1)[:, 1 + a:2 + a],
                                          accum_out=small(S_SUM, x1)[:, 1 + a:2 + a]).then_inc(ex.sem, 1)
                    probs[x1] = ex
                if 0 <= w < len(units):
                    j, qt, hf, n, h64 = parts(w)
                    b, p3 = w % 2, w % 3
                    tr, cp = up("pe_step"), up("act_step")
                    if on(pe, mult[w], copied.get(w - 1)):
                        NT.transpose(BANK[3][0:15, 0:P], PC[p3], ident)
                        for a in range(2):
                            for c in range(qt + 1):
                                mm = NT.transpose(BANK[4 + b][:, (2 * a + c) * P:(2 * a + c + 1) * P], PB[p3][:, a, c * P:(c + 1) * P], ident)
                        mm.then_inc(tr.sem, 1)
                    if on(act, tr, pv.get(w - 2)):
                        NS.activation(PT[b][0:15, 4, :], BANK[3][0:15, 0:P], ACT.Copy)
                        view = BANK[4 + b][:, :].rearrange("p (a c q) -> p a c q", a=2, c=2)[:, :, 0:qt + 1, :]
                        NS.activation(PT[b][:, 0:4, :].rearrange("p (a c) q -> p a c q", a=2)[:, :, 0:qt + 1, :], view, ACT.Copy)\
                            .then_inc(cp.sem, 1)
                    trans[w], copied[w] = tr, cp
                fill(6)
                if v >= 0:
                    j, qt, hf, n, h64 = parts(v)
                    b = v % 2
                    o = up("pe_step")
                    if on(pe, copied[v], o_kept.get(v // 2 - 1)):
                        dst = BANK[6][h64, 0:P]
                        NT.matmul(dst, VC[0:15, 64 * hf:64 * hf + 64], PT[b][0:15, 4, :], start=True, stop=False)
                        for a in range(2):
                            for c in range(qt + 1):
                                mm = NT.matmul(dst, VTOK[:, 2 * a + c, 64 * hf:64 * hf + 64], PT[b][:, 2 * a + c, :],
                                               start=False, stop=a == 1 and c == qt)
                        mm.then_inc(o.sem, 1)
                    pv[v] = o
                    if hf == 1:
                        o_kept[v // 2] = keep_split(BANK[6][:, 0:P], j, slice(qt * P, (qt + 1) * P), o)
            attended = o_kept[7]

            RV = CW1[0][:, 0:8, :]
            RSC = [CW1[1][:, 3 * b:3 * b + 3, :].rearrange("p a q -> p (a q)") for b in range(2)]
            RO = CW1[1][:, 8:16, :].rearrange("p a q -> p (a q)").rearrange("p (h t) -> p h t", h=4)
            roped = rope([Z[:, t, :] for t in range(10, 18)], vec("rot_ret"), COSR, SINR, attended, (0, 1), lambda j: fill(4))
            rv = all_by_token([Z[:, 18 + h, c * P:(c + 1) * P] for h in range(4) for c in range(2)], RV, attended, attended)
            got, used_s = {}, {}
            for h in range(4):
                b = h % 2
                sc = up("pe_step")
                if on(pe, rv, roped, used_s.get(h - 2)):
                    NT.matmul(BANK[b][:, 0:T], Z[:, 14 + h, 0:P], Z[:, 10 + h, :], start=True, stop=True)
                    NT.matmul(BANK[b][:, T:T + P], Z[:, 14 + h, P:T], Z[:, 10 + h, P:T], start=True, stop=True).then_inc(sc.sem, 1)
                de = up("dve_step")
                if on(dve, sc, got.get(h - 2)):
                    NV.tensor_tensor(RSC[b][:, 0:T], BANK[b][:, 0:T], DECAY[:, h, :], MUL)
                    NV.tensor_tensor(RSC[b][:, T:T + P], BANK[b][:, T:T + P], DECAY[:, h, 0:P], MUL).then_inc(de.sem, 1)
                used_s[h] = de
                ro = up("pe_step")
                if on(pe, de):
                    NT.matmul(BANK[2 + b][:, 0:T], RV[:, 2 * h, :], RSC[b][:, 0:T], start=True, stop=False)
                    NT.matmul(BANK[2 + b][:, P:T], RV[:, 2 * h + 1, :], RSC[b][:, T:T + P], start=False, stop=True).then_inc(ro.sem, 1)
                got[h] = ro
                cp = up("act_step")
                if on(act, ro):
                    NS.activation(RO[:, h, :], BANK[2 + b][:, 0:T], ACT.Copy).then_inc(cp.sem, 1)
                used_s[h] = cp
            sg = up("act_step")
            if on(act):
                NS.activation(Z[:, 22:26, :], Z[:, 22:26, :], ACT.Silu).then_inc(sg.sem, 1)
            for hh in range(2):
                o2 = RO[:, 2 * hh:2 * hh + 2, :].rearrange("p h t -> p (h t)")
                tot = up("pe_step")
                if on(pe, cp):
                    NT.matmul(BANK[4 + hh][:, :], ones, o2, start=True, stop=True).then_inc(tot.sem, 1)
                cen = up("dve_step")
                if on(dve, tot):
                    NV.scalar_tensor_tensor(o2, BANK[4 + hh][:, :], -1.0 / P, o2, MUL, ADD).then_inc(cen.sem, 1)
            nrm = tile_norm([(RO[:, h, :], T, None) for h in range(4)], lambda h: vec("gn_g", h, 1), None, [cen], vec("eps5"), (5, 6))
            for h in range(4):
                gated = up("dve_step")
                if on(dve, nrm, sg):
                    NV.tensor_tensor(RO[:, h, :], RO[:, h, :], Z[:, 22 + h, :], MUL).then_inc(gated.sem, 1)
                mixed = keep_split(RO[:, h, :], 4 + h, slice(0, T), gated)
            kept = fill_end()
            y = linear(4, T, Y, [None], squares=True, after=mixed)
            x = norms(T, gain1("mix_post", 1), T, gain1("ffn_pre", 1), [y], 6)
            gains = adaln_gains(0, x[2])
            y = ffn(T, x, x[2])
            x = norms(T, gain1("ffn_post", 1), T2, pre(0, 0), [y, gains], 8)

            def attend(unit_list, scale, V, PB, PT, neg_lam, ready, fills=0):
                exps, mult, trans, copied, pv, kept = {}, {}, {}, {}, {}, {}
                last = len(unit_list)

                def small(at, u, n=2):
                    return SMALL[:, at + 2 * (u % 3):at + 2 * (u % 3) + n]
                NEGM, MAXM, SUM, CO = 0, 6, 24, 30
                for it in range(last + 3):
                    u, x1, w, r = it, it - 1, it - 2, it - 3
                    if u < last:
                        q, k, v, q0, k0, parts, dest = unit_list[u]
                        nk, sc = T2 - k0, up("pe_step", len(parts))
                        if on(pe, exps.get(u - 2), *ready):
                            for a, pr in enumerate(parts):
                                NT.matmul(BANK[2 * (u % 2) + a][:, 0:nk], q[pr, q0:q0 + P], k[pr, k0:T2], start=True, stop=True)\
                                    .then_inc(sc.sem, 1)
                    fill(fills)
                    if 0 <= w < last:
                        q, k, v, q0, k0, parts, dest = unit_list[w]
                        b, nk, np_ = w % 3, T2 - k0, len(parts)
                        m1, m2, m3 = (up("dve_step") for _ in range(3))
                        m4 = up("dve_step") if np_ == 2 else m3
                        if on(dve, exps[w]):
                            NV.reciprocal(small(CO, w, np_), small(SUM, w, np_)).then_inc(m1.sem, 1)
                            dve.wait_ge(*m1)
                            if np_ == 2:
                                NV.tensor_tensor(small(CO, w)[:, 1:2], small(CO, w)[:, 1:2], neg_lam, MUL).then_inc(m2.sem, 1)
                                NV.tensor_scalar(PB[b][:, 0, 0:nk], PB[b][:, 0, 0:nk], small(CO, w)[:, 0:1], None, MUL).then_inc(m3.sem, 1)
                                dve.wait_ge(*m3)
                                NV.scalar_tensor_tensor(PB[b][:, 0, 0:nk], PB[b][:, 1, 0:nk], small(CO, w)[:, 1:2], PB[b][:, 0, 0:nk], MUL, ADD)\
                                    .then_inc(m4.sem, 1)
                            else:
                                NV.tensor_scalar(PB[b][:, 0, 0:nk], PB[b][:, 0, 0:nk], small(CO, w)[:, 0:1], None, MUL).then_inc(m4.sem, 2)
                        mult[w] = m4
                    if u < last:
                        q, k, v, q0, k0, parts, dest = unit_list[u]
                        nk, np_ = T2 - k0, len(parts)
                        mx, ng = up("dve_step"), up("dve_step")
                        if on(dve, sc):
                            for a in range(np_):
                                op = NV.tensor_reduce(small(MAXM, u)[:, a:a + 1], BANK[2 * (u % 2) + a][:, 0:nk], AX, ALU.max)
                            op.then_inc(mx.sem, 1)
                            dve.wait_ge(*mx)
                            NV.tensor_scalar(small(NEGM, u, np_), small(MAXM, u, np_), -scale, None, MUL).then_inc(ng.sem, 1)
                        exps[u] = ng
                    if 0 <= x1 < last:
                        q, k, v, q0, k0, parts, dest = unit_list[x1]
                        b, nk = x1 % 3, T2 - k0
                        ex = up("act_step", len(parts))
                        if on(act, exps[x1], trans.get(x1 - 3)):
                            for a in range(len(parts)):
                                NS.activation(PB[b][:, a, 0:nk], BANK[2 * (x1 % 2) + a][:, 0:nk], ACT.Exp, bias=small(NEGM, x1)[:, a:a + 1],
                                              scale=scale, accum_out=small(SUM, x1)[:, a:a + 1]).then_inc(ex.sem, 1)
                        exps[x1] = ex
                    if 0 <= w < last:
                        q, k, v, q0, k0, parts, dest = unit_list[w]
                        b, nk = w % 2, T2 - k0
                        tr, cp = up("pe_step"), up("act_step")
                        if on(pe, mult[w], copied.get(w - 2)):
                            for c in range(nk // P):
                                mm = NT.transpose(BANK[4 + b][:, c * P:(c + 1) * P], PB[w % 3][:, 0, c * P:(c + 1) * P], ident)
                            mm.then_inc(tr.sem, 1)
                        if on(act, tr, pv.get(w - 2)):
                            NS.activation(PT[b][:, 0:nk], BANK[4 + b][:, 0:nk], ACT.Copy).then_inc(cp.sem, 1)
                        trans[w], copied[w] = tr, cp
                    fill(fills)
                    if r >= 0:
                        q, k, v, q0, k0, parts, dest = unit_list[r]
                        b, nk = r % 2, T2 - k0
                        o, ke = up("pe_step"), up("act_step")
                        if on(pe, copied[r], kept.get(r - 1)):
                            for c in range(nk // P):
                                mm = NT.matmul(BANK[6][:, 0:P], V(k0 // P + c, v), PT[b][:, c * P:(c + 1) * P],
                                               start=c == 0, stop=c == nk // P - 1)
                            mm.then_inc(o.sem, 1)
                        if on(act, o):
                            NS.activation(Y[:, dest, q0:q0 + P], BANK[6][:, 0:P], ACT.Copy).then_inc(ke.sem, 1)
                        pv[r], kept[r] = o, ke
                return ke

            y = ffn(T2, x, x[2])
            piece = carve()
            Z = piece(24, T2)
            VTK = piece(32, P)
            PB = [piece(2, T2) for _ in range(3)]
            PT = [piece(T2) for _ in range(2)]
            CS = piece(2, T)
            LAM = piece(4, 64)
            in_tab = up("in_tab", 32)
            if on(act, y):
                act.dma_start(CS, A["tab_da"]).then_inc(in_tab.sem, 16)
                act.dma_start(LAM, A["da_lambda"]).then_inc(in_tab.sem, 16)
            x = norms(T2, post(0, 0), T2, pre(0, 1), [y], 10)
            z = linear(12, T2, Z, x, after=x[2])
            fill_begin(11, 7, z)
            l1, l2, l3 = up("dve_step"), up("dve_step"), up("dve_step")
            LP = SMALL[:, 16:24]
            if on(dve, in_tab, z):
                NV.tensor_tensor(LAM[:, 0, :], LAM[:, 0, :], LAM[:, 1, :], MUL).then_inc(l1.sem, 1)
                NV.tensor_tensor(LAM[:, 2, :], LAM[:, 2, :], LAM[:, 3, :], MUL).then_inc(l2.sem, 1)
                dve.wait_ge(*l2)
                NV.tensor_reduce(LP[:, 0:1], LAM[:, 0, :], AX, ADD)
                NV.tensor_reduce(LP[:, 1:2], LAM[:, 2, :], AX, ADD).then_inc(l3.sem, 1)
            le = up("act_step")
            if on(act, l3):
                NS.activation(LP[:, 2:4], LP[:, 0:2], ACT.Exp).then_inc(le.sem, 1)
            l4, l5 = up("dve_step"), up("dve_step")
            if on(dve, le):
                NV.tensor_tensor(LP[:, 4:5], LP[:, 3:4], LP[:, 2:3], SUB).then_inc(l4.sem, 1)
                dve.wait_ge(*l4)
                NV.tensor_scalar(LP[:, 5:6], LP[:, 4:5], -LAMBDA_INIT, None, ADD).then_inc(l5.sem, 1)
            step, vt = by_token([Z[:, 16 + h, c * P:(c + 1) * P] for c in range(4) for h in range(8)], VTK, z)

            def between(j):
                if j % 2 == 0:
                    step(j // 2)
                fill(3)
            roped = rope([Z[:, t, 0:T] for t in range(16)], vec("rot_ax"), CS[:, 0, :], CS[:, 1, :], z, (0, 1), between)
            both = (slice(0, 64), slice(64, P))
            units = [(Z[:, h, :], Z[:, 8 + h, :], h, qt * P, 0 if qt < 2 else T, both, h) for h in range(8) for qt in range(4)]
            o = attend(units, 0.125, lambda c, h: VTK[:, 8 * c + h, :], PB, PT, LP[:, 5:6], [roped, vt[-1], l5], 7)
            x = tile_norm([(Y[:, h, :], T2, h) for h in range(8)], lambda h: vec("subln"), 1.0 - LAMBDA_INIT, [o])
            kept = fill_end()
            y = linear(4, T2, Y, x, squares=True)
            x = norms(T2, post(0, 1), T2, pre(0, 2), [y], 12)
            gains = adaln_gains(1, x[2])
            y = ffn(T2, x, x[2])
            x = norms(T2, post(0, 2), T2, pre(1, 0), [y, gains], 14)

            y = ffn(T2, x)
            piece = carve()
            Z = piece(12, T2)
            VTK = piece(8, P)
            PB = [piece(2, T2) for _ in range(3)]
            PT = [piece(T2) for _ in range(2)]
            CS = piece(2, T)
            in_tab = up("in_tab", 16)
            if on(act, y):
                act.dma_start(CS, A["tab_ga"]).then_inc(in_tab.sem, 16)
            x = norms(T2, post(1, 0), T2, pre(1, 1), [y], 16)
            z = linear(4, T, Z, x)
            z = linear(2, T2, Z, [None], d0=8, after=z)
            step, vt = by_token([Z[:, 10 + g, c * P:(c + 1) * P] for c in range(4) for g in range(2)], VTK, z)
            step(0)
            step(1)
            nk = tile_norm([(Z[:, t, :], T2, None) for t in (8, 9)], lambda j: vec("k_norm"), None, [z, vt[-1]])
            nq = tile_norm([(Z[:, t, 0:T], T, None) for t in range(8)], lambda j: vec("q_norm"), None, [nk])
            if dve:
                dve.wait_ge(*in_tab)
            roped = rope([Z[:, t, 0:T] for t in (8, 9, *range(8))], vec("rot_ax"), CS[:, 0, :], CS[:, 1, :], nq, (0, 1))
            full = (slice(0, P),)
            units = [(Z[:, h, :], Z[:, 8 + h // 4, :], h // 4, qt * P, 0, full, h) for h in range(8) for qt in range(2)]
            o = attend(units, float(np.float32(P ** -0.5)), lambda c, g: VTK[:, 2 * c + g, :], PB, PT, None, [roped, vt[-1]])
            his, los = [], []
            for h in range(8):
                los.append(keep_split(Y[:, h, 0:T], h, slice(0, T), o))
                his.append(now("hn_hi"))
            y = linear(4, T, Y, [his, los], squares=True)
            x = norms(T, post(1, 1, 1), T, pre(1, 2, 1), [y], 18)
            y = ffn(T, x)
            finish(sp, norms(T, post(1, 2, 1), None, None, [y], None))

        def finish(sp, res):
            if sp:
                for m in res:
                    sp.wait_ge(*m)
                sp.dma_start(out, H[:, :, 0:T]).then_inc(sems["stored"], 16)
                sp.wait_ge(sems["stored"], 16)

        @block.sync
        def _(eng):
            program(sp=eng)

        @block.gpsimd
        def _(eng):
            program(pool=eng)

        @block.scalar
        def _(eng):
            program(act=eng)

        @block.vector
        def _(eng):
            program(dve=eng)

        @block.tensor
        def _(eng):
            program(pe=eng)


def by_feature(a):
    return np.ascontiguousarray(a.reshape(-1, P).T)


def main_blocks(w):
    return w.reshape(KD, P, -1, 256).transpose(2, 1, 0, 3).reshape(-1, P, BLK)


def down_blocks(w):
    return w.reshape(2, HALF, P, KD, P).transpose(3, 0, 2, 1, 4).reshape(-1, P, DBLK)


def gate_up_blocks(gate, up):
    return np.stack([main_blocks(gate), main_blocks(up)], axis=1).reshape(-1, P, BLK)


def axial(rot_dim, heads):
    rows = T // 64
    row = np.repeat(np.arange(rows), 64).astype(np.float32)
    col = np.tile(np.arange(64), rows).astype(np.float32)
    n = rot_dim // 4
    freqs = np.float32(10000.0) ** (-np.arange(n, dtype=np.float32) / np.float32(n))
    ang = np.concatenate([row[:, None] * freqs, col[:, None] * freqs], axis=-1)
    both = np.stack([np.cos(ang), np.sin(ang)]).astype(np.float32)
    return np.ascontiguousarray(np.tile(np.repeat(both, 2, axis=2), (1, 1, heads)).transpose(2, 0, 1))


def rotations():
    nsa, ret, ax = (np.zeros((P, P), np.float32) for _ in range(3))
    for b in (0, 64):
        for j in range(8):
            nsa[b + 8 + j, b + j], nsa[b + j, b + 8 + j] = -1, 1
    for j in range(64):
        ret[64 + j, j], ret[j, 64 + j] = -1, 1
        ax[2 * j + 1, 2 * j], ax[2 * j, 2 * j + 1] = -1, 1
    return nsa, ret, ax


def tables():
    t, f32 = np.arange(P), np.float32
    mask = np.zeros((P, 2 * P), f32)
    mask[:, P:] = np.where(t[None, :] <= t[:, None], 0, NEG)
    tq = np.arange(T).reshape(2, P)
    mask_c = np.where(np.arange(15) * 16 + 31 <= tq[:, :, None], 0, NEG).astype(f32).transpose(1, 0, 2)
    row_ok = (tq >= 31).astype(f32).T
    log_gamma = np.log1p(-np.exp2(-5.0 - np.arange(4)))
    rel = t[None, :] - t[:, None]
    same = np.where(rel[:, None] >= 0, np.exp(np.maximum(rel, 0)[:, None] * log_gamma[:, None]), 0)
    cross = np.exp((rel + P)[:, None] * log_gamma[:, None])
    decay = (np.concatenate([same, cross], axis=2) * P ** -0.5).astype(f32)
    count = np.stack([1.0 / np.minimum(np.arange(16) + 1, 2 ** (g + 1)) for g in range(4)]).reshape(1, 64)
    inv = 1.0 / f32(500000.0) ** (np.arange(0, 16, 2, dtype=f32) / f32(16))
    f_nsa = np.zeros(P, f32)
    for b in (0, 8, 64, 72):
        f_nsa[b:b + 8] = inv
    inv = 1.0 / f32(10000.0) ** (np.arange(0, P, 2, dtype=f32) / f32(P))
    return dict(mask=mask, mask_c=np.ascontiguousarray(mask_c), row_ok=row_ok, decay=decay,
                count=np.tile(count, (P, 1)).astype(f32), f_nsa=f_nsa[:, None], f_ret=np.tile(inv, 2)[:, None])


def kernel(**inputs):
    import concourse.bacc as bacc
    from concourse.bass_utils import run_bass_kernel_spmd

    I = {k: np.asarray(v) for k, v in inputs.items()}
    f32 = np.float32
    tab = tables()
    nsa, ret, ax = rotations()

    w = I["od_w_in"][0]
    heads = [h for j in range(4) for h in (j, j + 4)]
    cols = np.concatenate([np.arange(64 * h, 64 * h + 64) for h in heads] + [np.arange(512, 1280), np.arange(1304, 3352), np.arange(1280, 1304)])
    od_in = np.concatenate([w[:, cols], np.zeros((D, 28 * P - len(cols)), f32)], axis=1)
    rows = np.concatenate([np.arange(64 * h, 64 * h + 64) for h in heads] + [np.arange(512, 1024)])
    F2 = I["ffn_w_in_2"]
    main = [main_blocks(I["ev_w_in"][0]), main_blocks(I["ev_w_out"][0]),
            gate_up_blocks(I["ffn_w_gate"][0], I["ffn_w_up"][0]),
            main_blocks(od_in), main_blocks(I["od_w_out"][0][rows]),
            gate_up_blocks(I["ffn_w_gate"][1], I["ffn_w_up"][1]),
            gate_up_blocks(F2[0, 0][:, :F], F2[0, 0][:, F:]), main_blocks(I["da_w_in_2"][0]), main_blocks(I["da_w_out_2"][0]),
            gate_up_blocks(F2[0, 1][:, :F], F2[0, 1][:, F:]),
            gate_up_blocks(F2[1, 0][:, :F], F2[1, 0][:, F:]), main_blocks(I["ga_w_in_2"][0]), main_blocks(I["ga_w_out_2"][0]),
            gate_up_blocks(F2[1, 1][:, :F], F2[1, 1][:, F:])]
    down = [down_blocks(a) for a in (I["ffn_w_down"][0], I["ffn_w_down"][1], *I["ffn_w_out_2"].reshape(4, F, D))]

    parts = dict(
        mix_pre=by_feature(I["ln_mix_pre"]), mix_post=by_feature(I["ln_mix_post"]), ffn_pre=by_feature(I["ln_ffn_pre"]),
        ffn_post=by_feature(I["ln_ffn_post"]), norm_g=by_feature(I["norm_g_2"]), pool_scale=by_feature(I["ev_pool_scale"]),
        sgu_g=by_feature(I["ev_sgu_ln_g"]), sgu_b=by_feature(I["ev_sgu_ln_b"]), gn_g=by_feature(I["od_ret_gn_g"]),
        subln=by_feature(I["da_subln_2"]), q_norm=by_feature(I["ga_q_norm_2"]), k_norm=by_feature(I["ga_k_norm_2"]),
        ada_b=by_feature(I["ada_b_2"]),
        c=np.stack([by_feature(I["c_2"]), by_feature(I["c_ctx_2"])], axis=2).reshape(P, 16),
        eps6=np.full((P, 1), 1e-6, f32), eps5=np.full((P, 1), 1e-5, f32), f_nsa=tab["f_nsa"], f_ret=tab["f_ret"],
        row_ok=tab["row_ok"], ident=np.eye(P, dtype=f32), ones=np.ones((P, P), f32), rot_nsa=nsa, rot_ret=ret, rot_ax=ax)
    arrays = {
        "w_main": np.concatenate(main), "w_down": np.concatenate(down),
        "w_ada": np.concatenate([main_blocks(a) for a in I["ada_w_2"]]),
        "vec": np.concatenate([parts[n] for n in VEC_COLS], axis=1),
        "x0": np.ascontiguousarray(np.concatenate([I["x"][0].T, I["ctx_2"][0].T], axis=1).reshape(KD, P, T2).transpose(1, 0, 2)),
        "pool_w": np.ascontiguousarray(I["ev_pool_w"][0].transpose(1, 0, 2)),
        "sgu_w": np.ascontiguousarray(I["ev_sgu_w"][0].transpose(2, 0, 1)),
        "sgu_b": np.ascontiguousarray(np.broadcast_to(I["ev_sgu_b"][0], (P, 4, P))),
        "tab_count": tab["count"], "tab_mask": tab["mask"], "tab_mask_c": tab["mask_c"], "tab_decay": tab["decay"],
        "tab_da": axial(64, 2), "tab_ga": axial(128, 1),
        "pos": np.ascontiguousarray(np.broadcast_to(I["positions"].astype(np.int32), (P, T))),
        "cmp_w2": np.ascontiguousarray(np.stack([I["od_cmp_k_w2"][0], I["od_cmp_v_w2"][0]], axis=1)),
        "cmp_pos": np.ascontiguousarray(np.tile(np.stack([I["od_cmp_k_pos"][0].T, I["od_cmp_v_pos"][0].T], axis=1), (2, 1, 1))),
        "da_lambda": np.ascontiguousarray(np.broadcast_to(I["da_lambda_2"][0], (P, 4, 64))),
    }
    for kv in "kv":
        arrays[f"cmp_{kv}_w1"] = np.ascontiguousarray(np.tile(I[f"od_cmp_{kv}_w1"][0].reshape(32, 64, P).transpose(1, 0, 2), (2, 1, 1)))

    nc = bacc.Bacc("TRN2", target_bir_lowering=False, num_devices=1, dynamic_dma_scratch_size=1024)
    A = {}
    for name, a in arrays.items():
        A[name] = nc.dram_tensor(name, a.shape, mybir.dt.from_np(a.dtype), kind="ExternalInput").ap()
    out = nc.dram_tensor("out", (P, KD, T), mybir.dt.float32, kind="ExternalOutput").ap()
    build(nc, A, out)
    r = run_bass_kernel_spmd(nc, [arrays], core_ids=[0])
    return r.results[0]["out"].transpose(2, 1, 0).reshape(1, T, D)
```

```python
from collections import namedtuple
from contextlib import ExitStack

import numpy as np
import concourse.bass as bass
from concourse import mybir

P = 128
D = 1024
KD = D // P
T = 256
T2 = 2 * T
F = 2816
KF = F // P
HALF = KF // 2
BLK = KD * 2 * P
DBLK = HALF * P
NADA = 9 * D // 256
NEG = -1.0e30
LAMBDA_INIT = 0.2

GU, DOWN = 2 * 11, 16


def SEG(blocks):
    return blocks, BLK, 2


FFN = [SEG(GU), (DOWN, DBLK, 1)]
SEGMENTS = ([SEG(6), SEG(4)] + FFN + [SEG(14), SEG(4)] + FFN + FFN + [SEG(12), SEG(4)] + FFN
            + FFN + [SEG(6), SEG(4)] + FFN)
FILL = {0: 1, 1: 7}
GEMV, PER_PAIR = {8: 20, 10: 4, 12: 20, 14: 20}, {8: 2, 10: 1, 12: 2, 14: 2}
assert sum(FILL.values()) + sum(GEMV.values()) == 2 * NADA
SLOTS = 4

SIZES, DONE, ARRIVED, ORDER, ADA_SEG, GEMV_AT = [], [], [], [], {}, {}


def plan():
    loads, done, ada = [0] * SLOTS, 0, 0
    starts = []
    for seg, (blocks, size, tiles) in enumerate(SEGMENTS):
        starts.append(len(SIZES))
        for b in range(blocks):
            n = len(SIZES)
            done += tiles
            loads[n % SLOTS] += 1
            SIZES.append(size)
            DONE.append(done)
            ARRIVED.append(loads[n % SLOTS])
            ORDER.append(("w", seg, n))
            if b == 1:
                for j in range(FILL.get(seg, 0)):
                    slot = (n + 1 + j % 2) % SLOTS
                    loads[slot] += 1
                    ORDER.append(("ada", ada, slot, loads[slot], len(ADA_SEG) + 1))
                    ADA_SEG[ada] = seg
                    ada += 1
        GEMV_AT[seg] = ada
        ada += GEMV.get(seg, 0)
    return starts


STARTS = plan()
NBLK = len(SIZES)
GEMVS = {seg: sum(n for k, n in GEMV.items() if k < seg) for seg in GEMV}
GAINS_AFTER = {8: [(0, 0, 1), (0, 1, 0)], 10: [(0, 1, 1), (0, 2, 0)], 12: [(0, 2, 1), (1, 0, 0)],
               14: [(1, 0, 1), (1, 1, 0), (1, 1, 1), (1, 2, 0), (1, 2, 1)]}
FILLS = {seg: [x[1] for x in ORDER if x[0] == "ada" and ADA_SEG[x[1]] == seg] for seg in range(len(SEGMENTS))}
ADA_AT = {x[1]: (x[2], x[3]) for x in ORDER if x[0] == "ada"}


def lin(table, n, i):
    return table[n] if isinstance(i, int) else i * (table[n + SLOTS] - table[n]) + table[n]


VEC_COLS = {}
_at = 0
for _name, _n in [("mix_pre", 16), ("mix_post", 16), ("ffn_pre", 16), ("ffn_post", 16), ("norm_g", 96),
                  ("pool_scale", 4), ("sgu_g", 4), ("sgu_b", 4), ("gn_g", 4), ("subln", 1), ("q_norm", 1),
                  ("k_norm", 1), ("ada_b", 144), ("c", 16), ("eps6", 1), ("eps5", 1), ("f_nsa", 1),
                  ("f_ret", 1), ("row_ok", 2), ("ident", 128), ("ones", 128), ("rot_nsa", 128),
                  ("rot_ret", 128), ("rot_ax", 128)]:
    VEC_COLS[_name] = (_at, _n)
    _at += _n
NVEC = _at
TAB_COLS = {}
_at = 0
for _name, _n in [("mask", 128), ("mask_c", 30), ("decay", 4 * 256), ("count", 64)]:
    TAB_COLS[_name] = (_at, _n)
    _at += _n
NTAB = _at

Mark = namedtuple("Mark", "sem n")


def build(nc, A, out):
    fp32, f32r, i32 = mybir.dt.float32, mybir.dt.float32r, mybir.dt.int32
    ACT, ALU, AX = mybir.ActivationFunctionType, mybir.AluOpType, mybir.AxisListType.X
    MUL, ADD, SUB = ALU.mult, ALU.add, ALU.subtract
    ds = bass.ds

    with ExitStack() as ctx:
        def sb(name, shape, dt=fp32):
            return ctx.enter_context(nc.sbuf_tensor(name, shape, dt))

        H = sb("H", [P, KD, T2])
        HN = [sb("HN_hi", [P, KD, T2], f32r), sb("HN_lo", [P, KD, T2], f32r)]
        Y = sb("Y", [P, KD, T2])
        WHI = [sb(f"whi{s}", [P, BLK], f32r) for s in range(2)]
        with ExitStack() as g:
            RAW = [g.enter_context(nc.sbuf_tensor(f"raw{s}", [P, BLK], fp32)) for s in range(SLOTS)]
        WLO = [sb(f"wlo{s}", [P, BLK], f32r) for s in range(SLOTS)]
        TMP = [sb(f"tmp{s}", [P, T2]) for s in range(2)]
        HALVES = [sb("half0", [P, 2 * T2]), sb("half1", [P, 2 * T2])]
        SQ = [HALVES[1][:, s * T2:(s + 1) * T2] for s in range(2)]
        ACC = sb("acc", [P, T2])
        DIAG = sb("diag", [P, T2])
        VEC = sb("VEC", [P, NVEC])
        MOD = sb("MOD", [P, 144, 2])
        GA = sb("GA", [P, 2 * 6 * KD * 2])
        SMALL = sb("SMALL", [P, 64])
        with ExitStack() as g:
            G = [g.enter_context(nc.sbuf_tensor("G_hi", [P, KF, T2], f32r)),
                 g.enter_context(nc.sbuf_tensor("G_lo", [P, KF, T2], f32r))]
        ARENA = sb("ARENA", [P, 2 * KF * T2])
        BANK = [ctx.enter_context(nc.psum_tensor(f"bank{n}", [P, 512], fp32)) for n in range(8)]
        sems = {}
        names = ["w_in0", "w_in1", "w_in2", "w_in3", "w_hi", "w_lo", "tile_done",
                 "half_in0", "half_in1", "ada_sum", "ada_red", "ada_used", "ada_out", "gain",
                 "evac", "gate_read", "up_done", "g_hi", "g_lo", "in_h", "in_ctx", "in_vec", "in_tab",
                 "sq", "sq_sum", "gg", "gg_sum", "hg", "hg_sum", "total", "root", "rstd",
                 "scaled", "resid", "normed", "hn_hi", "hn_lo", "act_c",
                 "pe_step", "act_step", "dve_step", "pool_step", "stored"]
        for n in names:
            sems[n] = ctx.enter_context(nc.semaphore(n))
        block = ctx.enter_context(nc.Block())

        def vec(name, a=0, n=None):
            at, size = VEC_COLS[name]
            return VEC[:, at + a:at + (size if n is None else a + n)]

        ident, ones = vec("ident"), vec("ones")

        def carve():
            at = [0]

            def piece(n, *dims, dt=None):
                size = n
                for d in dims:
                    size *= d
                ap = ARENA[:, at[0]:at[0] + size]
                at[0] += size
                assert at[0] <= 2 * KF * T2, at[0]
                if dt is not None:
                    ap = ap.bitcast(dt)
                if len(dims) == 1:
                    ap = ap.rearrange("p (a b) -> p a b", a=n)
                if len(dims) == 2:
                    ap = ap.rearrange("p (a b c) -> p a b c", a=n, b=dims[0])
                return ap
            return piece

        def program(pe=None, act=None, dve=None, pool=None, sp=None):
            count = dict.fromkeys(names, 0)
            NV, NS, NT, NG = nc.vector, nc.scalar, nc.tensor, nc.gpsimd

            def up(name, n=1):
                count[name] += n
                return Mark(sems[name], count[name])

            def now(name):
                return Mark(sems[name], count[name])

            held_acc = [None]
            split = [0]

            def run(eng, blocks, unit, body, head=0):
                n, end = split[0], split[0] + blocks
                for _ in range(head):
                    body(0, n)
                    n += unit
                steps = (end - n - 2) // SLOTS
                if steps >= 2:
                    with eng.Fori(0, steps) as i:
                        for j in range(0, SLOTS, unit):
                            body(i, n + j)
                    n += SLOTS * steps
                while n < end:
                    body(0, n)
                    n += unit

            def load_weights():
                holds = [None] * SLOTS

                def load(slot, src, size, n_sem, n_count, dst_i=None):
                    if n_sem is not None:
                        sp.wait_ge(sems[n_sem], n_count)
                    sp.dma_start(RAW[slot][:, 0:size], src).then_inc(sems[f"w_in{slot}"], 16)

                n8 = nd = 0
                for seg, (blocks, size, tiles) in enumerate(SEGMENTS):
                    base = STARTS[seg]
                    src, at = (A["w_main"], n8) if size == BLK else (A["w_down"], nd)
                    if size == BLK:
                        n8 += blocks
                    else:
                        nd += blocks

                    def one(b):
                        slot = (base + b) % SLOTS
                        load(slot, src[at + b], size, *(holds[slot] or (None, 0)))
                        holds[slot] = ("tile_done", DONE[base + b])
                    for b in range(2 if seg else 0):
                        one(b)
                    for x in ORDER:
                        if x[0] == "ada" and x[1] in FILLS[seg]:
                            slot = x[2]
                            load(slot, A["w_ada"][x[1]], BLK, *(holds[slot] or (None, 0)))
                            holds[slot] = ("ada_used", x[4])
                    for b in range(0 if seg else 2):
                        one(b)
                    gemv, planned = PER_PAIR.get(seg, 0), GEMV.get(seg, 0)

                    def halves(i, t):
                        if t < 0:
                            return
                        for h in range(2 * gemv if t * gemv < planned else 0):
                            used = 8 * (2 * (GEMVS[seg] + gemv * t) + h - 1)
                            if used > 0:
                                sp.wait_ge(sems["ada_sum"], i * 32 * gemv + used)
                            src = A["w_ada"][ds(i * 2 * gemv + (GEMV_AT[seg] + gemv * t + h // 2), 1)].rearrange("a p n -> p (a n)")
                            sp.dma_start(HALVES[h % 2][:, :], src[:, h % 2 * (BLK // 2):(h % 2 + 1) * (BLK // 2)])\
                                .then_inc(sems[f"half_in{h % 2}"], 16)
                    for b in range(2, 6 if blocks > 4 else 4):
                        one(b)
                        if planned and b == 5:
                            yield
                        if b % 2:
                            halves(0, b // 2 - 2)
                    b, steps = 6, (blocks - 6) // SLOTS
                    if steps >= 2:
                        with sp.Fori(0, steps) as i:
                            for j in range(SLOTS):
                                slot = (base + b + j) % SLOTS
                                sp.wait_ge(sems["tile_done"], lin(DONE, base + b + j - SLOTS, i))
                                sp.dma_start(RAW[slot][:, 0:size],
                                             src[ds(i * SLOTS + (at + b + j), 1)].rearrange("a p n -> p (a n)"))\
                                    .then_inc(sems[f"w_in{slot}"], 16)
                                if j % 2:
                                    halves(i, (b + j) // 2 - 2)
                        b += SLOTS * steps
                        for j in range(SLOTS):
                            holds[(base + b - SLOTS + j) % SLOTS] = ("tile_done", DONE[base + b - SLOTS + j])
                    while b < blocks:
                        one(b)
                        if b % 2:
                            halves(0, b // 2 - 2)
                        b += 1
                    halves(0, blocks // 2 - 2)

            def split_hi(i, n):
                if n < NBLK:
                    slot, size = n % SLOTS, SIZES[n]
                    act.wait_ge(sems[f"w_in{slot}"], lin(ARRIVED, n, i) * 16)
                    NS.activation(WHI[n % 2][:, 0:size], RAW[slot][:, 0:size], ACT.Copy).then_inc(sems["w_hi"], 1)

            def split_lo(i, n):
                if n < NBLK:
                    slot, size = n % SLOTS, SIZES[n]
                    dve.wait_ge(sems["w_hi"], lin(range(1, NBLK + 1), n, i))
                    NV.tensor_tensor(WLO[slot][:, 0:size], RAW[slot][:, 0:size], WHI[n % 2][:, 0:size].bitcast(fp32), SUB)\
                        .then_inc(sems["w_lo"], 1)

            def product(out, n, col, wk, x, k, kx, N, w, xp, start, stop):
                return NT.matmul(out[:, 0:N], (WHI[n % 2], WLO[n % SLOTS])[w][:, k * wk + col:k * wk + col + P],
                                 x[xp][:, kx, 0:N], start=start, stop=stop)

            def three(bank, N, n, x, col, kt, wk, x0=0, start=True, stop=True):
                steps = [(a, b, k) for a, b in ((0, 0), (0, 1), (1, 0)) for k in range(kt)]
                for j, (a, b, k) in enumerate(steps):
                    mm = product(bank, n, col, wk, x, k, x0 + k, N, a, b, start and j == 0, stop and j == len(steps) - 1)
                return mm

            def first_blocks(N, n, ready, after):
                LAG = 5
                for j in range(KD + LAG):
                    for m in range(2):
                        if j < KD:
                            if m == 0:
                                pe.wait_ge(*ready[0][j])
                            for w in range(2):
                                product(BANK[m], n, m * P, 2 * P, HN, j, j, N, w, 0, j == 0 and w == 0, False)
                    for m in range(2):
                        if 1 <= j <= KD:
                            if m == 0:
                                pe.wait_ge(*ready[1][j - 1])
                            mm = product(BANK[m], n, m * P, 2 * P, HN, j - 1, j - 1, N, 0, 1, False, j == KD)
                            if j == KD:
                                mm.then_inc(sems["tile_done"], 1)
                    if j == LAG:
                        pe.wait_ge(sems["w_lo"], n + 2)
                        if after is not None:
                            pe.wait_ge(*after)
                    for m in range(2):
                        for w, xp in ((0, 0), (1, 0), (0, 1)) if j >= LAG else ():
                            k = j - LAG
                            mm = product(BANK[2 + m], n + 1, m * P, 2 * P, HN, k, k, N, w, xp, k == 0 and (w, xp) == (0, 0),
                                         k == KD - 1 and xp == 1)
                        if j == KD + LAG - 1:
                            mm.then_inc(sems["tile_done"], 1)

            YY, GG, HG = ACC, HALVES[0][:, 0:T2], HALVES[0][:, T2:2 * T2]

            def clear_sum(N):
                z = up("dve_step")
                if on(dve, held_acc[0]):
                    NV.memset(YY[:, 0:N], 0.0)
                    NV.memset(HALVES[0][:, :], 0.0).then_inc(z.sem, 1)
                return z

            def add_square(i, s0, step, index, k, buf, N):
                first = isinstance(i, int) and not index
                dve.wait_ge(sems["sq"], i * step + (s0[0] + index + 1))
                if not first:
                    dve.wait_ge(sems["sq_sum"], i * step + (s0[1] + index))
                NV.tensor_tensor(YY[:, 0:N], YY[:, 0:N], SQ[buf][:, 0:N], ADD).then_inc(sems["sq_sum"], 1)
                dve.wait_ge(sems["evac"], i * step + (s0[2] + index + 1))
                if not first:
                    dve.wait_ge(sems["hg_sum"], i * step + (s0[1] + index))
                NV.tensor_tensor(TMP[0][:, 0:N], H[:, k, 0:N], Y[:, k, 0:N], MUL).then_inc(sems["hg"], 1)
                dve.wait_ge(sems["gg"], i * step + (s0[1] + index + 1))
                NV.tensor_tensor(GG[:, 0:N], GG[:, 0:N], DIAG[:, 0:N], ADD).then_inc(sems["gg_sum"], 1)
                dve.wait_ge(sems["hg"], i * step + (s0[1] + index + 1))
                NV.tensor_tensor(HG[:, 0:N], HG[:, 0:N], TMP[0][:, 0:N], ADD).then_inc(sems["hg_sum"], 1)

            def put_out(i, s0, step, index, dst, bank, buf, N, gains, k=None):
                if gains is None:
                    NS.activation(dst, bank[:, 0:N], ACT.Copy).then_inc(sems["evac"], 1)
                    return
                first = isinstance(i, int) and not index
                if index >= 2 or not isinstance(i, int):
                    act.wait_ge(sems["sq_sum"], i * step + (s0[1] + index - 1))
                NS.activation(SQ[buf][:, 0:N], bank[:, 0:N], ACT.Square).then_inc(sems["sq"], 1)
                if not first:
                    act.wait_ge(sems["gg_sum"], i * step + (s0[1] + index))
                for c, n, gain, _ in gains:
                    op = NS.activation(DIAG[:, c:c + n], bank[:, c:c + n], ACT.Square, scale=gain(k))
                op.then_inc(sems["gg"], 1)
                for c, n, gain, _ in gains:
                    op = NS.activation(Y[:, k if isinstance(k, int) else ds(k, 1), c:c + n], bank[:, c:c + n], ACT.Copy, scale=gain(k))
                op.then_inc(sems["evac"], 1)

            def here():
                return split[0], count["evac"]

            def linear(blocks, N, dst, ready=(None,), gains=None, after=None, base=None):
                (n0, e0), s0 = base or here(), (count["sq"], count["sq_sum"], count["evac"])
                squares = gains is not None
                zero = clear_sum(N) if squares else None

                def at(i, n, per=2):
                    return 2 * (n - n0)
                if on(pe, None if ready[0] else after):
                    def body(i, n):
                        if n == n0 + 1 and isinstance(i, int) and ready[0] is not None:
                            return
                        pe.wait_ge(sems["w_lo"], lin(range(1, NBLK + 1), n, i))
                        banks = [BANK[2 * ((n - n0) % 2) + m] for m in range(2)]
                        if n - n0 >= 2:
                            pe.wait_ge(sems["evac"], i * 8 + (e0 + at(i, n) - 2))
                        if n == n0 and isinstance(i, int) and ready[0] is not None:
                            return first_blocks(N, n, ready, after)
                        for m in range(2):
                            three(banks[m], N, n, HN, m * P, KD, 2 * P).then_inc(sems["tile_done"], 1)
                    run(pe, blocks, 1, body, head=0 if base else 2)
                if on(act, now("gain") if squares and count["gain"] else None):
                    def body(i, n):
                        for m in range(2):
                            t = at(i, n) + m
                            act.wait_ge(sems["tile_done"], i * 8 + (DONE[n] - 1 + m))
                            put_out(i, s0, 8, t, dst[:, ds(i * 8 + t, 1), 0:N], BANK[2 * ((n - n0) % 2) + m], m, N, gains, t)
                        split_hi(i, n + 2)
                    run(act, blocks, 1, body, head=0 if base else 2)
                if on(dve, zero):
                    def body(i, n):
                        if squares:
                            for m in range(2):
                                add_square(i, s0, 8, at(i, n) + m, at(i, n) + m, m, N)
                        split_lo(i, n + 2)
                    run(dve, blocks, 1, body, head=0 if base else 2)
                split[0] += blocks
                for x in SUMS if squares else ():
                    up(x, 2 * blocks)
                return up("evac", 2 * blocks)

            def gemv_half(i, t, h, gemv, base):
                acc, dst = (t * gemv + h // 2) % 2, (ACC, DIAG)
                dve.wait_ge(sems[f"half_in{h % 2}"], i * 16 * 2 * gemv + 16 * (base + gemv * t + h // 2 + 1))
                if h % 2 == 0:
                    need = base + gemv * t + h // 2 - 1
                    if need > 0:
                        dve.wait_ge(sems["ada_red"], i * 2 * gemv + need)
                for k in range(4):
                    for s in range(2):
                        at = 16 * (base + gemv * t) + 8 * h + 2 * k + s
                        if at > 1:
                            dve.wait_ge(sems["ada_sum"], i * 32 * gemv + at - 1)
                        out, w, c = dst[acc][:, s * T:(s + 1) * T], HALVES[h % 2][:, k * T:(k + 1) * T], C[:, 4 * (h % 2) + k, s:s + 1]
                        if k == 0 and h % 2 == 0:
                            op = NV.tensor_scalar(out, w, c, None, MUL)
                        else:
                            op = NV.scalar_tensor_tensor(out, w, c, out, MUL, ADD)
                        op.then_inc(sems["ada_sum"], 1)

            def gemv_reduce(i, t, gemv, base):
                for a in range(gemv):
                    b = gemv * t + a
                    pe.wait_ge(sems["ada_sum"], i * 32 * gemv + 16 * (base + b + 1))
                    for m in range(2):
                        for s in range(2):
                            mm = NT.matmul(BANK[7][:, ds(i * 8 * gemv + (4 * b + 2 * m + s), 1)],
                                           (ACC, DIAG)[b % 2][:, s * T + m * P:s * T + (m + 1) * P], ones[:, 0:1],
                                           start=True, stop=True)
                    mm.then_inc(sems["ada_red"], 1)

            def adaln_gain(L, j, which, mods):
                at = (6 * L + 3 * which + j) * 2 * KD
                row, n = 3 * j + 1 + which, 2 * j + which
                mod = MOD[:, 72 * L + 8 * row:72 * L + 8 * row + 8, :]
                g = vec("norm_g", (6 * L + n) * KD, KD).unsqueeze(2).to_broadcast([P, KD, 2])
                done = up("gain")
                if on(dve, mods):
                    NV.scalar_tensor_tensor(GA[:, at:at + 2 * KD].rearrange("p (k s) -> p k s", s=2), mod, (0.5, 1.0, 0.5)[j] if which else 1.0, g,
                                            MUL if which else ADD, MUL).then_inc(done.sem, 1)
                return done

            def gemv_keep(seg):
                blocks, first = GEMV[seg], 2 * GEMV_AT[seg]
                up("ada_sum", 16 * blocks)
                reduced, kept = up("ada_red", blocks), up("ada_out")
                if on(dve, reduced):
                    NV.tensor_tensor(MOD[:, first:first + 2 * blocks, :], BANK[7][:, 0:4 * blocks].rearrange("p (a s) -> p a s", s=2),
                                     vec("ada_b")[:, first:first + 2 * blocks].unsqueeze(2).to_broadcast([P, 2 * blocks, 2]), ADD)\
                        .then_inc(kept.sem, 1)
                for L, j, which in GAINS_AFTER[seg]:
                    adaln_gain(L, j, which, kept)

            SUMS = ("sq", "sq_sum", "gg", "gg_sum", "hg", "hg_sum")

            def ffn(N, gains, ready, after=None, seg=None):
                gemv, planned = PER_PAIR.get(seg, 0), GEMV.get(seg, 0)
                n0 = split[0]
                g0, u0, h0, l0 = (count[x] for x in ("gate_read", "up_done", "g_hi", "g_lo"))
                base = count["ada_red"]
                if planned and sp:
                    sp.wait_ge(*now("hn_hi"))
                    next(loader, None)
                if pe:
                    def body(i, n):
                        if n == n0:
                            pe.wait_ge(sems["w_lo"], n + 1)
                            return first_blocks(N, n, ready, after)
                        for s in range(2):
                            if s == 0 and n > n0 + 2 and planned:
                                gemv_reduce(i, (n - n0) // 2 - 2, gemv, base)
                            pe.wait_ge(sems["w_lo"], lin(range(1, NBLK + 1), n + s, i))
                            if n > n0:
                                pe.wait_ge(sems["up_done" if s else "gate_read"], i * 4 + ((u0 if s else g0) + n - n0))

                            for m in range(2):
                                three(BANK[2 * s + m], N, n + s, HN, m * P, KD, 2 * P).then_inc(sems["tile_done"], 1)
                    run(pe, GU, 2, body, head=2)
                    if planned:
                        gemv_reduce(0, GU // 2 - 2, gemv, base)
                if act:
                    def body(i, n):
                        for m in range(2):
                            act.wait_ge(sems["tile_done"], i * 8 + (DONE[n] - 1 + m))
                            act.wait_ge(sems["g_lo"], i * 4 + (l0 + n - n0))
                            NS.activation(TMP[m][:, 0:N], BANK[m][:, 0:N], ACT.Silu).then_inc(sems["gate_read"], 1)
                        split_hi(i, n + 2)
                        act.wait_ge(sems["tile_done"], lin(DONE, n + 1, i))
                        split_hi(i, n + 3)
                        for m in range(2):
                            act.wait_ge(sems["up_done"], i * 4 + (u0 + n - n0 + m + 1))
                            NS.activation(G[0][:, ds(i * 4 + (n - n0 + m), 1), 0:N], TMP[m][:, 0:N], ACT.Copy)\
                                .then_inc(sems["g_hi"], 1)
                    run(act, GU, 2, body, head=1)
                if dve:
                    def body(i, n):
                        halves = 2 * gemv if n > n0 else 0
                        for h in range(halves // 2):
                            gemv_half(i, (n - n0) // 2 - 1, h, gemv, base)
                        split_lo(i, n + 2)
                        for h in range(halves // 2, halves):
                            gemv_half(i, (n - n0) // 2 - 1, h, gemv, base)
                        for m in range(2):
                            dve.wait_ge(sems["gate_read"], i * 4 + (g0 + n - n0 + m + 1))
                            dve.wait_ge(sems["tile_done"], i * 8 + (DONE[n + 1] - 1 + m))
                            NV.tensor_tensor(TMP[m][:, 0:N], TMP[m][:, 0:N], BANK[2 + m][:, 0:N], MUL)\
                                .then_inc(sems["up_done"], 1)
                        split_lo(i, n + 3)
                        for m in range(2):
                            dve.wait_ge(sems["g_hi"], i * 4 + (h0 + n - n0 + m + 1))
                            kt = ds(i * 4 + (n - n0 + m), 1)
                            NV.tensor_tensor(G[1][:, kt, 0:N], TMP[m][:, 0:N], G[0][:, kt, 0:N].bitcast(fp32), SUB)\
                                .then_inc(sems["g_lo"], 1)
                    run(dve, GU, 2, body, head=2)
                split[0] += GU
                for x in ("gate_read", "up_done", "g_hi"):
                    up(x, KF)
                hidden = up("g_lo", KF)
                if planned:
                    gemv_keep(seg)
                    if act:
                        act.wait_ge(*now("ada_sum"))

                n1, e1, s0 = split[0], count["evac"], (count["sq"], count["sq_sum"], count["evac"])
                zero = clear_sum(N)
                if pe:
                    pe.wait_ge(*now("gate_read"))
                    pe.wait_ge(hidden.sem, hidden.n - 2)

                    def body(i, n):
                        m = (n - n1) // 2
                        if m >= 2 or not isinstance(i, int):
                            pe.wait_ge(sems["evac"], i * 2 + (e1 + m - 1))
                        for s in range(2):
                            pe.wait_ge(sems["w_lo"], lin(range(1, NBLK + 1), n + s, i))
                            if m == 0 and s == 1:
                                pe.wait_ge(*hidden)
                            three(BANK[m % 2], N, n + s, G, 0, HALF, P, s * HALF, s == 0, s == 1).then_inc(sems["tile_done"], 1)
                    run(pe, DOWN, 2, body, head=1)
                if on(act, hidden, now("gain") if count["gain"] else None):
                    NS.activation(SMALL[:, 47:48], vec("eps6"), ACT.Sqrt)

                    def body(i, n):
                        m = (n - n1) // 2
                        act.wait_ge(sems["tile_done"], lin(DONE, n, i))
                        split_hi(i, n + 2)
                        act.wait_ge(sems["tile_done"], lin(DONE, n + 1, i))
                        put_out(i, s0, 2, m, None, BANK[m % 2], m % 2, N, gains, m if isinstance(i, int) else i * 2 + m)
                        split_hi(i, n + 3)
                    run(act, DOWN, 2, body, head=1)
                if on(dve, zero):
                    def body(i, n):
                        split_lo(i, n + 2)
                        m = (n - n1) // 2
                        add_square(i, s0, 2, m, m if isinstance(i, int) else ds(i * 2 + m, 1), m % 2, N)
                        split_lo(i, n + 3)
                    run(dve, DOWN, 2, body, head=1)
                split[0] += DOWN
                for x in SUMS:
                    up(x, KD)
                return up("evac", KD)

            def on(eng, *marks):
                if eng is None:
                    return False
                for m in marks:
                    if m is not None:
                        eng.wait_ge(*m)
                return True

            def bcast(ap, *shape):
                return ap.to_broadcast([P, *shape])

            filling = {}

            def fill_begin(seg, bank, *free):
                filling.update(blocks=FILLS[seg], at=0, bank=BANK[bank], free=free)

            def fill(products):
                for _ in range(products):
                    block, tile, k = filling["at"] // 16, filling["at"] // 8, filling["at"] % 8
                    if block >= len(filling["blocks"]):
                        return
                    if pe:
                        slot, loads = ADA_AT[filling["blocks"][block]]
                        if filling["at"] == 0:
                            for m in (*filling["free"], silu_c):
                                if m is not None:
                                    pe.wait_ge(*m)
                        if filling["at"] % 16 == 0:
                            pe.wait_ge(sems[f"w_in{slot}"], 16 * loads)
                        col = k * 2 * P + (tile % 2) * P
                        mm = NT.matmul(filling["bank"][:, 2 * tile:2 * tile + 2], RAW[slot][:, col:col + P], C[:, k, :],
                                       start=k == 0, stop=k == KD - 1)
                        if filling["at"] % 16 == 15:
                            mm.then_inc(sems["ada_used"], 1)
                    filling["at"] += 1

            def fill_end():
                fill(16 * len(filling["blocks"]))
                n = len(filling["blocks"])
                if not n:
                    return None
                done = up("ada_used", n)
                tiles = slice(2 * filling["blocks"][0], 2 * filling["blocks"][0] + 2 * n)
                kept = up("ada_out")
                if on(dve, done):
                    NV.tensor_tensor(MOD[:, tiles, :], filling["bank"][:, 0:4 * n].rearrange("p (a s) -> p a s", s=2),
                                     vec("ada_b")[:, tiles].unsqueeze(2).to_broadcast([P, 2 * n, 2]), ADD).then_inc(kept.sem, 1)
                return kept

            def inverse_root(N, total, sums, at, *ready):
                c = N // P
                root, inv = up("root"), up("rstd")
                if on(act, total, *ready):
                    NS.activation(SMALL[:, at:at + c], sums, ACT.Sqrt, bias=vec("eps6"), scale=1.0 / D).then_inc(root.sem, 1)
                if on(dve, root):
                    NV.reciprocal(SMALL[:, at:at + c], SMALL[:, at:at + c]).then_inc(inv.sem, 1)
                return inv

            def spread_out(N, at, buf, out_bank, inv):
                diag, spread = up("dve_step"), up("pe_step")
                if on(dve, inv):
                    for j in range(N // P):
                        op = NV.tensor_scalar(buf[:, j * P:(j + 1) * P], ident, SMALL[:, at + j:at + j + 1], None, MUL)
                    op.then_inc(diag.sem, 1)
                if on(pe, diag):
                    NT.matmul(out_bank[:, 0:N], ones, buf[:, 0:N], start=True, stop=True).then_inc(spread.sem, 1)
                return spread

            RMS_Y, RMS_H, T1, T2C, HH = 32, 36, 24, 28, 40

            def add_up(buf, N, bank, at, *ready):
                total = up("total")
                if on(pe, *ready):
                    for c in range(N // P):
                        mm = NT.matmul(bank[:, at + c:at + c + 1], buf[:, c * P:(c + 1) * P], ones[:, 0:1], start=True, stop=True)
                    mm.then_inc(total.sem, 1)
                return total

            def square_sum(c0, N, *ready, fills=0, first_block=False):
                s0, t0 = count["sq"], count["total"]
                if on(act, *ready):
                    for k in range(KD):
                        if k >= 2:
                            act.wait_ge(sems["total"], t0 + k - 1)
                        NS.activation(SQ[k % 2][:, 0:N], H[:, k, c0:c0 + N], ACT.Square).then_inc(sems["sq"], 1)
                        if first_block and k == KD - 4:
                            split_hi(0, 0)
                if dve and first_block:
                    split_lo(0, 0)
                for k in range(KD):
                    if pe:
                        pe.wait_ge(sems["sq"], s0 + k + 1)
                        for c in range(N // P):
                            mm = NT.matmul(BANK[4][:, c:c + 1], SQ[k % 2][:, c * P:(c + 1) * P], ones[:, 0:1],
                                           start=k == 0 and c == 0, stop=k == KD - 1, skip_group_check=True)
                        mm.then_inc(sems["total"], 1)
                    fill(fills)
                up("sq", KD)
                total, kept = up("total", KD), up("dve_step")
                if on(dve, total):
                    NV.tensor_copy(SMALL[:, HH + c0 // P:HH + (c0 + N) // P], BANK[4][:, 0:N // P]).then_inc(kept.sem, 1)
                return kept

            def norms(N, post, n_pre, pre, ready, seg):
                if seg != 0:
                    filling.update(blocks=[], at=0)
                if pe and count["ada_out"]:
                    pe.wait_ge(*now("ada_out"))
                if dve and count["gain"]:
                    dve.wait_ge(*now("gain"))
                known = ready[-1]
                if post:
                    c = N // P
                    total = add_up(YY, N, BANK[6], 0, now("sq_sum"), *ready)
                    held_acc[0] = total
                    inv = inverse_root(N, total, BANK[6][:, 0:c], RMS_Y, *ready)
                    if pre:
                        add_up(GG, N, BANK[4], 0, now("gg_sum"))
                        total = add_up(HG, N, BANK[4], 4, now("hg_sum"))
                        held_acc[0] = total
                    rs_y = spread_out(N, RMS_Y, DIAG, BANK[7], inv)
                    if pre:
                        a1, a2, a3, a4, a5, a6 = (up("dve_step") for _ in range(6))
                        rms, hh = SMALL[:, RMS_Y:RMS_Y + c], SMALL[:, HH:HH + c]
                        t1, t2 = SMALL[:, T1:T1 + c], SMALL[:, T2C:T2C + c]
                        if on(dve, total):
                            NV.tensor_tensor(t1, BANK[4][:, 4:4 + c], rms, MUL).then_inc(a1.sem, 1)
                            NV.tensor_tensor(t2, BANK[4][:, 0:c], rms, MUL).then_inc(a2.sem, 1)
                            dve.wait_ge(*a1)
                            NV.scalar_tensor_tensor(hh, t1, 2.0, hh, MUL, ADD).then_inc(a3.sem, 1)
                            dve.wait_ge(*a2)
                            NV.tensor_tensor(t2, t2, rms, MUL).then_inc(a4.sem, 1)
                            dve.wait_ge(*a4)
                            NV.tensor_tensor(hh, hh, t2, ADD).then_inc(a5.sem, 1)
                            dve.wait_ge(*a5)
                            NV.tensor_scalar(hh, hh, 0.0, None, ALU.max).then_inc(a6.sem, 1)
                        known = a6
                if not pre:
                    last = up("resid", KD)
                    c0, r0 = count["scaled"], last.n - KD
                    if on(dve, rs_y, *ready):
                        for k in range(KD + 1):
                            if k < KD:
                                if k >= 2:
                                    dve.wait_ge(sems["resid"], r0 + k - 1)
                                NV.tensor_tensor(TMP[k % 2][:, 0:N], Y[:, k, 0:N], BANK[7][:, 0:N], MUL).then_inc(sems["scaled"], 1)
                            if k:
                                dve.wait_ge(sems["scaled"], c0 + k)
                                NV.tensor_tensor(H[:, k - 1, 0:N], H[:, k - 1, 0:N], TMP[(k - 1) % 2][:, 0:N], ADD)\
                                    .then_inc(sems["resid"], 1)
                    up("scaled", KD)
                    return [last]
                inv = inverse_root(n_pre, known, SMALL[:, HH:HH + n_pre // P], RMS_H)
                rs_h = spread_out(n_pre, RMS_H, SQ[1], BANK[5], inv)
                kept = fill_end()
                c0, r0, n0, h0, l0 = (count[x] for x in ("scaled", "resid", "normed", "hn_hi", "hn_lo"))
                if on(dve, *ready):
                    if post:
                        dve.wait_ge(*rs_y)
                    for j in range(KD + 3):
                        if post and j < KD:
                            if j >= 2:
                                dve.wait_ge(sems["resid"], r0 + j - 1)
                            NV.tensor_tensor(TMP[j % 2][:, 0:N], Y[:, j, 0:N], BANK[7][:, 0:N], MUL).then_inc(sems["scaled"], 1)
                        k = j - 1
                        if post and 0 <= k < KD:
                            dve.wait_ge(sems["scaled"], c0 + k + 1)
                            NV.tensor_tensor(H[:, k, 0:N], H[:, k, 0:N], TMP[k % 2][:, 0:N], ADD).then_inc(sems["resid"], 1)
                        k = j - 2
                        if 0 <= k < KD:
                            if k == 0:
                                dve.wait_ge(*rs_h)
                            if post:
                                dve.wait_ge(sems["resid"], r0 + k + 1)
                            for c, n, gain, shift in pre:
                                op = NV.scalar_tensor_tensor(Y[:, k, c:c + n], H[:, k, c:c + n], gain(k), BANK[5][:, c:c + n], MUL, MUL)
                            op.then_inc(sems["normed"], 1)
                        k = j - 3
                        if k >= 0:
                            dve.wait_ge(sems["hn_hi"], h0 + k + 1)
                            for c, n, gain, shift in pre:
                                t, hi = Y[:, k, c:c + n], HN[0][:, k, c:c + n].bitcast(fp32)
                                if shift is None:
                                    op = NV.tensor_tensor(HN[1][:, k, c:c + n], t, hi, SUB)
                                else:
                                    op = NV.scalar_tensor_tensor(HN[1][:, k, c:c + n], t, shift(k), hi, ADD, SUB)
                            op.then_inc(sems["hn_lo"], 1)
                if act:
                    for k in range(KD):
                        act.wait_ge(sems["normed"], n0 + k + 1)
                        for c, n, gain, shift in pre:
                            if shift is None:
                                op = NS.activation(HN[0][:, k, c:c + n], Y[:, k, c:c + n], ACT.Copy)
                            else:
                                op = NS.activation(HN[0][:, k, c:c + n], Y[:, k, c:c + n], ACT.Identity, bias=shift(k))
                        op.then_inc(sems["hn_hi"], 1)
                if post:
                    up("scaled", KD)
                    up("resid", KD)
                for x in ("normed", "hn_hi", "hn_lo"):
                    up(x, KD)
                return [[Mark(sems["hn_hi"], h0 + k + 1) for k in range(KD)],
                        [Mark(sems["hn_lo"], l0 + k + 1) for k in range(KD)], kept]

            def keep_split(src, k, cols, *ready):
                hi = up("hn_hi")
                if on(act, *ready):
                    NS.activation(HN[0][:, k, cols], src, ACT.Copy).then_inc(hi.sem, 1)
                lo = up("hn_lo")
                if on(dve, hi):
                    NV.tensor_tensor(HN[1][:, k, cols], src, HN[0][:, k, cols].bitcast(fp32), SUB).then_inc(lo.sem, 1)
                return lo

            def rope(tiles, rot, cos, sin, *ready, banks=(4, 5, 6, 7)):
                free = [None] * len(banks)
                for j, t in enumerate(tiles):
                    b = j % len(banks)
                    bank = BANK[banks[b]]
                    turned = up("pe_step")
                    if on(pe, free[b], *ready):
                        NT.matmul(bank[:, 0:T], rot, t, start=True, stop=True).then_inc(turned.sem, 1)
                    part = up("dve_step")
                    if on(dve, turned):
                        NV.tensor_tensor(TMP[j % 2][:, 0:T], bank[:, 0:T], sin, MUL).then_inc(part.sem, 1)
                    free[b] = part
                    straight = up("dve_step")
                    if on(dve):
                        NV.tensor_tensor(t, t, cos, MUL).then_inc(straight.sem, 1)
                    done = up("dve_step")
                    if on(dve, straight):
                        NV.tensor_tensor(t, t, TMP[j % 2][:, 0:T], ADD).then_inc(done.sem, 1)
                return done

            def tile_norm(items, gain, factor, ready, eps=vec("eps6"), banks=(5, 6)):
                sums, chunks, last = BANK[4], 0, [None, None]
                for j, (src, N, k) in enumerate(items):
                    sq, total = up("act_step"), up("pe_step")
                    if on(act, last[j % 2], *ready):
                        NS.activation(SQ[j % 2][:, 0:N], src, ACT.Square).then_inc(sq.sem, 1)
                    if on(pe, sq):
                        for c in range(N // P):
                            mm = NT.matmul(sums[:, chunks + c:chunks + c + 1], SQ[j % 2][:, c * P:(c + 1) * P], ones[:, 0:1],
                                           start=True, stop=True)
                        mm.then_inc(total.sem, 1)
                    last[j % 2] = total
                    chunks += N // P
                root, inv, fac = up("act_step"), up("dve_step"), up("dve_step")
                if on(act, total):
                    NS.activation(TMP[0][:, 0:chunks], sums[:, 0:chunks], ACT.Sqrt, bias=eps, scale=1.0 / P).then_inc(root.sem, 1)
                if on(dve, root):
                    NV.reciprocal(TMP[0][:, 0:chunks], TMP[0][:, 0:chunks]).then_inc(inv.sem, 1)
                    dve.wait_ge(*inv)
                    NV.tensor_scalar(TMP[0][:, 0:chunks], TMP[0][:, 0:chunks], 1.0 if factor is None else factor, None, MUL).then_inc(fac.sem, 1)
                ats = [sum(N // P for _, N, _ in items[:j]) for j in range(len(items))]
                spreads, dones, his, los = [None, None], [None, None], [], []

                def diagonal(j):
                    N, b = items[j][1], j % 2
                    diag, spread = up("dve_step"), up("pe_step")
                    if on(dve, fac, spreads[b]):
                        for c in range(N // P):
                            op = NV.tensor_scalar(SQ[b][:, c * P:(c + 1) * P], ident, TMP[0][:, ats[j] + c:ats[j] + c + 1], None, MUL)
                        op.then_inc(diag.sem, 1)
                    if on(pe, diag, dones[b]):
                        NT.matmul(BANK[banks[b]][:, 0:N], ones, SQ[b][:, 0:N], start=True, stop=True).then_inc(spread.sem, 1)
                    spreads[b] = spread
                diagonal(0)
                for j in range(len(items) + 1):
                    if j + 1 < len(items):
                        diagonal(j + 1)
                    if j < len(items):
                        src, N, k = items[j]
                        done = up("dve_step")
                        if on(dve, spreads[j % 2]):
                            NV.scalar_tensor_tensor(src, src, gain(j), BANK[banks[j % 2]][:, 0:N], MUL, MUL).then_inc(done.sem, 1)
                        dones[j % 2] = done
                        if k is not None:
                            hi = up("hn_hi")
                            if on(act, done):
                                NS.activation(HN[0][:, k, 0:N], src, ACT.Copy).then_inc(hi.sem, 1)
                            his.append(hi)
                    if his and j:
                        src, N, k = items[j - 1]
                        lo = up("hn_lo")
                        if on(dve, his[j - 1]):
                            NV.tensor_tensor(HN[1][:, k, 0:N], src, HN[0][:, k, 0:N].bitcast(fp32), SUB).then_inc(lo.sem, 1)
                        los.append(lo)
                return [his, los, None] if his else done

            def by_token(src, dst, ready, free=None, banks=(4, 5)):
                last, marks = [free] * len(banks), []

                def step(g):
                    j, b = 4 * g, g % len(banks)
                    turned = up("pe_step")
                    n = min(4, len(src) - j)
                    if on(pe, last[b], ready):
                        for m in range(n):
                            mm = NT.transpose(BANK[banks[b]][:, m * P:(m + 1) * P], src[j + m], ident)
                        mm.then_inc(turned.sem, 1)
                    kept = up("act_step")
                    if on(act, turned):
                        NS.activation(dst[:, j:j + n, :].rearrange("p a q -> p (a q)"), BANK[banks[b]][:, 0:n * P], ACT.Copy).then_inc(kept.sem, 1)
                    last[b] = kept
                    marks.append(kept)
                return step, marks

            def all_by_token(src, dst, ready, free=None, banks=(4, 5)):
                step, marks = by_token(src, dst, ready, free, banks)
                for g in range((len(src) + 3) // 4):
                    step(g)
                return marks[-1]

            head_turned = {}
            in_h, in_vec, in_ctx = up("in_h", 16), up("in_vec", 16), up("in_ctx", 16)
            if act:
                act.dma_start(VEC[:, :], A["vec"]).then_inc(in_vec.sem, 16)
            if sp:
                sp.dma_start(H[:, :, 0:T], A["x0"][:, :, 0:T]).then_inc(in_h.sem, 16)
            loader = load_weights() if sp else None
            if sp:
                next(loader, None)

            silu_c = up("act_c")
            C = SMALL[:, 48:64].rearrange("p (k s) -> p k s", s=2)
            if on(act, in_vec):
                NS.activation(SMALL[:, 48:64], vec("c"), ACT.Silu).then_inc(silu_c.sem, 1)



            def column(ap, first, step, k):
                return ap[:, first + step * k:first + step * k + 1] if isinstance(k, int) else ap[:, ds(k * step + first, 1)]

            def gain1(name, layer):
                return [(0, T, lambda k: column(VEC, VEC_COLS[name][0] + layer * KD, 1, k), None)]

            def pre(L, j, seqs=2):
                return [(T * s, T, lambda k, s=s: column(GA, ((L * 6 + j) * KD) * 2 + s, 2, k), lambda k, s=s: MOD[:, 72 * L + 24 * j + k, s:s + 1])
                        for s in range(seqs)]

            def post(L, j, seqs=2):
                return [(T * s, T, lambda k, s=s: column(GA, ((L * 6 + 3 + j) * KD) * 2 + s, 2, k), None) for s in range(seqs)]

            piece = carve()
            Z = piece(12, T)
            DIFF = piece(4, T)
            W1, W2 = piece(T), piece(T)
            POOLW, SGUW, SGUB = piece(4, P), piece(4, P), piece(4, P)
            COUNT = piece(4, 16)
            VT = piece(8, P)
            fill_begin(0, 7)
            hh = square_sum(0, T, in_h, in_vec, fills=2, first_block=True)
            if act:
                split_hi(0, 1)
            if dve:
                split_lo(0, 1)
            x = norms(T, None, T, gain1("mix_pre", 0), [hh], 0)
            in_tab = up("in_tab", 64)
            if act:
                act.dma_start(H[:, :, T:T2], A["x0"][:, :, T:T2]).then_inc(in_ctx.sem, 16)
                act.dma_start(POOLW, A["pool_w"]).then_inc(in_tab.sem, 16)
                act.dma_start(SGUW, A["sgu_w"]).then_inc(in_tab.sem, 16)
                act.dma_start(SGUB, A["sgu_b"]).then_inc(in_tab.sem, 16)
                act.dma_start(COUNT, A["tab_count"].rearrange("p (a b) -> p a b", a=4)).then_inc(in_tab.sem, 16)
            z = linear(6, T, Z, x, after=x[2])
            square_sum(T, T, in_ctx, z)
            fill_begin(1, 6, z)

            sguw = up("pool_step")
            if on(pool, in_tab):
                NG.affine_select(out=SGUW, in_=SGUW, compare_op=ALU.is_ge, fill=0.0, base=0,
                                 pattern=[[0, 4], [1, P]], channel_multiplier=-1).then_inc(sguw.sem, 1)
            act_uv = up("act_step")
            if on(act, z):
                NS.activation(Z[:, 4:12, :], Z[:, 4:12, :], ACT.Gelu_apprx_tanh).then_inc(act_uv.sem, 1)

            last = z
            for g in range(4):
                a = Z[:, g, :]
                src, w = a, 1
                for level in range(g + 1):
                    dst = (W1, W2)[level % 2]
                    s1, s2 = up("dve_step"), up("dve_step")
                    if on(dve, last):
                        NV.tensor_copy(dst[:, 0:w], src[:, 0:w]).then_inc(s1.sem, 1)
                        NV.tensor_tensor(dst[:, w:T], src[:, w:T], src[:, 0:T - w], ADD).then_inc(s2.sem, 1)
                    src, w, last = dst, 2 * w, s2
                d1, d2, d3 = up("dve_step"), up("dve_step"), up("dve_step")
                if on(dve, last):
                    NV.scalar_tensor_tensor(DIFF[:, g, w:T], src[:, w:T], 1.0 / w, a[:, w:T], MUL, SUB).then_inc(d1.sem, 1)
                    dve.wait_ge(*in_tab)
                    NV.tensor_tensor(DIFF[:, g, 0:w], src[:, 0:w], COUNT[:, g, 0:w], MUL).then_inc(d2.sem, 1)
                    dve.wait_ge(*d2)
                    NV.tensor_tensor(DIFF[:, g, 0:w], DIFF[:, g, 0:w], a[:, 0:w], SUB).then_inc(d3.sem, 1)
                last = d3
                fill((0, 14, 16, 18)[g])
                pooled = up("pe_step")
                if on(pe, d3, in_tab):
                    NT.matmul(BANK[g][:, 0:T], POOLW[:, g, :], DIFF[:, g, :], start=True, stop=True).then_inc(pooled.sem, 1)
                scaled = up("act_step")
                if on(act, pooled):
                    NS.activation(DIFF[:, g, :], BANK[g][:, 0:T], ACT.Copy, scale=vec("pool_scale", g, 1)).then_inc(scaled.sem, 1)
                mixed = keep_split(DIFF[:, g, :], g, slice(0, T), scaled)

            V = Z[:, 8:12, :]

            def feature_sum(src, b, m0):
                s1, s2, s3, tot = up("dve_step"), up("dve_step"), up("dve_step"), up("pe_step")
                if on(dve, m0):
                    NV.tensor_tensor(W1, src[:, 0, :], src[:, 1, :], ADD).then_inc(s1.sem, 1)
                    NV.tensor_tensor(W2, src[:, 2, :], src[:, 3, :], ADD).then_inc(s2.sem, 1)
                    dve.wait_ge(*s2)
                    NV.tensor_tensor(W1, W1, W2, ADD).then_inc(s3.sem, 1)
                if on(pe, s3):
                    NT.matmul(BANK[b][:, 0:T], ones, W1, start=True, stop=True).then_inc(tot.sem, 1)
                return tot

            fill(8)
            tot = feature_sum(V, 4, act_uv)
            fill(10)
            mu = up("act_step")
            if on(act, tot):
                NS.activation(DIAG[:, 0:T], BANK[4][:, 0:T], ACT.Copy, scale=1.0 / 512).then_inc(mu.sem, 1)
            cen = up("dve_step")
            if on(dve, mu):
                NV.tensor_tensor(V, V, DIAG[:, 0:T].unsqueeze(1).to_broadcast([P, 4, T]), SUB).then_inc(cen.sem, 1)
            vsq = up("act_step")
            if on(act, cen, mixed):
                NS.activation(DIFF, V, ACT.Square).then_inc(vsq.sem, 1)
            tot = feature_sum(DIFF, 5, vsq)
            fill(14)
            root = up("act_step")
            if on(act, tot):
                NS.activation(DIAG[:, 0:T], BANK[5][:, 0:T], ACT.Sqrt, bias=vec("eps5"), scale=1.0 / 512).then_inc(root.sem, 1)
            inv = up("dve_step")
            if on(dve, root):
                NV.reciprocal(DIAG[:, 0:T], DIAG[:, 0:T]).then_inc(inv.sem, 1)
            nrm = up("dve_step")
            if on(dve, inv):
                NV.tensor_tensor(V, V, DIAG[:, 0:T].unsqueeze(1).to_broadcast([P, 4, T]), MUL).then_inc(nrm.sem, 1)
            aff = up("dve_step")
            if on(dve, nrm):
                for g in range(4):
                    op = NV.tensor_scalar(Z[:, 8 + g, :], Z[:, 8 + g, :], vec("sgu_g", g, 1), vec("sgu_b", g, 1), MUL, ADD)
                op.then_inc(aff.sem, 1)
            vt = all_by_token([Z[:, 8 + g, c * P:(c + 1) * P] for g in range(4) for c in range(2)], VT, aff)
            gate_mm = []
            for g in range(4):
                mm_done = up("pe_step")
                if on(pe, vt, sguw, mixed):
                    for c in range(2):
                        mm = NT.matmul(BANK[g][:, c * P:(c + 1) * P], VT[:, 2 * g + c, :], SGUW[:, g, :], start=True, stop=True)
                    mm.then_inc(mm_done.sem, 1)
                gate_mm.append(mm_done)
            for g in range(4):
                mm_done = gate_mm[g]
                b1, b2 = up("dve_step"), up("dve_step")
                if on(dve, mm_done):
                    NV.tensor_tensor(DIFF[:, g, :].rearrange("p (c t) -> p c t", c=2), BANK[g][:, 0:T].rearrange("p (c t) -> p c t", c=2),
                                     SGUB[:, g, :].unsqueeze(1).to_broadcast([P, 2, P]), ADD).then_inc(b1.sem, 1)
                    dve.wait_ge(*b1)
                    NV.tensor_tensor(DIFF[:, g, :], DIFF[:, g, :], Z[:, 4 + g, :], MUL).then_inc(b2.sem, 1)
                mixed = keep_split(DIFF[:, g, :], 4 + g, slice(0, T), b2)
                fill(16)
            adaln_gain(0, 0, 0, fill_end())
            y = linear(4, T, Y, [None], gain1("mix_post", 0), after=mixed)
            x = norms(T, gain1("mix_post", 0), T, gain1("ffn_pre", 0), [y], 2)
            y = ffn(T, gain1("ffn_post", 0), x, x[2])
            x = norms(T, gain1("ffn_post", 0), T, gain1("mix_pre", 1), [y], 4)

            piece = carve()
            Z = piece(28, T)
            MASK, MASKC, DECAY, POSI = piece(2 * P), piece(2, 15), piece(4, T), piece(T, dt=i32)
            CW1 = [piece(32, P), piece(32, P)]
            CW2 = piece(2, 64)
            CPOS = piece(2, 32)
            PBS = piece(6, T)
            PB = [PBS[:, 2 * b:2 * b + 2] for b in range(3)]
            BLKS = PBS.rearrange("p a q -> p (a q)")[:, 0:32 * 30].rearrange("p (l n) -> p l n", l=32)
            COSN, SINN, COSR, SINR = (piece(T) for _ in range(4))
            HID = piece(4, 15)
            KCT, VC = piece(15), piece(P)
            VTOK = piece(4, P)
            GT = piece(2, 24)
            PC = [piece(15) for _ in range(3)]
            PT = [piece(5, P) for _ in range(2)]
            in_tab = up("in_tab", 8 * 16)
            if on(act, y):
                for dst, name in [(MASK, "tab_mask"), (MASKC, "tab_mask_c"), (DECAY, "tab_decay"), (POSI, "pos"),
                                  (CW1[0], "cmp_k_w1"), (CW1[1], "cmp_v_w1"), (CW2, "cmp_w2"), (CPOS, "cmp_pos")]:
                    act.dma_start(dst, A[name]).then_inc(in_tab.sem, 16)

            first = here()
            z1 = linear(5, T, Z, x, after=x[2])
            posf = up("dve_step")
            if on(dve, in_tab):
                NV.tensor_copy(ACC[:, 0:T], POSI).then_inc(posf.sem, 1)
            tables = []
            for f, cos, sin in (("f_nsa", COSN, SINN), ("f_ret", COSR, SINR)):
                m = [up("dve_step") for _ in range(11)]
                if on(dve, posf):
                    ang, q = DIAG[:, 0:T], DIAG[:, T:T2]
                    C1 = 6.28125
                    C2 = float(np.float32(np.round((2 * np.pi - C1) * 2**20) / 2**20))
                    C3 = float(2 * np.pi - C1 - C2)
                    PI = 3.1415925
                    NV.tensor_scalar(ang, ACC[:, 0:T], vec(f), None, MUL).then_inc(m[0].sem, 1)
                    dve.wait_ge(*m[0])
                    NV.tensor_scalar(q, ang, 1.0 / (2 * np.pi), 12582912.0, MUL, ADD).then_inc(m[1].sem, 1)
                    dve.wait_ge(*m[1])
                    NV.tensor_scalar(q, q, -12582912.0, None, ADD).then_inc(m[2].sem, 1)
                    for j, c in enumerate((C1, C2, C3)):
                        dve.wait_ge(*m[2 + j])
                        NV.scalar_tensor_tensor(ang, q, -c, ang, MUL, ADD).then_inc(m[3 + j].sem, 1)
                    dve.wait_ge(*m[5])
                    NV.tensor_scalar(sin, ang, PI, -PI, ALU.min, ALU.max).then_inc(m[6].sem, 1)
                    NV.tensor_scalar(cos, ang, 0.5 * np.pi, None, ADD).then_inc(m[7].sem, 1)
                    dve.wait_ge(*m[7])
                    NV.tensor_scalar(q, cos, PI, -2 * np.pi, ALU.is_gt, MUL).then_inc(m[8].sem, 1)
                    dve.wait_ge(*m[8])
                    NV.tensor_tensor(cos, cos, q, ADD).then_inc(m[9].sem, 1)
                    dve.wait_ge(*m[9])
                    NV.tensor_scalar(cos, cos, PI, -PI, ALU.min, ALU.max).then_inc(m[10].sem, 1)
                posf = m[10]
                tables.append(m[10])

            linear(1, T, Z, base=first)
            trig = up("act_step", 4)
            if on(act, tables[1]):
                for t in (COSN, SINN, COSR, SINR):
                    NS.activation(t, t, ACT.Sin).then_inc(trig.sem, 1)
            vtok = all_by_token([Z[:, t, c * P:(c + 1) * P] for t in (7, 9) for c in range(2)], VTOK, z1)
            if dve:
                dve.wait_ge(*trig)
            ROT = (vec("rot_nsa"), COSN, SINN)
            roped = rope([Z[:, t, :] for t in (4, 6, 8)], *ROT, z1, vtok, banks=(5, 6, 7))
            z2 = linear(2, T, Z, base=first)
            roped = rope([Z[:, t, :] for t in range(4)], *ROT, z1, roped)
            clear = up("dve_step")
            if on(dve, roped):
                NV.memset(BLKS, 0.0).then_inc(clear.sem, 1)

            def blocks_of(kv, *ready):
                blk = up("dve_step", 2)
                src = Z[:, 4 + kv, :]
                win = bass.AP(tensor=src.tensor, offset=src.offset, ap=[list(src.ap[0]), [1, 32], [16, 15]])
                if on(dve, *ready):
                    for g in range(2):
                        rows = slice(64 * g, 64 * g + 64)
                        NV.tensor_tensor(BLKS[rows, :, 15 * g:15 * g + 15], win[rows], CPOS[rows, kv, :].unsqueeze(2).to_broadcast([64, 32, 15]), ADD)\
                            .then_inc(blk.sem, 1)
                return blk

            def hidden_of(kv, *ready):
                hid, ge = up("pe_step"), up("act_step")
                if on(pe, *ready):
                    for l in range(32):
                        mm = NT.matmul(BANK[6][:, 0:30], CW1[kv][:, l, :], BLKS[:, l, :], start=l == 0, stop=l == 31)
                    mm.then_inc(hid.sem, 1)
                if on(act, hid):
                    NS.activation(HID[:, 2 * kv:2 * kv + 2, :], BANK[6][:, 0:30].rearrange("p (g n) -> p g n", g=2), ACT.Gelu_apprx_tanh)\
                        .then_inc(ge.sem, 1)
                return hid, ge
            blk = blocks_of(0, clear)
            linear(1, T, Z, base=first)
            hid, ge = hidden_of(0, blk)
            ROT = (vec("rot_ret"), COSR, SINR)
            z3 = linear(1, T, Z, base=first)
            roped = rope([Z[:, t, :] for t in range(10, 14)], *ROT, z2, roped, ge)
            blk = blocks_of(1, hid)
            z4 = linear(2, T, Z, base=first)
            hid, ge = hidden_of(1, blk, roped)
            roped = rope([Z[:, t, :] for t in range(14, 18)], *ROT, z3, roped, ge)
            z = linear(2, T, Z, base=first)
            cmp_mm, cmp_kv = up("pe_step"), up("act_step")
            if on(pe, ge, roped):
                for g in range(2):
                    NT.matmul(BANK[6][64 * g:64 * g + 64, 0:15], CW2[:, 0, :], HID[:, g, :], start=True, stop=True)
                for g in range(2):
                    mm = NT.matmul(BANK[7][0:15, 64 * g:64 * g + 64], HID[:, 2 + g, :], CW2[:, 1, :], start=True, stop=True)
                mm.then_inc(cmp_mm.sem, 1)
            if on(act, cmp_mm):
                NS.activation(KCT, BANK[6][:, 0:15], ACT.Copy)
                NS.activation(VC[0:15, :], BANK[7][0:15, 0:P], ACT.Copy).then_inc(cmp_kv.sem, 1)
            turned = up("pe_step")
            if on(pe, z, cmp_kv):
                for c in range(2):
                    mm = NT.transpose(BANK[6][:, c * P:(c + 1) * P], Z[:, 26, c * P:(c + 1) * P], ident)
                mm.then_inc(turned.sem, 1)
            th = up("act_step")
            if on(act, turned):
                NS.activation(GT, BANK[6][:, 0:T].rearrange("p (c g) -> p c g", c=2)[:, :, 0:24], ACT.Tanh, scale=0.5).then_inc(th.sem, 1)
            sg, ok = up("dve_step"), up("dve_step")
            if on(dve, th):
                NV.tensor_scalar(GT, GT, 0.5, 0.5, MUL, ADD).then_inc(sg.sem, 1)
                dve.wait_ge(*sg)
                for c in range(2):
                    op = NV.tensor_scalar(GT[:, c, 0:24:3], GT[:, c, 0:24:3], vec("row_ok", c, 1), None, MUL)
                op.then_inc(ok.sem, 1)
            gates = ok

            RV = CW1[0][:, 0:8, :]
            rv = all_by_token([Z[:, 18 + h, c * P:(c + 1) * P] for h in range(4) for c in range(2)], RV, hid, gates)
            units = [(j, qt, hf) for j in range(4) for qt in range(2) for hf in range(2)]
            S_NEG, S_MAX, S_SUM, S_CO = 0, 9, 18, 27

            def small(at, u, n=3):
                return SMALL[:, at + 3 * (u % 3):at + 3 * (u % 3) + n]
            probs, read_s, mult, trans, copied, pv, o_kept = {}, {}, {}, {}, {}, {}, {}

            def parts(u):
                j, qt, hf = units[u]
                return j, qt, hf, (qt + 1) * P, slice(64 * hf, 64 * hf + 64)
            RSC = [CW1[1][:, 3 * b:3 * b + 3, :].rearrange("p a q -> p (a q)") for b in range(2)]
            RO = CW1[1][:, 8:16, :].rearrange("p a q -> p (a q)").rearrange("p (h t) -> p h t", h=4)
            retained = [None]

            def retention(h, stage):
                b, done, taken = h % 2, up("pe_step"), up("act_step" if stage else "dve_step")
                if stage == 0:
                    if on(pe, rv, roped, retained[0]):
                        NT.matmul(BANK[7][:, 0:T], Z[:, 14 + h, 0:P], Z[:, 10 + h, :], start=True, stop=True)
                        NT.matmul(BANK[7][:, T:T + P], Z[:, 14 + h, P:T], Z[:, 10 + h, P:T], start=True, stop=True).then_inc(done.sem, 1)
                    if on(dve, done):
                        NV.tensor_tensor(RSC[b][:, 0:T], BANK[7][:, 0:T], DECAY[:, h, :], MUL)
                        NV.tensor_tensor(RSC[b][:, T:T + P], BANK[7][:, T:T + P], DECAY[:, h, 0:P], MUL).then_inc(taken.sem, 1)
                else:
                    if on(pe, retained[0]):
                        NT.matmul(BANK[7][:, 0:T], RV[:, 2 * h, :], RSC[b][:, 0:T], start=True, stop=False)
                        NT.matmul(BANK[7][:, P:T], RV[:, 2 * h + 1, :], RSC[b][:, T:T + P], start=False, stop=True).then_inc(done.sem, 1)
                    if on(act, done):
                        NS.activation(RO[:, h, :], BANK[7][:, 0:T], ACT.Copy).then_inc(taken.sem, 1)
                retained[0] = taken
            for it in range(len(units) + 3):
                u, x1, w, v = it, it - 1, it - 2, it - 3
                if u < len(units):
                    j, qt, hf, n, h64 = parts(u)
                    sc = up("pe_step")
                    if on(pe, roped, vtok, cmp_kv, gates, read_s.get(u - 1)):
                        q = Z[h64, j, qt * P:(qt + 1) * P]
                        NT.matmul(BANK[2][:, 0:15], q, KCT[h64, :], start=True, stop=True)
                        NT.matmul(BANK[u % 2][:, 0:n], q, Z[h64, 6, 0:n], start=True, stop=True)
                        NT.matmul(BANK[u % 2][:, T:T + n], q, Z[h64, 8, 0:n], start=True, stop=True).then_inc(sc.sem, 1)
                if 0 <= w < len(units):
                    j, qt, hf, n, h64 = parts(w)
                    b, head = w % 3, j + 4 * hf
                    m1, m2, m3 = up("dve_step"), up("dve_step"), up("dve_step")
                    if on(dve, probs[w], gates):
                        NV.reciprocal(small(S_CO, w), small(S_SUM, w)).then_inc(m1.sem, 1)
                        dve.wait_ge(*m1)
                        NV.tensor_tensor(small(S_CO, w), small(S_CO, w), GT[:, qt, 3 * head:3 * head + 3], MUL).then_inc(m2.sem, 1)
                        dve.wait_ge(*m2)
                        NV.tensor_scalar(PC[b], PC[b], small(S_CO, w)[:, 0:1], None, MUL)
                        for a in range(2):
                            op = NV.tensor_scalar(PB[b][:, a, 0:n], PB[b][:, a, 0:n], small(S_CO, w)[:, 1 + a:2 + a], None, MUL)
                        op.then_inc(m3.sem, 1)
                    mult[w] = m3
                if u < len(units):
                    j, qt, hf, n, h64 = parts(u)
                    b = u % 3
                    m1, m2, m3, m4, m5 = (up("dve_step") for _ in range(5))
                    if on(dve, sc, trans.get(u - 3)):
                        NV.scalar_tensor_tensor(PC[b], BANK[2][:, 0:15], 0.125, MASKC[:, qt, :], MUL, ADD).then_inc(m1.sem, 1)
                        NV.scalar_tensor_tensor(PB[b][:, :, 0:n], BANK[u % 2][:, :].rearrange("p (a n) -> p a n", a=2)[:, :, 0:n], 0.125,
                                                MASK[:, 2 * P - n:2 * P].unsqueeze(1).to_broadcast([P, 2, n]), MUL, ADD).then_inc(m2.sem, 1)
                        dve.wait_ge(*m2)
                        NV.tensor_reduce(small(S_MAX, u, 1), PC[b], AX, ALU.max).then_inc(m3.sem, 1)
                        NV.tensor_reduce(small(S_MAX, u)[:, 1:3], PB[b][:, :, 0:n], AX, ALU.max).then_inc(m4.sem, 1)
                        dve.wait_ge(*m4)
                        NV.tensor_scalar(small(S_NEG, u), small(S_MAX, u), -1.0, None, MUL).then_inc(m5.sem, 1)
                    read_s[u], probs[u] = m2, m5
                if 0 <= x1 < len(units):
                    j, qt, hf, n, h64 = parts(x1)
                    b = x1 % 3
                    ex = up("act_step", 3)
                    if on(act, probs[x1]):
                        NS.activation(PC[b], PC[b], ACT.Exp, bias=small(S_NEG, x1)[:, 0:1], accum_out=small(S_SUM, x1)[:, 0:1]).then_inc(ex.sem, 1)
                        for a in range(2):
                            NS.activation(PB[b][:, a, 0:n], PB[b][:, a, 0:n], ACT.Exp, bias=small(S_NEG, x1)[:, 1 + a:2 + a],
                                          accum_out=small(S_SUM, x1)[:, 1 + a:2 + a]).then_inc(ex.sem, 1)
                    probs[x1] = ex
                if 0 <= w < len(units):
                    j, qt, hf, n, h64 = parts(w)
                    b, p3 = w % 2, w % 3
                    tr, cp = up("pe_step"), up("act_step")
                    if on(pe, mult[w], copied.get(w - 1)):
                        NT.transpose(BANK[3][0:15, 0:P], PC[p3], ident)
                        for a in range(2):
                            for c in range(qt + 1):
                                mm = NT.transpose(BANK[4 + b][:, (2 * a + c) * P:(2 * a + c + 1) * P], PB[p3][:, a, c * P:(c + 1) * P], ident)
                        mm.then_inc(tr.sem, 1)
                    if on(act, tr, pv.get(w - 2)):
                        NS.activation(PT[b][0:15, 4, :], BANK[3][0:15, 0:P], ACT.Copy)
                        view = BANK[4 + b][:, :].rearrange("p (a c q) -> p a c q", a=2, c=2)[:, :, 0:qt + 1, :]
                        NS.activation(PT[b][:, 0:4, :].rearrange("p (a c) q -> p a c q", a=2)[:, :, 0:qt + 1, :], view, ACT.Copy)\
                            .then_inc(cp.sem, 1)
                    trans[w], copied[w] = tr, cp
                if v >= 0:
                    j, qt, hf, n, h64 = parts(v)
                    b = v % 2
                    o = up("pe_step")
                    if on(pe, copied[v], o_kept.get(v // 2 - 1)):
                        dst = BANK[6][h64, 0:P]
                        NT.matmul(dst, VC[0:15, 64 * hf:64 * hf + 64], PT[b][0:15, 4, :], start=True, stop=False)
                        for a in range(2):
                            for c in range(qt + 1):
                                mm = NT.matmul(dst, VTOK[:, 2 * a + c, 64 * hf:64 * hf + 64], PT[b][:, 2 * a + c, :],
                                               start=False, stop=a == 1 and c == qt)
                        mm.then_inc(o.sem, 1)
                    pv[v] = o
                    if hf == 1:
                        o_kept[v // 2] = keep_split(BANK[6][:, 0:P], j, slice(qt * P, (qt + 1) * P), o)
                if it % 4 in (1, 2) and it < 16:
                    retention(it // 4, it % 4 - 1)
            attended = o_kept[7]

            sg = up("act_step")
            if on(act):
                NS.activation(Z[:, 22:26, :], Z[:, 22:26, :], ACT.Silu).then_inc(sg.sem, 1)
            for hh in range(2):
                o2 = RO[:, 2 * hh:2 * hh + 2, :].rearrange("p h t -> p (h t)")
                tot = up("pe_step")
                if on(pe, retained[0], attended):
                    NT.matmul(BANK[4 + hh][:, :], ones, o2, start=True, stop=True).then_inc(tot.sem, 1)
                cen = up("dve_step")
                if on(dve, tot):
                    NV.scalar_tensor_tensor(o2, BANK[4 + hh][:, :], -1.0 / P, o2, MUL, ADD).then_inc(cen.sem, 1)
            nrm = tile_norm([(RO[:, h, :], T, None) for h in range(4)], lambda h: vec("gn_g", h, 1), None, [cen], vec("eps5"), (5, 6))
            for h in range(4):
                gated = up("dve_step")
                if on(dve, nrm, sg):
                    NV.tensor_tensor(RO[:, h, :], RO[:, h, :], Z[:, 22 + h, :], MUL).then_inc(gated.sem, 1)
                mixed = keep_split(RO[:, h, :], 4 + h, slice(0, T), gated)
            y = linear(4, T, Y, [None], gain1("mix_post", 1), after=mixed)
            x = norms(T, gain1("mix_post", 1), T, gain1("ffn_pre", 1), [y], 6)
            y = ffn(T, gain1("ffn_post", 1), x, x[2])
            x = norms(T, gain1("ffn_post", 1), T2, pre(0, 0), [y], 8)

            def attend(unit_list, scale, V, PB, PT, neg_lam, ready, between=None):
                exps, mult, trans, copied, pv, kept = {}, {}, {}, {}, {}, {}
                last = len(unit_list)

                def small(at, u, n=2):
                    return SMALL[:, at + 2 * (u % 3):at + 2 * (u % 3) + n]
                NEGM, MAXM, SUM, CO = 0, 6, 24, 30
                for it in range(last + 3):
                    u, x1, w, r = it, it - 1, it - 2, it - 3
                    if u < last:
                        q, k, v, q0, k0, parts, dest = unit_list[u]
                        nk, sc = T2 - k0, up("pe_step", len(parts))
                        if on(pe, exps.get(u - 2), *ready):
                            if between and head_turned[dest]:
                                pe.wait_ge(*head_turned[dest])
                            for a, pr in enumerate(parts):
                                NT.matmul(BANK[2 * (u % 2) + a][:, 0:nk], q[pr, q0:q0 + P], k[pr, k0:T2], start=True, stop=True)\
                                    .then_inc(sc.sem, 1)
                    if 0 <= w < last:
                        q, k, v, q0, k0, parts, dest = unit_list[w]
                        b, nk, np_ = w % 3, T2 - k0, len(parts)
                        m1, m2, m3 = (up("dve_step") for _ in range(3))
                        m4 = up("dve_step") if np_ == 2 else m3
                        if on(dve, exps[w]):
                            NV.reciprocal(small(CO, w, np_), small(SUM, w, np_)).then_inc(m1.sem, 1)
                            dve.wait_ge(*m1)
                            if np_ == 2:
                                NV.tensor_tensor(small(CO, w)[:, 1:2], small(CO, w)[:, 1:2], neg_lam, MUL).then_inc(m2.sem, 1)
                                NV.tensor_scalar(PB[b][:, 0, 0:nk], PB[b][:, 0, 0:nk], small(CO, w)[:, 0:1], None, MUL).then_inc(m3.sem, 1)
                                dve.wait_ge(*m3)
                                NV.scalar_tensor_tensor(PB[b][:, 0, 0:nk], PB[b][:, 1, 0:nk], small(CO, w)[:, 1:2], PB[b][:, 0, 0:nk], MUL, ADD)\
                                    .then_inc(m4.sem, 1)
                            else:
                                NV.tensor_scalar(PB[b][:, 0, 0:nk], PB[b][:, 0, 0:nk], small(CO, w)[:, 0:1], None, MUL).then_inc(m4.sem, 2)
                        mult[w] = m4
                    if u < last:
                        q, k, v, q0, k0, parts, dest = unit_list[u]
                        nk, np_ = T2 - k0, len(parts)
                        mx, ng = up("dve_step"), up("dve_step")
                        if on(dve, sc):
                            for a in range(np_):
                                op = NV.tensor_reduce(small(MAXM, u)[:, a:a + 1], BANK[2 * (u % 2) + a][:, 0:nk], AX, ALU.max)
                            op.then_inc(mx.sem, 1)
                            dve.wait_ge(*mx)
                            NV.tensor_scalar(small(NEGM, u, np_), small(MAXM, u, np_), -scale, None, MUL).then_inc(ng.sem, 1)
                        exps[u] = ng
                    if 0 <= x1 < last:
                        q, k, v, q0, k0, parts, dest = unit_list[x1]
                        b, nk = x1 % 3, T2 - k0
                        ex = up("act_step", len(parts))
                        if on(act, exps[x1], trans.get(x1 - 3)):
                            for a in range(len(parts)):
                                NS.activation(PB[b][:, a, 0:nk], BANK[2 * (x1 % 2) + a][:, 0:nk], ACT.Exp, bias=small(NEGM, x1)[:, a:a + 1],
                                              scale=scale, accum_out=small(SUM, x1)[:, a:a + 1]).then_inc(ex.sem, 1)
                        exps[x1] = ex
                    if 0 <= w < last:
                        q, k, v, q0, k0, parts, dest = unit_list[w]
                        b, nk = w % 2, T2 - k0
                        tr, cp = up("pe_step"), up("act_step")
                        if on(pe, mult[w], copied.get(w - 2)):
                            for c in range(nk // P):
                                mm = NT.transpose(BANK[4 + b][:, c * P:(c + 1) * P], PB[w % 3][:, 0, c * P:(c + 1) * P], ident)
                            mm.then_inc(tr.sem, 1)
                        if on(act, tr, pv.get(w - 2)):
                            NS.activation(PT[b][:, 0:nk], BANK[4 + b][:, 0:nk], ACT.Copy).then_inc(cp.sem, 1)
                        trans[w], copied[w] = tr, cp
                    if r >= 0:
                        q, k, v, q0, k0, parts, dest = unit_list[r]
                        b, nk = r % 2, T2 - k0
                        o, ke = up("pe_step"), up("act_step")
                        if on(pe, copied[r], kept.get(r - 1)):
                            for c in range(nk // P):
                                mm = NT.matmul(BANK[6][:, 0:P], V(k0 // P + c, v), PT[b][:, c * P:(c + 1) * P],
                                               start=c == 0, stop=c == nk // P - 1)
                            mm.then_inc(o.sem, 1)
                        if on(act, o):
                            NS.activation(Y[:, dest, q0:q0 + P], BANK[6][:, 0:P], ACT.Copy).then_inc(ke.sem, 1)
                        pv[r], kept[r] = o, ke
                    if between:
                        between(it)
                return ke

            y = ffn(T2, post(0, 0), x, x[2], 8)
            piece = carve()
            Z = piece(24, T2)
            VTK = piece(32, P)
            PB = [piece(2, T2) for _ in range(3)]
            PT = [piece(T2) for _ in range(2)]
            CS = piece(2, T)
            LAM = piece(4, 64)
            in_tab = up("in_tab", 32)
            if on(act, y):
                act.dma_start(CS, A["tab_da"]).then_inc(in_tab.sem, 16)
                act.dma_start(LAM, A["da_lambda"]).then_inc(in_tab.sem, 16)
            x = norms(T2, post(0, 0), T2, pre(0, 1), [y], 10)
            first = here()
            ROT = (vec("rot_ax"), CS[:, 0, :], CS[:, 1, :])
            ada0 = count["ada_red"]
            if sp:
                sp.wait_ge(*now("hn_hi"))
                next(loader, None)

            def ada_block(t):
                if dve and t < 4:
                    gemv_half(0, t, 0, 1, ada0)
                    gemv_half(0, t, 1, 1, ada0)
                if pe and t:
                    gemv_reduce(0, t - 1, 1, ada0)
            done = [linear(4, T2, Z, x, after=x[2])]
            roped = done[0]
            for n, turn in enumerate([(0, 1, 2), (3, 4, 5), (6, 7, 8), (9, 10, 11), (12, 13), (14, 15), (), ()]):
                done.append(linear(1, T2, Z, base=first))
                if dve and not n:
                    dve.wait_ge(*in_tab)
                if turn:
                    roped = rope([Z[:, t, 0:T] for t in turn], *ROT, done[n], roped, banks=(4, 5, 6))
                if n % 2 == 0:
                    ada_block(n // 2)
            z4, z = done[-2:]
            ada_block(4)
            gemv_keep(10)
            roped = now("dve_step")
            vt = roped
            for f in range(2):
                vt = all_by_token([Z[:, 16 + 4 * f + h, c * P:(c + 1) * P] for c in range(4) for h in range(4)],
                                  VTK[:, 16 * f:16 * f + 16, :], (z4, z)[f], vt, (4, 5, 6))
            l1, l2, l3 = up("dve_step"), up("dve_step"), up("dve_step")
            LP = SMALL[:, 16:24]
            if on(dve, in_tab, z):
                NV.tensor_tensor(LAM[:, 0, :], LAM[:, 0, :], LAM[:, 1, :], MUL).then_inc(l1.sem, 1)
                NV.tensor_tensor(LAM[:, 2, :], LAM[:, 2, :], LAM[:, 3, :], MUL).then_inc(l2.sem, 1)
                dve.wait_ge(*l2)
                NV.tensor_reduce(LP[:, 0:1], LAM[:, 0, :], AX, ADD)
                NV.tensor_reduce(LP[:, 1:2], LAM[:, 2, :], AX, ADD).then_inc(l3.sem, 1)
            le = up("act_step")
            if on(act, l3):
                NS.activation(LP[:, 2:4], LP[:, 0:2], ACT.Exp).then_inc(le.sem, 1)
            l4, l5 = up("dve_step"), up("dve_step")
            if on(dve, le):
                NV.tensor_tensor(LP[:, 4:5], LP[:, 3:4], LP[:, 2:3], SUB).then_inc(l4.sem, 1)
                dve.wait_ge(*l4)
                NV.tensor_scalar(LP[:, 5:6], LP[:, 4:5], -LAMBDA_INIT, None, ADD).then_inc(l5.sem, 1)
            both = (slice(0, 64), slice(64, P))
            units = [(Z[:, h, :], Z[:, 8 + h, :], h, qt * P, 0 if qt < 2 else T, both, h) for h in range(8) for qt in range(4)]
            o = attend(units, 0.125, lambda c, h: VTK[:, 16 * (h // 4) + 4 * c + h % 4, :], PB, PT, LP[:, 5:6], [roped, vt, l5])
            x = tile_norm([(Y[:, h, :], T2, h) for h in range(8)], lambda h: vec("subln"), 1.0 - LAMBDA_INIT, [o])
            y = linear(4, T2, Y, x, post(0, 1))
            x = norms(T2, post(0, 1), T2, pre(0, 2), [y], 12)
            y = ffn(T2, post(0, 2), x, x[2], 12)
            x = norms(T2, post(0, 2), T2, pre(1, 0), [y], 14)

            y = ffn(T2, post(1, 0), x, None, 14)
            piece = carve()
            Z = piece(12, T2)
            VTK = piece(8, P)
            PB = [piece(2, T2) for _ in range(3)]
            PT = [piece(T2) for _ in range(2)]
            CS = piece(2, T)
            in_tab = up("in_tab", 16)
            if on(act, y):
                act.dma_start(CS, A["tab_ga"]).then_inc(in_tab.sem, 16)
            x = norms(T2, post(1, 0), T2, pre(1, 1), [y], 16)
            first = here()
            z1 = linear(2, T2, Z, x)
            linear(1, T, Z, base=first)
            vt = all_by_token([Z[:, 2 + g, c * P:(c + 1) * P] for c in range(4) for g in range(2)], VTK, z1)
            z = linear(3, T, Z, base=first)
            nqk = tile_norm([(Z[:, t, :], T2, None) for t in (0, 1)] + [(Z[:, t, 0:T], T, None) for t in range(4, 12)],
                            lambda j: vec("k_norm" if j < 2 else "q_norm"), None, [z, vt])
            if dve:
                dve.wait_ge(*in_tab)
            ROT = (vec("rot_ax"), CS[:, 0, :], CS[:, 1, :])
            roped = rope([Z[:, t, 0:T] for t in (0, 1, *range(4, 12))], *ROT, nqk)
            full = (slice(0, P),)
            units = [(Z[:, 4 + h, :], Z[:, h // 4, :], h // 4, qt * P, 0, full, h) for h in range(8) for qt in range(2)]
            o = attend(units, float(np.float32(P ** -0.5)), lambda c, g: VTK[:, 2 * c + g, :], PB, PT, None, [roped, vt])
            his, los = [], []
            for h in range(8):
                los.append(keep_split(Y[:, h, 0:T], h, slice(0, T), o))
                his.append(now("hn_hi"))
            y = linear(4, T, Y, [his, los], post(1, 1, 1))
            x = norms(T, post(1, 1, 1), T, pre(1, 2, 1), [y], 18)
            y = ffn(T, post(1, 2, 1), x)
            finish(sp, norms(T, post(1, 2, 1), None, None, [y], None))

        def finish(sp, res):
            if sp:
                for m in res:
                    sp.wait_ge(*m)
                sp.dma_start(out, H[:, :, 0:T]).then_inc(sems["stored"], 16)
                sp.wait_ge(sems["stored"], 16)

        @block.sync
        def _(eng):
            program(sp=eng)

        @block.gpsimd
        def _(eng):
            program(pool=eng)

        @block.scalar
        def _(eng):
            program(act=eng)

        @block.vector
        def _(eng):
            program(dve=eng)

        @block.tensor
        def _(eng):
            program(pe=eng)


def by_feature(a):
    return np.ascontiguousarray(a.reshape(-1, P).T)


def main_blocks(w):
    return w.reshape(KD, P, -1, 256).transpose(2, 1, 0, 3).reshape(-1, P, BLK)


def down_blocks(w):
    return w.reshape(2, HALF, P, KD, P).transpose(3, 0, 2, 1, 4).reshape(-1, P, DBLK)


def gate_up_blocks(gate, up):
    return np.stack([main_blocks(gate), main_blocks(up)], axis=1).reshape(-1, P, BLK)


def axial(rot_dim, heads):
    rows = T // 64
    row = np.repeat(np.arange(rows), 64).astype(np.float32)
    col = np.tile(np.arange(64), rows).astype(np.float32)
    n = rot_dim // 4
    freqs = np.float32(10000.0) ** (-np.arange(n, dtype=np.float32) / np.float32(n))
    ang = np.concatenate([row[:, None] * freqs, col[:, None] * freqs], axis=-1)
    both = np.stack([np.cos(ang), np.sin(ang)]).astype(np.float32)
    return np.ascontiguousarray(np.tile(np.repeat(both, 2, axis=2), (1, 1, heads)).transpose(2, 0, 1))


def rotations():
    nsa, ret, ax = (np.zeros((P, P), np.float32) for _ in range(3))
    for b in (0, 64):
        for j in range(8):
            nsa[b + 8 + j, b + j], nsa[b + j, b + 8 + j] = -1, 1
    for j in range(64):
        ret[64 + j, j], ret[j, 64 + j] = -1, 1
        ax[2 * j + 1, 2 * j], ax[2 * j, 2 * j + 1] = -1, 1
    return nsa, ret, ax


def tables():
    t, f32 = np.arange(P), np.float32
    mask = np.zeros((P, 2 * P), f32)
    mask[:, P:] = np.where(t[None, :] <= t[:, None], 0, NEG)
    tq = np.arange(T).reshape(2, P)
    mask_c = np.where(np.arange(15) * 16 + 31 <= tq[:, :, None], 0, NEG).astype(f32).transpose(1, 0, 2)
    row_ok = (tq >= 31).astype(f32).T
    log_gamma = np.log1p(-np.exp2(-5.0 - np.arange(4)))
    rel = t[None, :] - t[:, None]
    same = np.where(rel[:, None] >= 0, np.exp(np.maximum(rel, 0)[:, None] * log_gamma[:, None]), 0)
    cross = np.exp((rel + P)[:, None] * log_gamma[:, None])
    decay = (np.concatenate([same, cross], axis=2) * P ** -0.5).astype(f32)
    count = np.stack([1.0 / np.minimum(np.arange(16) + 1, 2 ** (g + 1)) for g in range(4)]).reshape(1, 64)
    inv = 1.0 / f32(500000.0) ** (np.arange(0, 16, 2, dtype=f32) / f32(16))
    f_nsa = np.zeros(P, f32)
    for b in (0, 8, 64, 72):
        f_nsa[b:b + 8] = inv
    inv = 1.0 / f32(10000.0) ** (np.arange(0, P, 2, dtype=f32) / f32(P))
    return dict(mask=mask, mask_c=np.ascontiguousarray(mask_c), row_ok=row_ok, decay=decay,
                count=np.tile(count, (P, 1)).astype(f32), f_nsa=f_nsa[:, None], f_ret=np.tile(inv, 2)[:, None])


def kernel(**inputs):
    import concourse.bacc as bacc
    from concourse.bass_utils import run_bass_kernel_spmd

    I = {k: np.asarray(v) for k, v in inputs.items()}
    f32 = np.float32
    tab = tables()
    nsa, ret, ax = rotations()

    w = I["od_w_in"][0]
    heads = [h for j in range(4) for h in (j, j + 4)]
    cols = np.concatenate([np.arange(64 * h, 64 * h + 64) for h in heads] + [np.arange(512, 1280), np.arange(1304, 3352), np.arange(1280, 1304)])
    od_in = np.concatenate([w[:, cols], np.zeros((D, 28 * P - len(cols)), f32)], axis=1)
    rows = np.concatenate([np.arange(64 * h, 64 * h + 64) for h in heads] + [np.arange(512, 1024)])
    F2 = I["ffn_w_in_2"]
    main = [main_blocks(I["ev_w_in"][0]), main_blocks(I["ev_w_out"][0]),
            gate_up_blocks(I["ffn_w_gate"][0], I["ffn_w_up"][0]),
            main_blocks(od_in), main_blocks(I["od_w_out"][0][rows]),
            gate_up_blocks(I["ffn_w_gate"][1], I["ffn_w_up"][1]),
            gate_up_blocks(F2[0, 0][:, :F], F2[0, 0][:, F:]), main_blocks(I["da_w_in_2"][0]), main_blocks(I["da_w_out_2"][0]),
            gate_up_blocks(F2[0, 1][:, :F], F2[0, 1][:, F:]),
            gate_up_blocks(F2[1, 0][:, :F], F2[1, 0][:, F:]), main_blocks(np.roll(I["ga_w_in_2"][0], 4 * P, axis=1)), main_blocks(I["ga_w_out_2"][0]),
            gate_up_blocks(F2[1, 1][:, :F], F2[1, 1][:, F:])]
    down = [down_blocks(a) for a in (I["ffn_w_down"][0], I["ffn_w_down"][1], *I["ffn_w_out_2"].reshape(4, F, D))]

    parts = dict(
        mix_pre=by_feature(I["ln_mix_pre"]), mix_post=by_feature(I["ln_mix_post"]), ffn_pre=by_feature(I["ln_ffn_pre"]),
        ffn_post=by_feature(I["ln_ffn_post"]), norm_g=by_feature(I["norm_g_2"]), pool_scale=by_feature(I["ev_pool_scale"]),
        sgu_g=by_feature(I["ev_sgu_ln_g"]), sgu_b=by_feature(I["ev_sgu_ln_b"]), gn_g=by_feature(I["od_ret_gn_g"]),
        subln=by_feature(I["da_subln_2"]), q_norm=by_feature(I["ga_q_norm_2"]), k_norm=by_feature(I["ga_k_norm_2"]),
        ada_b=by_feature(I["ada_b_2"]),
        c=np.stack([by_feature(I["c_2"]), by_feature(I["c_ctx_2"])], axis=2).reshape(P, 16),
        eps6=np.full((P, 1), 1e-6, f32), eps5=np.full((P, 1), 1e-5, f32), f_nsa=tab["f_nsa"], f_ret=tab["f_ret"],
        row_ok=tab["row_ok"], ident=np.eye(P, dtype=f32), ones=np.ones((P, P), f32), rot_nsa=nsa, rot_ret=ret, rot_ax=ax)
    arrays = {
        "w_main": np.concatenate(main), "w_down": np.concatenate(down),
        "w_ada": np.concatenate([main_blocks(a) for a in I["ada_w_2"]]),
        "vec": np.concatenate([parts[n] for n in VEC_COLS], axis=1),
        "x0": np.ascontiguousarray(np.concatenate([I["x"][0].T, I["ctx_2"][0].T], axis=1).reshape(KD, P, T2).transpose(1, 0, 2)),
        "pool_w": np.ascontiguousarray(I["ev_pool_w"][0].transpose(1, 0, 2)),
        "sgu_w": np.ascontiguousarray(I["ev_sgu_w"][0].transpose(2, 0, 1)),
        "sgu_b": np.ascontiguousarray(np.broadcast_to(I["ev_sgu_b"][0], (P, 4, P))),
        "tab_count": tab["count"], "tab_mask": tab["mask"], "tab_mask_c": tab["mask_c"], "tab_decay": tab["decay"],
        "tab_da": axial(64, 2), "tab_ga": axial(128, 1),
        "pos": np.ascontiguousarray(np.broadcast_to(I["positions"].astype(np.int32), (P, T))),
        "cmp_w2": np.ascontiguousarray(np.stack([I["od_cmp_k_w2"][0], I["od_cmp_v_w2"][0]], axis=1)),
        "cmp_pos": np.ascontiguousarray(np.tile(np.stack([I["od_cmp_k_pos"][0].T, I["od_cmp_v_pos"][0].T], axis=1), (2, 1, 1))),
        "da_lambda": np.ascontiguousarray(np.broadcast_to(I["da_lambda_2"][0], (P, 4, 64))),
    }
    for kv in "kv":
        arrays[f"cmp_{kv}_w1"] = np.ascontiguousarray(np.tile(I[f"od_cmp_{kv}_w1"][0].reshape(32, 64, P).transpose(1, 0, 2), (2, 1, 1)))

    nc = bacc.Bacc("TRN2", target_bir_lowering=False, num_devices=1, dynamic_dma_scratch_size=1024)
    A = {}
    for name, a in arrays.items():
        A[name] = nc.dram_tensor(name, a.shape, mybir.dt.from_np(a.dtype), kind="ExternalInput").ap()
    out = nc.dram_tensor("out", (P, KD, T), mybir.dt.float32, kind="ExternalOutput").ap()
    build(nc, A, out)
    r = run_bass_kernel_spmd(nc, [arrays], core_ids=[0])
    return r.results[0]["out"].transpose(2, 1, 0).reshape(1, T, D)
```
